# Optimizing a Trainium2 kernel written in Bass

```python
import math
import jax, jax.numpy as jnp
from jax import lax
import numpy as np

D_MODEL = 1024
BATCH = 1
SEQ = 1024
DEPTH = 1
DEC_BATCH = 8
DEC_SEQ = 4
PAST_LEN = 8192
PAGE_SIZE = 128

HEAD_DIM = 128
MIX_WIDTH = D_MODEL // 2
N_HEADS = MIX_WIDTH // HEAD_DIM
N_BRANCH = 3
CONV_W = 4
D_FF = 4 * D_MODEL
CHUNK = 64
EPS = 1e-6

_SPLIT_SIZES = [MIX_WIDTH] * 4 + [N_HEADS] * 2 \
    + [MIX_WIDTH] * 4 + [N_HEADS] * 2 \
    + [MIX_WIDTH] * 4 \
    + [D_MODEL] * N_BRANCH
IN_COLS = sum(_SPLIT_SIZES)

kernel_name = "hybrid_mlstm_gdn_hgrn2_decode_step"

def rmsnorm(x, w):
    xf = x.astype(jnp.float32)
    y = xf * lax.rsqrt(jnp.mean(xf * xf, -1, keepdims=True) + EPS)
    return (y * w.astype(jnp.float32)).astype(x.dtype)

def head_rms(x):
    return x * lax.rsqrt(jnp.mean(x * x, -1, keepdims=True) + EPS)

def l2n(x):
    return x * lax.rsqrt(jnp.sum(x * x, -1, keepdims=True) + EPS)

def heads(x):
    b, t, _ = x.shape
    return x.reshape(b, t, N_HEADS, HEAD_DIM).transpose(0, 2, 1, 3)

def unheads(x):
    b, h, t, d = x.shape
    return x.transpose(0, 2, 1, 3).reshape(b, t, h * d)

def to_chunks(x, c):
    b, h, t = x.shape[:3]
    x = x.reshape(b, h, t // c, c, *x.shape[3:])
    return jnp.moveaxis(x, 2, 0)

def from_chunks(y):
    y = jnp.moveaxis(y, 0, 2)
    return y.reshape(y.shape[0], y.shape[1], -1, *y.shape[4:])

def split_cols(proj):
    idx = [int(i) for i in np.cumsum(_SPLIT_SIZES)[:-1]]
    return jnp.split(proj, idx, axis=-1)

def mlstm_scan(q, k, v, i_log, f_log, C0, n0, m0):
    t_len = q.shape[2]
    c = math.gcd(t_len, CHUNK)
    causal = jnp.tril(jnp.ones((c, c), bool))

    def step(carry, inp):
        C, n, m = carry
        qc, kc, vc, ic, fc = inp
        b = jnp.cumsum(fc, -1)
        a = b + m[..., None]
        D = b[..., :, None] - b[..., None, :] + ic[..., None, :]
        D = jnp.where(causal, D, -jnp.inf)
        mt = jnp.maximum(a, jnp.max(D, -1))
        P = jnp.einsum('bhtd,bhsd->bhts', qc, kc) * jnp.exp(D - mt[..., None])
        w_st = jnp.exp(a - mt)
        num = jnp.einsum('bhts,bhsv->bhtv', P, vc) + w_st[..., None] * jnp.einsum('bhtk,bhkv->bhtv', qc, C)
        den = jnp.sum(P, -1) + w_st * jnp.einsum('bhtk,bhk->bht', qc, n)
        h = num / jnp.maximum(jnp.abs(den), jnp.exp(-mt))[..., None]
        m_new = mt[..., -1]
        ws = jnp.exp(D[..., -1, :] - m_new[..., None])
        wc = jnp.exp(a[..., -1] - m_new)
        C_new = wc[..., None, None] * C + jnp.einsum('bhs,bhsk,bhsv->bhkv', ws, kc, vc)
        n_new = wc[..., None] * n + jnp.einsum('bhs,bhsk->bhk', ws, kc)
        return (C_new, n_new, m_new), h

    xs = tuple(to_chunks(z, c) for z in (q, k, v, i_log, f_log))
    (C, n, m), h = lax.scan(step, (C0, n0, m0), xs)
    return from_chunks(h), C, n, m

def gdn_scan(q, k, v, beta, logg, S0):
    t_len = q.shape[2]
    dv = v.shape[-1]
    c = math.gcd(t_len, CHUNK)
    incl = jnp.tril(jnp.ones((c, c), bool))
    strict = jnp.tril(jnp.ones((c, c), bool), -1)
    eye = jnp.eye(c, dtype=jnp.float32)

    def step(S, inp):
        qc, kc, vc, bc, gc = inp
        G = jnp.cumsum(gc, -1)
        decay = jnp.exp(jnp.where(incl, G[..., :, None] - G[..., None, :], -jnp.inf))
        kk = jnp.einsum('bhtd,bhsd->bhts', kc, kc)
        A = eye + jnp.where(strict, bc[..., :, None] * kk * decay, 0.0)
        rhs = jnp.concatenate([bc[..., None] * vc, (bc * jnp.exp(G))[..., None] * kc], -1)
        sol = lax.linalg.triangular_solve(A, rhs, left_side=True, lower=True, unit_diagonal=True)
        u, w = sol[..., :dv], sol[..., dv:]
        v_new = u - jnp.einsum('bhtk,bhkv->bhtv', w, S)
        qk = jnp.einsum('bhtd,bhsd->bhts', qc, kc) * decay
        o = jnp.einsum('bhtk,bhkv->bhtv', qc * jnp.exp(G)[..., None], S) \
            + jnp.einsum('bhts,bhsv->bhtv', qk, v_new)
        GL = G[..., -1]
        S_new = jnp.exp(GL)[..., None, None] * S \
            + jnp.einsum('bhsk,bhsv->bhkv', kc * jnp.exp(GL[..., None] - G)[..., None], v_new)
        return S_new, o

    xs = tuple(to_chunks(z, c) for z in (q, k, v, beta, logg))
    S, o = lax.scan(step, S0, xs)
    return from_chunks(o), S

def hgrn_scan(q, k, v, f_log, S0):
    t_len = q.shape[2]
    c = math.gcd(t_len, CHUNK)
    incl = jnp.tril(jnp.ones((c, c), bool))

    def step(S, inp):
        qc, kc, vc, fc = inp
        Bc = jnp.cumsum(fc, 2)
        diff = Bc[:, :, :, None, :] - Bc[:, :, None, :, :]
        diff = jnp.where(incl[..., None], diff, -jnp.inf)
        A = jnp.einsum('bhtk,bhsk,bhtsk->bhts', qc, kc, jnp.exp(diff))
        o = jnp.einsum('bhtk,bhkv->bhtv', qc * jnp.exp(Bc), S) + jnp.einsum('bhts,bhsv->bhtv', A, vc)
        BL = Bc[:, :, -1]
        S_new = jnp.exp(BL)[..., None] * S \
            + jnp.einsum('bhsk,bhsv->bhkv', kc * jnp.exp(BL[:, :, None] - Bc), vc)
        return S_new, o

    xs = tuple(to_chunks(z, c) for z in (q, k, v, f_log))
    S, o = lax.scan(step, S0, xs)
    return from_chunks(o), S

def mixer(xn, p, st):
    f32 = jnp.float32
    t_len = xn.shape[1]
    proj = jnp.einsum('btd,dc->btc', xn, p['w_in']).astype(f32)
    (ml_q, ml_k, ml_v, ml_o, ml_i, ml_f,
     gd_q, gd_k, gd_v, gd_z, gd_b, gd_a,
     hg_q, hg_f, hg_i, hg_g,
     gate_a, gate_b, gate_c) = split_cols(proj)
    C0, n0, m0, S0_gd, conv0, S0_hg = st

    i_log = jnp.swapaxes(ml_i + p['ml_i_bias'].astype(f32), 1, 2)
    f_log = jnp.swapaxes(jax.nn.log_sigmoid(ml_f + p['ml_f_bias'].astype(f32)), 1, 2)
    h, C1, n1, m1 = mlstm_scan(heads(ml_q), heads(ml_k) * HEAD_DIM ** -0.5, heads(ml_v),
                               i_log, f_log, C0.astype(f32), n0.astype(f32), m0.astype(f32))
    y_ml = unheads(head_rms(h)) * p['ml_norm_w'].astype(f32) * jax.nn.sigmoid(ml_o)

    qkv = jnp.concatenate([gd_q, gd_k, gd_v], -1)
    buf = jnp.concatenate([conv0.astype(f32), qkv], 1)
    cw = p['gd_conv_w'].astype(f32)
    conv = sum(buf[:, j:j + t_len] * cw[j] for j in range(CONV_W))
    conv = jax.nn.silu(conv)
    conv1 = buf[:, t_len:]
    cq, ck, cv = jnp.split(conv, 3, axis=-1)
    beta = jnp.swapaxes(jax.nn.sigmoid(gd_b), 1, 2)
    logg = jnp.swapaxes(-jnp.exp(p['gd_A_log'].astype(f32))
                        * jax.nn.softplus(gd_a + p['gd_dt_bias'].astype(f32)), 1, 2)
    o_gd, S1_gd = gdn_scan(l2n(heads(cq)) * HEAD_DIM ** -0.5, l2n(heads(ck)), heads(cv),
                           beta, logg, S0_gd.astype(f32))
    y_gd = unheads(head_rms(o_gd) * p['gd_norm_w'].astype(f32)) * jax.nn.silu(gd_z)

    lb = p['hg_lb'].astype(f32)
    g_f = lb + (1.0 - lb) * jax.nn.sigmoid(hg_f)
    k_hg = (1.0 - lb) * jax.nn.sigmoid(-hg_f)
    o_hg, S1_hg = hgrn_scan(heads(jax.nn.silu(hg_q)), heads(k_hg), heads(hg_i),
                            heads(jnp.log(g_f)), S0_hg.astype(f32))
    y_hg = rmsnorm(unheads(o_hg), p['hg_norm_w']) * jax.nn.silu(hg_g)

    ys = jnp.stack([y_ml, y_gd, y_hg], 2)
    br = jnp.einsum('btnw,nwd->btnd', ys, p['w_branch'].astype(f32))
    gates = jax.nn.sigmoid(jnp.stack([gate_a, gate_b, gate_c], 2))
    merged = jnp.sum(gates * br, 2).astype(xn.dtype)
    out = jnp.einsum('btd,de->bte', merged, p['w_out'])
    return out, (C1, n1, m1, S1_gd, conv1, S1_hg)

def run_group(x, states, params):
    new = [[] for _ in range(len(states))]
    for l in range(DEPTH):
        p = {name: arr[l] for name, arr in params.items()}
        mix, st = mixer(rmsnorm(x, p['norm1_w']), p, tuple(s[l] for s in states))
        x = x + mix
        xn = rmsnorm(x, p['norm2_w'])
        hid = jnp.square(jax.nn.relu(xn @ p['w_up']))
        x = x + hid @ p['w_down']
        for lst, s in zip(new, st):
            lst.append(s)
    return x, tuple(jnp.stack(s) for s in new)

def setup_inputs(seed: int = 0) -> dict:
    key = jax.random.key(seed)
    ks = iter(jax.random.split(key, 32))

    def nrm(shape, s):
        return jax.random.normal(next(ks), shape, jnp.float32) * s

    W, H, Dh, D = MIX_WIDTH, N_HEADS, HEAD_DIM, D_MODEL
    dt = jnp.exp(jax.random.uniform(next(ks), (DEPTH, H), jnp.float32, math.log(1e-3), math.log(1e-1)))
    inp = {}
    inp['x_prompt'] = nrm((BATCH, SEQ, D), 1.0)
    inp['x_sample'] = nrm((DEC_BATCH, DEC_SEQ, D), 1.0)
    inp['state_mlstm_C'] = nrm((DEPTH, DEC_BATCH, H, Dh, Dh), 0.3)
    inp['state_mlstm_n'] = nrm((DEPTH, DEC_BATCH, H, Dh), 0.3)
    inp['state_mlstm_m'] = nrm((DEPTH, DEC_BATCH, H), 1.0)
    inp['state_gdn_S'] = nrm((DEPTH, DEC_BATCH, H, Dh, Dh), 0.3)
    inp['state_gdn_conv'] = nrm((DEPTH, DEC_BATCH, CONV_W - 1, 3 * W), 1.0)
    inp['state_hgrn_S'] = nrm((DEPTH, DEC_BATCH, H, Dh, Dh), 0.5)
    inp['norm1_w'] = 1.0 + nrm((DEPTH, D), 0.1)
    inp['w_in'] = nrm((DEPTH, D, IN_COLS), D ** -0.5)
    inp['ml_i_bias'] = nrm((DEPTH, H), 0.1)
    inp['ml_f_bias'] = jnp.linspace(3.0, 6.0, H, dtype=jnp.float32) + nrm((DEPTH, H), 0.1)
    inp['ml_norm_w'] = 1.0 + nrm((DEPTH, W), 0.1)
    inp['gd_conv_w'] = nrm((DEPTH, CONV_W, 3 * W), 0.5)
    inp['gd_A_log'] = jnp.log(jax.random.uniform(next(ks), (DEPTH, H), jnp.float32, 1.0, 16.0))
    inp['gd_dt_bias'] = dt + jnp.log(-jnp.expm1(-dt))
    inp['gd_norm_w'] = 1.0 + nrm((DEPTH, Dh), 0.1)
    inp['hg_lb_logits'] = nrm((DEPTH, W), 0.5)
    inp['hg_norm_w'] = 1.0 + nrm((DEPTH, W), 0.1)
    inp['w_branch'] = nrm((DEPTH, N_BRANCH, W, D), W ** -0.5)
    inp['w_out'] = nrm((DEPTH, D, D), D ** -0.5)
    inp['norm2_w'] = 1.0 + nrm((DEPTH, D), 0.1)
    inp['w_up'] = nrm((DEPTH, D, D_FF), D ** -0.5)
    inp['w_down'] = nrm((DEPTH, D_FF, D), 0.5 * D_FF ** -0.5)
    inp['final_norm_w'] = 1.0 + nrm((D,), 0.1)
    return inp

def reference(x_prompt, x_sample, state_mlstm_C, state_mlstm_n, state_mlstm_m, state_gdn_S,
              state_gdn_conv, state_hgrn_S, norm1_w, w_in, ml_i_bias, ml_f_bias, ml_norm_w,
              gd_conv_w, gd_A_log, gd_dt_bias, gd_norm_w, hg_lb_logits, hg_norm_w, w_branch,
              w_out, norm2_w, w_up, w_down, final_norm_w):
    f32 = jnp.float32
    sm = jax.nn.softmax(hg_lb_logits.astype(f32), axis=0)
    hg_lb = jnp.cumsum(sm, axis=0) - sm[0:1]
    params = dict(norm1_w=norm1_w, w_in=w_in, ml_i_bias=ml_i_bias, ml_f_bias=ml_f_bias,
                  ml_norm_w=ml_norm_w, gd_conv_w=gd_conv_w, gd_A_log=gd_A_log,
                  gd_dt_bias=gd_dt_bias, gd_norm_w=gd_norm_w, hg_lb=hg_lb, hg_norm_w=hg_norm_w,
                  w_branch=w_branch, w_out=w_out, norm2_w=norm2_w, w_up=w_up, w_down=w_down)

    bp = x_prompt.shape[0]
    zero_states = (jnp.zeros((DEPTH, bp, N_HEADS, HEAD_DIM, HEAD_DIM), f32),
                   jnp.zeros((DEPTH, bp, N_HEADS, HEAD_DIM), f32),
                   jnp.zeros((DEPTH, bp, N_HEADS), f32),
                   jnp.zeros((DEPTH, bp, N_HEADS, HEAD_DIM, HEAD_DIM), f32),
                   jnp.zeros((DEPTH, bp, CONV_W - 1, 3 * MIX_WIDTH), f32),
                   jnp.zeros((DEPTH, bp, N_HEADS, HEAD_DIM, HEAD_DIM), f32))
    hp, (p_mC, p_mn, p_mm, p_gS, p_gc, p_hS) = run_group(x_prompt, zero_states, params)
    y_prompt = rmsnorm(hp, final_norm_w)

    past = (state_mlstm_C, state_mlstm_n, state_mlstm_m, state_gdn_S, state_gdn_conv, state_hgrn_S)
    hs, (s_mC, s_mn, s_mm, s_gS, s_gc, s_hS) = run_group(x_sample, past, params)
    y_sample = rmsnorm(hs, final_norm_w)

    return (y_prompt, y_sample, p_mC, p_mn, p_mm, p_gS, p_gc, p_hS,
            s_mC, s_mn, s_mm, s_gS, s_gc, s_hS)


_drawn_inputs = setup_inputs


def setup_inputs(seed=0):
    import zlib

    import numpy as np

    out = dict(_drawn_inputs(seed))
    spreads = {}
    factors = {}
    for name, (base, spread) in spreads.items():
        noise = np.random.default_rng([zlib.crc32(name.encode()), seed]).standard_normal(out[name].shape)
        drawn = base * np.exp(spread * noise) if base else spread * noise
        out[name] = __import__('jax').numpy.asarray(drawn.astype(out[name].dtype))
    for name, factor in factors.items():
        out[name] = (out[name] * factor).astype(out[name].dtype)
    return out
```

```python
import math
from contextlib import ExitStack

import numpy as np

import concourse.bass as bass
from concourse import mybir

ALU = mybir.AluOpType
ACT = mybir.ActivationFunctionType
F32 = mybir.dt.float32
F32R = mybir.dt.float32r

P = 128
D_MODEL = 1024
SEQ = 1024
DEC_BATCH = 8
DEC_SEQ = 4
NS = DEC_BATCH * DEC_SEQ
T = SEQ + NS
W_MIX = D_MODEL // 2
H = 4
HD = 128
CONV_W = 4
HALO = CONV_W - 1
D_FF = 4 * D_MODEL
EPS = 1e-6
KT = D_MODEL // P
CH = 128
NCH = SEQ // CH
TG = 3
GN = T // TG
NPIECE = 3
ROWS_TILE = 0
HG_TILE = 1
GD_TILE = HG_TILE + 16
ML_TILE = GD_TILE + 16
GATE_TILE = ML_TILE + 16
NPROJ = GATE_TILE + 24
FB = 8
FT = D_FF // P // FB
CLAMP = -44.0
MASKED = -1e30
HALVES = [1, 2, 4, 8, 16, 32, 64]
ML, GD, HG = range(3)
ROW_U, ROW_ELW, ROW_EM, ROW_G, ROW_BETA, ROW_EG, ROW_BEG = range(7)
TOK_W, TOK_EWS, TOK_NG, TOK_BETA, TOK_KD = range(5)
PC_N1, PC_N2, PC_NF, PC_MLN, PC_GDN, PC_HGN, PC_LB, PC_CONV = 0, 8, 16, 24, 28, 29, 33, 37
PC_ALL = PC_CONV + CONV_W * 12
CC_ID, CC_ONE, CC_NEGP, CC_NEGS, CC_LEV, CC_SEGP, CC_SEGS, CC_IND = 0, 128, 256, 384, 416, 1312, 1824, 1952
CC_HGP = 1960
CC_HGS = CC_HGP + 7 * 256
CC_ALL = CC_HGS + 2 * 64


def lin(const, step, i):
    return i * step + const


class Steps:

    def __init__(self, sem, names, credit=0):
        self.sem, self.names, self.credit, self.at = sem, names, credit, 0

    def step(self, name):
        assert self.names[self.at % len(self.names)] == name, (name, self.names[self.at % len(self.names)])
        self.at += 1
        return self.sem, 1

    def after(self, name, n=0):
        return self.sem, lin(self.names.index(name) + 1 + self.credit, len(self.names), n)

    def all_of(self, n):
        return self.sem, lin(self.credit, len(self.names), n)


class Tile:

    def __init__(self, base, step=0, i=0):
        self.base, self.stride, self.i = base, step, i

    def next(self, k=1):
        return Tile(self.base + k, self.stride, self.i)

    @property
    def slot(self):
        return self.base % 2

    def number(self, times=1, plus=0):
        return lin(self.base * times + plus, self.stride * times, self.i)

    def uses(self, plus=0):
        return lin(self.base // 2 + plus, self.stride // 2, self.i)

    def bank(self, g):
        return (TG * self.base + g) % 2

    def bank_uses(self, g, plus=0):
        return lin((TG * self.base + g) // 2 + plus, TG * self.stride // 2, self.i)


def build(nc, xT, w_proj, w_half, w_full, par, con, rowpar, segrow, m0, conv0, st_ml, st_mn, st_gd, st_hg,
          yT, p_C, p_n, p_m, p_S, p_conv, p_H, s_C, s_n, s_m, s_S, s_conv, s_H):
    proj = nc.dram_tensor("proj", (NPROJ, P, HALO + T), F32, kind="Internal").ap()
    rowd = nc.dram_tensor("rowd", (7, H, T), F32, kind="Internal").ap()
    yd = nc.dram_tensor("yd", (12, P, T), F32, kind="Internal").ap()
    with ExitStack() as ctx:
        def sb(name, shape, dt=F32):
            return ctx.enter_context(nc.sbuf_tensor(name, shape, dt))

        def sem(name):
            return ctx.enter_context(nc.semaphore(name))

        xn_hi, xn_lo = sb("xn_hi", [P, KT, T], F32R), sb("xn_lo", [P, KT, T], F32R)
        w_raw = sb("w_raw", [P, 2, KT * P])
        w_hi, w_lo = [sb(f"w_hi{s}", [P, KT, P], F32R) for s in range(2)], [sb(f"w_lo{s}", [P, KT, P], F32R) for s in range(2)]
        stage = sb("stage", [P, 2, T])
        cst = sb("cst", [P, CC_ALL])
        prm = sb("prm", [P, PC_ALL])
        tok = sb("tok", [P, 5, NCH + 1, H])
        tokc = sb("tokc", [P, 5, H])
        lbt = sb("lbt", [P, 6, H])
        halo0 = sb("halo0", [P, 12 * HALO])
        ident, ones = cst[:, CC_ID:CC_ID + P], cst[:, CC_ONE:CC_ONE + P]

        arena_of = {}

        def arena(stack, name, shape, dt=F32):
            arena_of[name] = stack.enter_context(nc.sbuf_tensor(name, shape, dt))
            return arena_of[name]

        with ExitStack() as a:
            xin = arena(a, "xin", [P, KT, T])
            nsq = arena(a, "nsq", [P, T])
            ntmp = arena(a, "ntmp", [P, T])
            nrs = arena(a, "nrs", [P, T])
        with ExitStack() as a:
            r_in = arena(a, "r_in", [H, 4, T])
            r_a = arena(a, "r_a", [H, 3, T])
            r_b = arena(a, "r_b", [H, 2, T])
            r_m = arena(a, "r_m", [H, T])
            r_row = arena(a, "r_row", [H, 7, T])
            r_tok = arena(a, "r_tok", [H, 5, T])
            r_mp = arena(a, "r_mp", [H, 2 * NCH])
            r_t8 = arena(a, "r_t8", [H, DEC_BATCH])
            r_mo = arena(a, "r_mo", [H, 1 + DEC_BATCH])
            r_par = arena(a, "r_par", [H, 5])
        N4 = H * CH
        with ExitStack() as a:
            g_in = arena(a, "g_in", [P, 3 * N4])
            g_v = arena(a, "g_v", [P, N4])
            g_x = arena(a, "g_x", [P, 3 * N4])
            g_sg = arena(a, "g_sg", [P, 3 * N4])
            g_sl = arena(a, "g_sl", [P, 2 * N4])
            g_k = arena(a, "g_k", [P, N4])
            g_lf = arena(a, "g_lf", [P, N4])
            g_b = arena(a, "g_b", [P, N4])
            g_dq = arena(a, "g_dq", [P, 7 * 256])
            g_dk = arena(a, "g_dk", [P, 7 * 256])
            g_e2 = arena(a, "g_e2", [P, 2, N4])
            g_ql = arena(a, "g_ql", [P, 7 * 256])
            g_kl = arena(a, "g_kl", [P, 7 * N4])
            g_vt = arena(a, "g_vt", [P, N4])
            g_rr = arena(a, "g_rr", [P, CH])
            g_S = arena(a, "g_S", [P, N4])
            g_Ss = arena(a, "g_Ss", [P, DEC_BATCH, H, HD])
            g_at, g_kt, g_mm, g_y, g_vx = g_v, g_b, g_dq, g_k, g_dq
        with ExitStack() as a:
            d_ch = arena(a, "d_ch", [P, 12 * (CH + HALO)])
            d_sx = arena(a, "d_sx", [P, 12, DEC_BATCH, HALO + DEC_SEQ])
            d_cv = arena(a, "d_cv", [P, 16 * CH])
            d_pa = arena(a, "d_pa", [P, 16 * CH])
            d_pb = arena(a, "d_pb", [P, 16 * CH])
            d_qk = arena(a, "d_qk", [P, 2 * N4])
            d_bc = arena(a, "d_bc", [P, 4 * N4])
            d_de = arena(a, "d_de", [P, N4])
            d_at = arena(a, "d_at", [P, N4])
            d_lt = arena(a, "d_lt", [P, N4])
            d_mt = arena(a, "d_mt", [P, 7 * N4])
            d_tt = arena(a, "d_tt", [P, N4])
            d_t = arena(a, "d_t", [P, N4])
            d_vb = arena(a, "d_vb", [P, N4])
            d_kd = arena(a, "d_kd", [P, N4])
            d_r = arena(a, "d_r", [P, N4])
            d_S = arena(a, "d_S", [P, N4])
            d_Ss = arena(a, "d_Ss", [P, DEC_BATCH, H, HD])
            d_xs, d_vn = d_de, d_lt
        with ExitStack() as a:
            m_in = arena(a, "m_in", [P, 4 * N4])
            m_bc = arena(a, "m_bc", [P, 3 * N4])
            m_ks = arena(a, "m_ks", [P, N4])
            m_e = arena(a, "m_e", [P, N4])
            m_pt = arena(a, "m_pt", [P, N4])
            m_so = arena(a, "m_so", [P, N4])
            m_gw = arena(a, "m_gw", [P, N4])
            m_qw = arena(a, "m_qw", [P, N4])
            m_vt = arena(a, "m_vt", [P, N4])
            m_kt = arena(a, "m_kt", [P, N4])
            m_dn = arena(a, "m_dn", [P, N4])
            m_rd = arena(a, "m_rd", [P, N4])
            m_h = arena(a, "m_h", [P, N4])
            m_sq = arena(a, "m_sq", [P, N4])
            m_y = arena(a, "m_y", [P, N4])
            m_C = arena(a, "m_C", [P, N4])
            m_N = arena(a, "m_N", [P, N4])
            m_no = arena(a, "m_no", [P, H])
            m_Cs = arena(a, "m_Cs", [P, DEC_BATCH, H, HD])
            m_Ns = arena(a, "m_Ns", [P, DEC_BATCH, H])
            m_Nb = arena(a, "m_Nb", [P, DEC_BATCH, H, HD])
            m_vx = arena(a, "m_vx", [NS, DEC_BATCH * HD])
        with ExitStack() as a:
            acc = arena(a, "acc", [P, KT, T])
            y_hi = arena(a, "y_hi", [P, 4, T], F32R)
            y_lo = arena(a, "y_lo", [P, 4, T], F32R)
            e_a = arena(a, "e_a", [P, T])
            e_b = arena(a, "e_b", [P, T])
            e_c = arena(a, "e_c", [P, T])

        D = [ctx.enter_context(nc.psum_tensor(f"D{i}", [P, 512], F32)) for i in range(2)]
        M = [ctx.enter_context(nc.psum_tensor(f"M{i}", [P, 512], F32)) for i in range(6)]

        const_ld, x_ld = sem("const_ld"), sem("x_ld")
        w_loaded = [sem(f"w_loaded{s}") for s in range(2)]
        w_hi_made, w_lo_made, groups_done = sem("w_hi_made"), sem("w_lo_made"), sem("groups_done")
        bank_free = [sem(f"bank_free{b}") for b in range(2)]
        evacuated = sem("evacuated")
        stage_stored = [sem(f"stage_stored{s}") for s in range(2)]

        def steps(name, names, credit=0):
            return Steps(sem(name), names.split(), credit)

        def load_w(sp, t, src, kt=KT):
            if not (isinstance(t.i, int) and t.base < 2):
                sp.wait_ge(w_lo_made, t.number(plus=-1))
            sp.dma_start(w_raw[:, t.slot, 0:kt * P], src).then_inc(w_loaded[t.slot], 16)

        def make_hi(act, t, kt=KT):
            if not (isinstance(t.i, int) and t.base < 2):
                act.wait_ge(groups_done, t.number(TG, -TG))
            act.wait_ge(w_loaded[t.slot], lin(16 * (t.base // 2 + 1), 8 * t.stride, t.i))
            nc.scalar.activation(w_hi[t.slot][:, 0:kt, :], w_raw[:, t.slot, 0:kt * P].rearrange("p (k m) -> p k m", m=P),
                                 ACT.Copy).then_inc(w_hi_made, 1)

        def make_lo(pool, t, kt=KT):
            pool.wait_ge(w_hi_made, t.number(plus=1))
            nc.gpsimd.tensor_tensor(w_lo[t.slot][:, 0:kt, :], w_raw[:, t.slot, 0:kt * P].rearrange("p (k m) -> p k m", m=P),
                                    w_hi[t.slot][:, 0:kt, :].bitcast(F32), ALU.subtract).then_inc(w_lo_made, 1)

        def dense(pe, t, g, third, kt=KT, src=None):
            hi, lo = src or (xn_hi, xn_lo)
            b = t.bank(g)
            ks = range(kt) if third is None else range(kt * third // NPIECE, kt * (third + 1) // NPIECE)
            if ks[0] == 0:
                if g == 0:
                    pe.wait_ge(w_lo_made, t.number(plus=1))
                pe.wait_ge(bank_free[b], t.bank_uses(g, 1))
            cols = slice(g * GN, (g + 1) * GN)
            for k in ks:
                last = None
                for n, (w, x) in enumerate(((w_hi, hi), (w_hi, lo), (w_lo, hi))):
                    last = nc.tensor.matmul(D[b][:, 0:GN], w[t.slot][:, k, :], x[:, k, cols],
                                            start=(k == 0 and n == 0), stop=(k == kt - 1 and n == 2))
                if k == kt - 1:
                    last.then_inc(groups_done, 1)

        def evac_proj(act, t, g):
            if g == 0 and not (isinstance(t.i, int) and t.base < 2):
                act.wait_ge(stage_stored[t.slot], lin(16 * (t.base // 2), 8 * t.stride, t.i))
            act.wait_ge(groups_done, t.number(TG, g + 1))
            nc.scalar.activation(stage[:, t.slot, g * GN:(g + 1) * GN], D[t.bank(g)][:, 0:GN],
                                 ACT.Copy).then_inc(bank_free[t.bank(g)], 1)
            if g == TG - 1:
                act.wait_ge(bank_free[t.bank(2)], t.bank_uses(2, 2))
                act.wait_ge(bank_free[t.bank(1)], t.bank_uses(1, 2))
                act.dma_start(proj[t.number(), :, HALO:HALO + T], stage[:, t.slot, :]).then_inc(stage_stored[t.slot], 16)

        def stored_all(eng, n_tiles):
            eng.wait_ge(stage_stored[0], 16 * ((n_tiles + 1) // 2))
            eng.wait_ge(stage_stored[1], 16 * (n_tiles // 2))

        class Filler:
            def __init__(self, kind, eng, tile, n_tiles, n_slots, last_kt=KT):
                self.last_kt, self.kind, self.eng, self.tile, self.n, self.slots, self.at = last_kt, kind, eng, tile, n_tiles, n_slots, 0

            def __call__(self):
                pieces = self.n * TG * NPIECE
                a, b = pieces * self.at // self.slots, pieces * (self.at + 1) // self.slots
                self.at += 1
                for j in range(a, b):
                    t = self.tile.next(j // (TG * NPIECE))
                    next_kt = self.last_kt if j // (TG * NPIECE) == self.n - 1 else KT
                    g, third = j % (TG * NPIECE) // NPIECE, j % NPIECE
                    if self.kind == "pe":
                        dense(self.eng, t, g, third)
                    elif self.kind == "act":
                        if g == 0 and third == 0:
                            make_hi(self.eng, t.next(), next_kt)
                        if third == NPIECE - 1:
                            evac_proj(self.eng, t, g)
                    elif self.kind == "pool":
                        if g == 0 and third == 0:
                            make_lo(self.eng, t.next(), next_kt)

            def done(self):
                assert self.at == self.slots, (self.at, self.slots)

        hg_in = sem("hg_in")
        hg_pe = steps("hg_pe", "vt diag lev kt o kv ss", credit=1)
        hg_act = steps("hg_act", "e l s lf eq ek eb ed vt kt sq rl rr", credit=1)
        hg_dve = steps("hg_dve", "cl sl g1 g2 b " + " ".join(f"dq{j}" for j in range(7)) + " "
                       + " ".join(f"ql{j}" for j in range(7)) + " qe at mk0 mk1 mk2 mk3 "
                       + " ".join(f"ad{j}" for j in range(7)) + " s1 s2 y1 y2", credit=1)
        hg_pool = steps("hg_pool", "k1 k2 gw " + " ".join(f"dk{j}" for j in range(7)) + " dl "
                        + " ".join(f"kl{j}" for j in range(7)) + " kd", credit=1)
        hg_out = sem("hg_out")
        hs_in = sem("hs_in")
        hs_st = sem("hs_st")
        hs_pe = steps("hs_pe", "vt diag lev kt o ss " + " ".join(f"kv{h}" for h in range(H)))
        hs_act = steps("hs_act", "e l s lf eq ek eb ed vt kt sq rl rr")
        hs_dve = steps("hs_dve", "cl sl g1 g2 b dq0 dq1 ql0 ql1 qe at mk0 ad0 ad1 y1 y2 "
                       + " ".join(f"vx{h} s1{h} s2{h}a s2{h}b" for h in range(H)))
        hs_pool = steps("hs_pool", "k1 k2 gw dk0 dk1 dl kl0 kl1 kd")
        lb_dve, lb_act = steps("lb_dve", "d r n lb om"), steps("lb_act", "e")

        def pcols(tile, ntile, col, n):
            v = proj[tile:tile + ntile].rearrange("t p c -> p t c")
            return v[:, :, bass.ds(col, n)]

        def ycols(branch, col, n):
            return yd[4 * branch:4 * branch + 4].rearrange("t p c -> p t c")[:, :, bass.ds(col, n)]

        def next_chunk(n):
            return (None, 0) if n is None else (n, n * CH + CH)

        def prefetch(eng, prev, step):
            if prev is not None:
                eng.wait_ge(*step[0].after(step[1], prev))

        def after_chunks(eng, n, of, out):
            for s in of:
                eng.wait_ge(*s.all_of(n))
            eng.wait_ge(out, lin(16, 16, n))

        def hgrn(kind, eng, n, slot, sample):
            N = NS if sample else CH
            C4 = H * N
            halves = HALVES[:2] if sample else HALVES
            L = len(halves)
            HF = C4 // 2
            pe_, act_, dve_, pool_ = (hs_pe, hs_act, hs_dve, hs_pool) if sample else (hg_pe, hg_act, hg_dve, hg_pool)
            col0 = SEQ if sample else None if n is None else n * CH

            def hn(x, o=0):
                return x[:, o:o + C4].rearrange("p (h n) -> p h n", n=N)

            def blk(x, hf, o=0):
                return x[:, o:o + C4].rearrange("p (b c) -> p b c", c=2 * hf)

            def cb(x, hf, o):
                return x[:, o:o + HF].rearrange("p (b c) -> p b c", c=hf)

            def tk(x, h=None):
                v = x[0:N, :].rearrange("p (h n) -> p h n", n=HD)
                return v if h is None else v[:, h, :]

            if kind == "sp":
                sm = hs_in if sample else hg_in
                if sample:
                    for s in (hg_pe, hg_act, hg_dve, hg_pool):
                        eng.wait_ge(*s.all_of(NCH))
                    eng.wait_ge(hg_out, 16 * (NCH + 1))
                else:
                    n, col0 = next_chunk(n)
                    prefetch(eng, n, (dve_, "sl"))
                for i, tile in enumerate((0, 12, 4)):
                    eng.dma_start(hn(g_in, i * C4), pcols(HG_TILE + tile, 4, lin(HALO, 1, col0), N)).then_inc(sm, 16)
                if not sample:
                    prefetch(eng, n, (pe_, "o"))
                eng.dma_start(hn(g_v), pcols(HG_TILE + 8, 4, lin(HALO, 1, col0), N)).then_inc(sm, 16)
                return
            loaded = (hs_in, 64) if sample else None if n is None else (hg_in, lin(64, 64, n))
            if not sample:
                after_chunks(eng, n, [x for k, x in (("pe", pe_), ("act", act_), ("dve", dve_), ("pool", pool_)) if k != kind], hg_out)
            if kind == "act":
                eng.wait_ge(*dve_.after("cl", n))
                eng.activation(g_x[:, 0:3 * C4], g_x[:, 0:3 * C4], ACT.Exp, scale=-1.0).then_inc(*act_.step("e"))
                eng.wait_ge(*act_.after("e", n))
                eng.activation(g_sg[:, 0:3 * C4], g_x[:, 0:3 * C4], ACT.Ln, bias=1.0).then_inc(*act_.step("l"))
                eng.wait_ge(*act_.after("l", n))
                eng.activation(g_sg[:, 0:3 * C4], g_sg[:, 0:3 * C4], ACT.Exp, scale=-1.0).then_inc(*act_.step("s"))
                slot()
                eng.wait_ge(*dve_.after("g2", n))
                eng.activation(g_lf[:, 0:C4], g_lf[:, 0:C4], ACT.Ln).then_inc(*act_.step("lf"))
                slot()
                eng.wait_ge(*dve_.after(f"dq{L - 1}", n))
                eng.activation(g_dq[:, 0:L * HF], g_dq[:, 0:L * HF], ACT.Exp).then_inc(*act_.step("eq"))
                eng.wait_ge(*pool_.after("dl", n))
                eng.activation(g_dk[:, 0:L * HF], g_dk[:, 0:L * HF], ACT.Exp).then_inc(*act_.step("ek"))
                eng.activation(g_e2[:, 0, 0:C4], g_b[:, 0:C4], ACT.Exp).then_inc(*act_.step("eb"))
                eng.activation(g_e2[:, 1, 0:C4], g_e2[:, 1, 0:C4], ACT.Exp).then_inc(*act_.step("ed"))
                slot()
                eng.wait_ge(*pe_.after("vt", n))
                eng.activation(g_vt[0:N, :], M[5][0:N, :], ACT.Copy).then_inc(*act_.step("vt"))
                slot()
                eng.wait_ge(*pe_.after("kt", n))
                eng.activation(g_kt[0:N, :], M[0][0:N, :], ACT.Copy).then_inc(*act_.step("kt"))
                slot()
                eng.wait_ge(*pe_.after("o", n))
                eng.activation(g_y[:, 0:C4], M[1][:, 0:C4], ACT.Square).then_inc(*act_.step("sq"))
                slot()
                eng.wait_ge(*pe_.after("ss", n))
                eng.activation(g_rr[:, 0:N], M[3][:, 0:N], ACT.Ln, bias=EPS, scale=1.0 / W_MIX).then_inc(*act_.step("rl"))
                eng.wait_ge(*act_.after("rl", n))
                eng.activation(g_rr[:, 0:N], g_rr[:, 0:N], ACT.Exp, scale=-0.5).then_inc(*act_.step("rr"))
                slot()
                eng.wait_ge(*dve_.after("y2", n))
                eng.dma_start(ycols(HG, col0, N), hn(g_y)).then_inc(hs_st if sample else hg_out, 16)
                slot()
            if kind == "dve":
                eng.wait_ge(*loaded)
                eng.tensor_scalar(g_x[:, 0:3 * C4], g_in[:, 0:3 * C4], CLAMP, None, ALU.max).then_inc(*dve_.step("cl"))
                eng.wait_ge(*act_.after("s", n))
                eng.tensor_tensor(g_sl[:, 0:2 * C4], g_in[:, 0:2 * C4], g_sg[:, 0:2 * C4], ALU.mult).then_inc(*dve_.step("sl"))
                eng.tensor_tensor(hn(g_lf), hn(g_sg, 2 * C4), lbt[:, 5, :].unsqueeze(2).to_broadcast([P, H, N]),
                                  ALU.mult).then_inc(*dve_.step("g1"))
                eng.wait_ge(*dve_.after("g1", n))
                eng.tensor_tensor(hn(g_lf), hn(g_lf), lbt[:, 4, :].unsqueeze(2).to_broadcast([P, H, N]),
                                  ALU.add).then_inc(*dve_.step("g2"))
                slot()
                eng.wait_ge(*act_.after("lf", n))
                seg = cst[:, CC_SEGS:CC_SEGS + C4] if sample else cst[:, CC_SEGP:CC_SEGP + C4]
                eng.tensor_tensor_scan(g_b[:, 0:C4], seg, g_lf[:, 0:C4], 0.0, ALU.mult, ALU.add).then_inc(*dve_.step("b"))
                eng.wait_ge(*dve_.after("b", n))
                for j, hf in enumerate(halves):
                    b = blk(g_b, hf)
                    eng.tensor_tensor(cb(g_dq, hf, j * HF), b[:, :, hf:2 * hf],
                                      b[:, :, hf - 1:hf].to_broadcast([P, C4 // (2 * hf), hf]),
                                      ALU.subtract).then_inc(*dve_.step(f"dq{j}"))
                slot()
                eng.wait_ge(*act_.after("eq", n))
                for j, hf in enumerate(halves):
                    eng.tensor_tensor(cb(g_ql, hf, j * HF), blk(g_sl, hf)[:, :, hf:2 * hf], cb(g_dq, hf, j * HF),
                                      ALU.mult).then_inc(*dve_.step(f"ql{j}"))
                eng.wait_ge(*act_.after("eb", n))
                eng.tensor_tensor(g_x[:, 0:C4], g_sl[:, 0:C4], g_e2[:, 0, 0:C4], ALU.mult).then_inc(*dve_.step("qe"))
                slot()
                eng.wait_ge(*pe_.after("diag", n))
                eng.tensor_tensor(g_at[0:N, 0:C4].rearrange("p (h n) -> p h n", n=N), M[0][0:N, 0:C4].rearrange("p (h n) -> p h n", n=N),
                                  cst[0:N, CC_ID:CC_ID + N].unsqueeze(1).to_broadcast([N, H, N]), ALU.mult).then_inc(*dve_.step("at"))
                eng.wait_ge(*pe_.after("lev", n))
                msk = CC_HGS if sample else CC_HGP
                for q in range((L + 1) // 2):
                    w = min(2, L - 2 * q) * HF
                    eng.tensor_tensor(g_mm[0:N, 2 * q * HF:2 * q * HF + w], M[1 + q][0:N, 0:w],
                                      cst[0:N, msk + 2 * q * HF:msk + 2 * q * HF + w], ALU.mult).then_inc(*dve_.step(f"mk{q}"))
                for j, hf in enumerate(halves):
                    eng.wait_ge(*(dve_.after(f"mk{(L + 1) // 2 - 1}" if j == 0 else f"ad{j - 1}", n)))
                    a = g_at[0:N, 0:C4].rearrange("p (b c) -> p b c", c=2 * hf)[:, :, hf:2 * hf]
                    eng.tensor_tensor(a, a, g_mm[0:N, j * HF:(j + 1) * HF].rearrange("p (b c) -> p b c", c=hf),
                                      ALU.add).then_inc(*dve_.step(f"ad{j}"))
                slot()
                slot()
                if not sample:
                    eng.wait_ge(*pe_.after("o", n))
                    eng.tensor_tensor(hn(g_S), hn(g_S), hn(g_e2[:, 0, :])[:, :, N - 1:N].to_broadcast([P, H, HD]),
                                      ALU.mult).then_inc(*dve_.step("s1"))
                    eng.wait_ge(*dve_.after("s1", n))
                    eng.wait_ge(*pe_.after("kv", n))
                    eng.tensor_tensor(g_S[:, :], g_S[:, :], M[2][:, :], ALU.add).then_inc(*dve_.step("s2"))
                slot()
                eng.wait_ge(*act_.after("rr", n))
                eng.tensor_tensor(hn(g_y), hn(M[1]), g_rr[:, 0:N].unsqueeze(1).to_broadcast([P, H, N]),
                                  ALU.mult).then_inc(*dve_.step("y1"))
                eng.wait_ge(*dve_.after("y1", n))
                eng.wait_ge(*pool_.after("gw", n))
                eng.tensor_tensor(g_y[:, 0:C4], g_y[:, 0:C4], g_sg[:, C4:2 * C4], ALU.mult).then_inc(*dve_.step("y2"))
                slot()
                if sample:
                    for h in range(H):
                        if h:
                            eng.wait_ge(*pe_.after(f"kv{h - 1}", n))
                        else:
                            eng.wait_ge(*act_.after("vt", n))
                        eng.tensor_tensor(g_vx[0:NS, 0:DEC_BATCH * HD].rearrange("p (b v) -> p b v", v=HD),
                                          tk(g_vt, h).unsqueeze(1).to_broadcast([NS, DEC_BATCH, HD]),
                                          cst[0:NS, CC_IND:CC_IND + DEC_BATCH].unsqueeze(2).to_broadcast([NS, DEC_BATCH, HD]),
                                          ALU.mult).then_inc(*dve_.step(f"vx{h}"))
                        if h == 0:
                            eng.wait_ge(*pe_.after("o", n))
                        ends = hn(g_e2[:, 0, :])[:, h, DEC_SEQ - 1::DEC_SEQ].unsqueeze(2).to_broadcast([P, DEC_BATCH, HD])
                        eng.tensor_tensor(g_Ss[:, :, h, :], g_Ss[:, :, h, :], ends, ALU.mult).then_inc(*dve_.step(f"s1{h}"))
                        eng.wait_ge(*dve_.after(f"s1{h}", n))
                        eng.wait_ge(*pe_.after(f"kv{h}", n))
                        for q, x in enumerate("ab"):
                            eng.tensor_tensor(g_Ss[:, 4 * q:4 * q + 4, h, :], g_Ss[:, 4 * q:4 * q + 4, h, :],
                                              M[4 + q][:, :].rearrange("p (b v) -> p b v", v=HD), ALU.add).then_inc(*dve_.step(f"s2{h}{x}"))
                slot()
            if kind == "pool":
                eng.wait_ge(*act_.after("s", n))
                eng.tensor_tensor(g_k[:, 0:C4], g_x[:, 2 * C4:3 * C4], g_sg[:, 2 * C4:3 * C4], ALU.mult).then_inc(*pool_.step("k1"))
                eng.wait_ge(*pool_.after("k1", n))
                eng.tensor_tensor(hn(g_k), hn(g_k), lbt[:, 5, :].unsqueeze(2).to_broadcast([P, H, N]), ALU.mult).then_inc(*pool_.step("k2"))
                eng.wait_ge(*dve_.after("g1", n))
                eng.tensor_tensor(hn(g_sg, C4), hn(g_sl, C4), prm[:, PC_HGN:PC_HGN + H].unsqueeze(2).to_broadcast([P, H, N]),
                                  ALU.mult).then_inc(*pool_.step("gw"))
                slot()
                eng.wait_ge(*dve_.after("b", n))
                for j, hf in enumerate(halves):
                    b = blk(g_b, hf)
                    eng.tensor_tensor(cb(g_dk, hf, j * HF), b[:, :, hf - 1:hf].to_broadcast([P, C4 // (2 * hf), hf]),
                                      b[:, :, 0:hf], ALU.subtract).then_inc(*pool_.step(f"dk{j}"))
                if sample:
                    bb = g_b[:, 0:C4].rearrange("p (g c) -> p g c", c=DEC_SEQ)
                    eng.tensor_tensor(g_e2[:, 1, 0:C4].rearrange("p (g c) -> p g c", c=DEC_SEQ),
                                      bb[:, :, DEC_SEQ - 1:DEC_SEQ].to_broadcast([P, C4 // DEC_SEQ, DEC_SEQ]), bb,
                                      ALU.subtract).then_inc(*pool_.step("dl"))
                else:
                    eng.tensor_tensor(hn(g_e2[:, 1, :]), hn(g_b)[:, :, N - 1:N].to_broadcast([P, H, N]), hn(g_b),
                                      ALU.subtract).then_inc(*pool_.step("dl"))
                slot()
                eng.wait_ge(*act_.after("ek", n))
                for j, hf in enumerate(halves):
                    eng.tensor_tensor(blk(g_kl, hf, j * N4)[:, :, 0:hf], blk(g_k, hf)[:, :, 0:hf], cb(g_dk, hf, j * HF),
                                      ALU.mult).then_inc(*pool_.step(f"kl{j}"))
                eng.wait_ge(*act_.after("ed", n))
                eng.tensor_tensor(g_lf[:, 0:C4], g_k[:, 0:C4], g_e2[:, 1, 0:C4], ALU.mult).then_inc(*pool_.step("kd"))
                slot()
                slot()
                slot()
                slot()
                slot()
                slot()
            if kind == "pe":
                eng.wait_ge(*loaded)
                for h in range(H):
                    i = eng.transpose(M[5][0:N, h * HD:(h + 1) * HD], hn(g_v)[:, h, :], ident)
                i.then_inc(*pe_.step("vt"))
                slot()
                slot()
                eng.wait_ge(*dve_.after("sl", n))
                eng.wait_ge(*pool_.after("k2", n))
                for h in range(H):
                    i = eng.matmul(M[0][0:N, h * N:(h + 1) * N], hn(g_k)[:, h, :], hn(g_sl)[:, h, :], start=True, stop=True)
                i.then_inc(*pe_.step("diag"))
                slot()
                eng.wait_ge(*dve_.after(f"ql{L - 1}", n))
                eng.wait_ge(*pool_.after(f"kl{L - 1}", n))
                for j in range(L):
                    for h in range(H):
                        o = (j % 2) * HF + h * (N // 2)
                        i = eng.matmul(M[1 + j // 2][0:N, o:o + N // 2], hn(g_kl, j * N4)[:, h, :],
                                       g_ql[:, j * HF + h * (N // 2):j * HF + (h + 1) * (N // 2)], start=True, stop=True)
                i.then_inc(*pe_.step("lev"))
                slot()
                eng.wait_ge(*dve_.after("at", n))
                eng.wait_ge(*pool_.after("kd", n))
                for h in range(H):
                    i = eng.transpose(M[0][0:N, h * HD:(h + 1) * HD], hn(g_lf)[:, h, :], ident)
                i.then_inc(*pe_.step("kt"))
                slot()
                eng.wait_ge(*act_.after("vt", n))
                eng.wait_ge(*dve_.after(f"ad{L - 1}", n))
                for h in range(H):
                    i = eng.matmul(M[1][:, h * N:(h + 1) * N], tk(g_vt, h), g_at[0:N, h * N:(h + 1) * N], start=(not sample or h == 0), stop=False, skip_group_check=sample)
                    if sample:
                        for b in range(DEC_BATCH):
                            c = h * N + b * DEC_SEQ
                            i = eng.matmul(M[1][:, c:c + DEC_SEQ], g_Ss[:, b, h, :], g_x[:, c:c + DEC_SEQ],
                                           start=False, stop=(h == H - 1 and b == DEC_BATCH - 1), skip_group_check=True)
                    else:
                        i = eng.matmul(M[1][:, h * N:(h + 1) * N], g_S[:, h * HD:(h + 1) * HD], g_x[:, h * N:(h + 1) * N],
                                       start=False, stop=True)
                i.then_inc(*pe_.step("o"))
                if not sample:
                    eng.wait_ge(*act_.after("kt", n))
                    for h in range(H):
                        i = eng.matmul(M[2][:, h * HD:(h + 1) * HD], tk(g_kt, h), tk(g_vt, h), start=True, stop=True)
                    i.then_inc(*pe_.step("kv"))
                slot()
                eng.wait_ge(*act_.after("sq", n))
                for h in range(H):
                    i = eng.matmul(M[3][:, 0:N], ones, g_y[:, h * N:(h + 1) * N], start=(h == 0), stop=(h == H - 1))
                i.then_inc(*pe_.step("ss"))
                slot()
                if sample:
                    for h in range(H):
                        eng.wait_ge(*act_.after("kt", n))
                        eng.wait_ge(*dve_.after(f"vx{h}", n))
                        if h:
                            eng.wait_ge(*dve_.after(f"s2{h - 1}b", n))
                        for q in range(2):
                            i = eng.matmul(M[4 + q][:, :], tk(g_kt, h), g_vx[0:NS, q * 512:(q + 1) * 512], start=True, stop=True)
                        i.then_inc(*pe_.step(f"kv{h}"))
                slot()

        rw_in, rw_out, rw_mo, seg_ld = sem("rw_in"), sem("rw_out"), sem("rw_mo"), sem("seg_ld")
        rw_act = steps("rw_act", "e l ea be bl bs em elw ews kd eg tok toks")
        rw_dve = steps("rw_dve", "i z az x ax bc mn fl mx sp g bcum gcum m "
                       + " ".join(f"t{k} m{k}" for k in range(DEC_SEQ))
                       + " mp0 mp1 mp2 u w lw1 lw2 em ew1 ew2 ng kd1 kd2 beg mo1 mo2")
        rw_pe = steps("rw_pe", "tok")

        def rows(kind, eng, slot):
            def ends(x):
                return x[:, CH - 1:SEQ:CH], x[:, SEQ + DEC_SEQ - 1:T:DEC_SEQ]

            def cut(x):
                return (x[:, 0:SEQ].rearrange("h (c n) -> h c n", n=CH), x[:, SEQ:T].rearrange("h (c n) -> h c n", n=DEC_SEQ))

            if kind == "sp":
                eng.dma_start(r_mp[:, NCH:2 * NCH], m0).then_inc(rw_in, 16)
                eng.dma_start(r_tok[:, TOK_KD, :], segrow).then_inc(seg_ld, 16)
                eng.dma_start(r_par[:, 0:4], rowpar).then_inc(rw_in, 16)
                stored_rows(eng)
                eng.dma_start(r_in[:, :, :], proj[ROWS_TILE, 0:4 * H, HALO:HALO + T].rearrange("(q h) t -> h q t", h=H)).then_inc(rw_in, 16)
                return
            if kind == "dve":
                eng.wait_ge(rw_in, 48)

                def ts(name, out, in_, s1, s2, o0, o1=None):
                    a = (o0,) if o1 is None else (o0, o1)
                    eng.tensor_scalar(out, in_, s1, s2, *a).then_inc(*rw_dve.step(name))
                    eng.wait_ge(*rw_dve.after(name))

                def tt(name, out, a, b, op):
                    eng.tensor_tensor(out, a, b, op).then_inc(*rw_dve.step(name))
                    eng.wait_ge(*rw_dve.after(name))

                def mag(name, out, x):
                    eng.scalar_tensor_tensor(out, x, -1.0, x, ALU.mult, ALU.max).then_inc(*rw_dve.step(name))
                    eng.wait_ge(*rw_dve.after(name))
                ts("i", r_in[:, 0, :], r_in[:, 0, :], r_par[:, 0:1], None, ALU.add)
                ts("z", r_in[:, 1, :], r_in[:, 1, :], r_par[:, 1:2], None, ALU.add)
                mag("az", r_a[:, 0, :], r_in[:, 1, :])
                ts("x", r_in[:, 3, :], r_in[:, 3, :], r_par[:, 3:4], None, ALU.add)
                mag("ax", r_a[:, 1, :], r_in[:, 3, :])
                ts("bc", r_a[:, 2, :], r_in[:, 2, :], CLAMP, None, ALU.max)
                slot()
                eng.wait_ge(*rw_act.after("l"))
                ts("mn", r_m[:, :], r_in[:, 1, :], 0.0, None, ALU.min)
                tt("fl", r_in[:, 1, :], r_m[:, :], r_a[:, 0, :], ALU.subtract)
                ts("mx", r_m[:, :], r_in[:, 3, :], 0.0, None, ALU.max)
                tt("sp", r_m[:, :], r_m[:, :], r_a[:, 1, :], ALU.add)
                eng.wait_ge(*rw_act.after("ea"))
                ts("g", r_in[:, 3, :], r_m[:, :], r_par[:, 4:5], -1.0, ALU.mult, ALU.mult)
                seg = r_tok[:, TOK_KD, :]
                eng.wait_ge(seg_ld, 16)
                eng.tensor_tensor_scan(r_a[:, 0, :], seg, r_in[:, 1, :], 0.0, ALU.mult, ALU.add).then_inc(*rw_dve.step("bcum"))
                eng.tensor_tensor_scan(r_row[:, ROW_G, :], seg, r_in[:, 3, :], 0.0, ALU.mult, ALU.add).then_inc(*rw_dve.step("gcum"))
                slot()
                eng.tensor_tensor_scan(r_m[:, 0:SEQ], r_in[:, 1, 0:SEQ], r_in[:, 0, 0:SEQ], 0.0, ALU.add,
                                       ALU.max).then_inc(*rw_dve.step("m"))
                for k in range(DEC_SEQ):
                    at = slice(SEQ + k, T, DEC_SEQ)
                    prev = r_mp[:, NCH:2 * NCH] if k == 0 else r_m[:, SEQ + k - 1:T:DEC_SEQ]
                    tt(f"t{k}", r_t8[:, :], r_in[:, 1, at], prev, ALU.add)
                    tt(f"m{k}", r_m[:, at], r_t8[:, :], r_in[:, 0, at], ALU.max)
                eng.memset(r_mp[:, 0:1], 0.0).then_inc(*rw_dve.step("mp0"))
                ts("mp1", r_mp[:, 1:NCH], r_m[:, CH - 1:SEQ - CH:CH], 0.0, None, ALU.add)
                ts("mp2", r_mo[:, 0:1], r_m[:, SEQ - 1:SEQ], 0.0, None, ALU.add)
                slot()
                tt("u", r_row[:, ROW_U, :], r_a[:, 0, :], r_m[:, :], ALU.subtract)
                tt("w", r_tok[:, TOK_W, :], r_in[:, 0, :], r_a[:, 0, :], ALU.subtract)
                prev = (r_mp[:, 0:NCH].unsqueeze(2).to_broadcast([H, NCH, CH]),
                        r_mp[:, NCH:2 * NCH].unsqueeze(2).to_broadcast([H, DEC_BATCH, DEC_SEQ]))
                for k, (o, u, m_) in enumerate(zip(cut(r_row[:, ROW_ELW, :]), cut(r_row[:, ROW_U, :]), prev)):
                    tt(f"lw{k + 1}", o, u, m_, ALU.add)
                ts("em", r_row[:, ROW_EM, :], r_m[:, :], -1.0, None, ALU.mult)
                for k, (o, w, u) in enumerate(zip(cut(r_tok[:, TOK_EWS, :]), cut(r_tok[:, TOK_W, :]), cut(r_row[:, ROW_U, :]))):
                    n = (CH, DEC_SEQ)[k]
                    tt(f"ew{k + 1}", o, w, u[:, :, n - 1:n].to_broadcast([H, 8, n]), ALU.add)
                ts("ng", r_tok[:, TOK_NG, :], r_row[:, ROW_G, :], -1.0, None, ALU.mult)
                for k, (o, gg) in enumerate(zip(cut(r_tok[:, TOK_KD, :]), cut(r_row[:, ROW_G, :]))):
                    n = (CH, DEC_SEQ)[k]
                    tt(f"kd{k + 1}", o, gg[:, :, n - 1:n].to_broadcast([H, 8, n]), gg, ALU.subtract)
                slot()
                eng.wait_ge(*rw_act.after("eg"))
                tt("beg", r_row[:, ROW_BEG, :], r_row[:, ROW_BETA, :], r_row[:, ROW_EG, :], ALU.mult)
                ts("mo1", r_mo[:, 1:1 + DEC_BATCH], r_m[:, SEQ + DEC_SEQ - 1:T:DEC_SEQ], 0.0, None, ALU.add)
                ts("mo2", r_tok[:, TOK_BETA, :], r_row[:, ROW_BETA, :], 0.0, None, ALU.add)
                slot()
                slot()
            if kind == "act":
                eng.wait_ge(*rw_dve.after("bc"))
                eng.activation(r_b[:, :, :], r_a[:, 0:2, :], ACT.Exp, scale=-1.0).then_inc(*rw_act.step("e"))
                eng.wait_ge(*rw_act.after("e"))
                eng.activation(r_a[:, 0:2, :], r_b[:, :, :], ACT.Ln, bias=1.0).then_inc(*rw_act.step("l"))
                eng.activation(r_par[:, 4:5], r_par[:, 2:3], ACT.Exp).then_inc(*rw_act.step("ea"))
                eng.activation(r_a[:, 2, :], r_a[:, 2, :], ACT.Exp, scale=-1.0).then_inc(*rw_act.step("be"))
                eng.wait_ge(*rw_act.after("be"))
                eng.activation(r_a[:, 2, :], r_a[:, 2, :], ACT.Ln, bias=1.0).then_inc(*rw_act.step("bl"))
                eng.wait_ge(*rw_act.after("bl"))
                eng.activation(r_row[:, ROW_BETA, :], r_a[:, 2, :], ACT.Exp, scale=-1.0).then_inc(*rw_act.step("bs"))
                slot()
                slot()
                slot()
                eng.wait_ge(*rw_dve.after("em"))
                eng.activation(r_row[:, ROW_EM, :], r_row[:, ROW_EM, :], ACT.Exp).then_inc(*rw_act.step("em"))
                eng.activation(r_row[:, ROW_ELW, :], r_row[:, ROW_ELW, :], ACT.Exp).then_inc(*rw_act.step("elw"))
                eng.wait_ge(*rw_dve.after("kd2"))
                eng.activation(r_tok[:, TOK_EWS, :], r_tok[:, TOK_EWS, :], ACT.Exp).then_inc(*rw_act.step("ews"))
                eng.activation(r_tok[:, TOK_KD, :], r_tok[:, TOK_KD, :], ACT.Exp).then_inc(*rw_act.step("kd"))
                eng.activation(r_row[:, ROW_EG, :], r_row[:, ROW_G, :], ACT.Exp).then_inc(*rw_act.step("eg"))
                slot()
                eng.wait_ge(*rw_dve.after("mo2"))
                eng.wait_ge(*rw_act.after("eg"))
                eng.dma_start(rowd.rearrange("q h t -> h q t"), r_row[:, :, :]).then_inc(rw_out, 16)
                eng.dma_start(p_m, r_mo[:, 0:1]).then_inc(rw_mo, 16)
                eng.dma_start(s_m, r_mo[:, 1:1 + DEC_BATCH]).then_inc(rw_mo, 16)
                slot()
                eng.wait_ge(*rw_pe.after("tok"))
                eng.activation(tok[:, :, 0:NCH, :].rearrange("p q c h -> p q (c h)"),
                               M[0][:, 0:5 * NCH * H].rearrange("p (q c) -> p q c", q=5), ACT.Copy).then_inc(*rw_act.step("tok"))
                eng.activation(tok[0:NS, :, NCH, :], M[1][0:NS, 0:5 * H].rearrange("p (q h) -> p q h", q=5),
                               ACT.Copy).then_inc(*rw_act.step("toks"))
                slot()
            if kind == "pool":
                for _ in range(6):
                    slot()
            if kind == "pe":
                for _ in range(5):
                    slot()
                eng.wait_ge(*rw_dve.after("mo2"))
                eng.wait_ge(*rw_act.after("eg"))
                for q in range(5):
                    for c in range(NCH):
                        i = eng.transpose(M[0][:, (q * NCH + c) * H:(q * NCH + c + 1) * H], r_tok[:, q, c * CH:(c + 1) * CH], ident[0:H, 0:H])
                    i = eng.transpose(M[1][0:NS, q * H:(q + 1) * H], r_tok[:, q, SEQ:T], ident[0:H, 0:H])
                i.then_inc(*rw_pe.step("tok"))
                slot()

        def stored_rows(eng):
            eng.wait_ge(stage_stored[0], 16)

        gd_in, gd_rows, gd_out = sem("gd_in"), sem("gd_rows"), sem("gd_out")
        gx_in, gx_st = sem("gx_in"), sem("gx_st")
        inv0 = sem("inv0")
        d_vx = d_mt[:, 0:DEC_BATCH * HD]
        gd_pe = steps("gd_pe", "nq kkqk vk ks tr " + " ".join(f"x{j} y{j}" for j in range(1, 7)) + " vn o su ss", credit=1)
        gd_act = steps("gd_act", "e l s sq lq lk rq rk de0 de1 de2 de3 tr " + " ".join(f"x{j}" for j in range(1, 7)) + " vn sq2 rl rr", credit=1)
        gd_dve = steps("gd_dve", "tc c0 c2 a1 a2 cl cs qn kn ga qkd lt lb m0 vb kd r " + " ".join(f"tt{j} tm{j}" for j in range(1, 6))
                       + " tt6 s1 s2 y1 y2", credit=1)
        gd_pool = steps("gd_pool", "c1 c3 a zw kb qg " + " ".join(f"mt{j}" for j in range(1, 7)), credit=1)
        gx_pe = steps("gx_pe", "nq kkqk vk ks kst tr x1 y1 vn o ss " + " ".join(f"su{h}" for h in range(H)))
        gx_act = steps("gx_act", "e l s sq lq lk rq rk de0 de1 de2 de3 kst tr x1 vn sq2 rl rr")
        gx_dve = steps("gx_dve", "sx1 sx2 sx3 tc c0 c2 a1 a2 cl cs qn kn ga qkd lt lb m0 vb kd r tt1 y1 y2 "
                       + " ".join(f"vx{h} s1{h} s2{h}a s2{h}b" for h in range(H)))
        gx_pool = steps("gx_pool", "c1 c3 a zw kb qg mt1")

        def gdn(kind, eng, n, slot, sample):
            N = NS if sample else CH
            C4 = H * N
            J = 2 if sample else 7
            pe_, act_, dve_, pool_ = (gx_pe, gx_act, gx_dve, gx_pool) if sample else (gd_pe, gd_act, gd_dve, gd_pool)
            col0 = SEQ if sample else None if n is None else n * CH
            C12, C16 = 12 * N, 16 * N

            def hn(x, o=0):
                return x[:, o:o + C4].rearrange("p (h n) -> p h n", n=N)

            def sq(x, h=None, o=0):
                v = x[0:N, o:o + C4].rearrange("p (h n) -> p h n", n=N)
                return v if h is None else v[:, h, :]

            def tk(x, h=None):
                v = x[0:N, :].rearrange("p (h n) -> p h n", n=HD)
                return v if h is None else v[:, h, :]

            def tap(j):
                if sample:
                    return d_sx[:, :, :, j:j + DEC_SEQ]
                return d_ch[:, :].rearrange("p (t c) -> p t c", c=CH + HALO)[:, :, j:j + CH]

            def conv(x):
                if sample:
                    return x[:, 0:C12].rearrange("p (t b c) -> p t b c", b=DEC_BATCH, c=DEC_SEQ)
                return x[:, 0:C12].rearrange("p (t c) -> p t c", c=CH)

            def weight(j):
                w = prm[:, PC_CONV + 12 * j:PC_CONV + 12 * (j + 1)].unsqueeze(2)
                return w.unsqueeze(3).to_broadcast([P, 12, DEC_BATCH, DEC_SEQ]) if sample else w.to_broadcast([P, 12, CH])

            if kind == "sp":
                sm = gx_in if sample else gd_in
                if sample:
                    for s in (gd_pe, gd_act, gd_dve, gd_pool):
                        eng.wait_ge(*s.all_of(NCH))
                    eng.wait_ge(gd_out, 16 * (NCH + 1))
                    eng.dma_start(d_ch[:, 0:C12].rearrange("p (t c) -> p t c", c=N), pcols(GD_TILE, 12, col0 + HALO, N)).then_inc(sm, 16)
                    eng.dma_start(d_ch[:, C12:C12 + 12 * DEC_BATCH * HALO], conv0).then_inc(sm, 16)
                else:
                    n, col0 = next_chunk(n)
                    prefetch(eng, n, (dve_, "c2"))
                    prefetch(eng, n, (pool_, "c3"))
                    eng.dma_start(d_ch[:, :].rearrange("p (t c) -> p t c", c=CH + HALO), pcols(GD_TILE, 12, col0, CH + HALO)).then_inc(sm, 16)
                    prefetch(eng, n, (pool_, "zw"))
                eng.dma_start(d_cv[:, C12:C16].rearrange("p (t c) -> p t c", c=N), pcols(GD_TILE + 12, 4, lin(HALO, 1, col0), N)).then_inc(sm, 16)
                if not sample:
                    prefetch(eng, n, (dve_, "s1"))
                for k, q in enumerate((ROW_G, ROW_BETA, ROW_EG, ROW_BEG)):
                    eng.dma_start(hn(d_bc, k * C4), rowd[q:q + 1][:, :, bass.ds(col0, N)].rearrange("a h t -> (a h) t").unsqueeze(0).to_broadcast([P, H, N])).then_inc(sm if sample else gd_rows, 16)
                return
            loaded = (gx_in, 16 * 7) if sample else None if n is None else (gd_in, lin(32, 32, n))
            if not sample:
                after_chunks(eng, n, [x for k, x in (("pe", pe_), ("act", act_), ("dve", dve_), ("pool", pool_)) if k != kind], gd_out)
            GBC, BBC, EGB, BEGB = (hn(d_bc, k * C4) for k in range(4))
            if kind == "dve":
                eng.wait_ge(*loaded)
                if sample:
                    eng.tensor_copy(d_sx[:, :, :, HALO:], d_ch[:, 0:C12].rearrange("p (t b c) -> p t b c", b=DEC_BATCH, c=DEC_SEQ)).then_inc(*dve_.step("sx1"))
                    eng.tensor_copy(d_sx[:, :, :, 0:HALO], d_ch[:, C12:C12 + 12 * DEC_BATCH * HALO].rearrange("p (t b c) -> p t b c", b=DEC_BATCH, c=HALO)).then_inc(*dve_.step("sx2"))
                    eng.wait_ge(*dve_.after("sx2"))
                    eng.tensor_copy(d_ch[:, C12:C12 + 12 * DEC_BATCH * HALO].rearrange("p (t b c) -> p t b c", b=DEC_BATCH, c=HALO),
                                    d_sx[:, :, :, DEC_SEQ:]).then_inc(*dve_.step("sx3"))
                tok_at = tok[:, :, NCH, :] if sample else tok[:, :, bass.ds(n, 1), :].squeeze(2)
                eng.tensor_scalar(tokc[0:N, :, :], tok_at[0:N], 0.0, None, ALU.add).then_inc(*dve_.step("tc"))
                eng.tensor_tensor(conv(d_cv), tap(0), weight(0), ALU.mult).then_inc(*dve_.step("c0"))
                eng.tensor_tensor(conv(d_pb), tap(2), weight(2), ALU.mult).then_inc(*dve_.step("c2"))
                eng.wait_ge(*dve_.after("c2", n))
                eng.tensor_tensor(d_cv[:, 0:C12], d_cv[:, 0:C12], d_pb[:, 0:C12], ALU.add).then_inc(*dve_.step("a1"))
                eng.wait_ge(*dve_.after("a1", n))
                eng.wait_ge(*pool_.after("a", n))
                eng.tensor_tensor(d_cv[:, 0:C12], d_cv[:, 0:C12], d_pa[:, 0:C12], ALU.add).then_inc(*dve_.step("a2"))
                eng.wait_ge(*dve_.after("a2", n))
                eng.tensor_scalar(d_pa[:, 0:C16], d_cv[:, 0:C16], CLAMP, None, ALU.max).then_inc(*dve_.step("cl"))
                slot()
                eng.wait_ge(*act_.after("s", n))
                eng.tensor_tensor(d_cv[:, 0:C16], d_cv[:, 0:C16], d_pa[:, 0:C16], ALU.mult).then_inc(*dve_.step("cs"))
                slot()
                eng.wait_ge(*act_.after("rk", n))
                eng.tensor_tensor(d_qk[:, 0:C4], d_cv[:, 0:C4], d_pb[:, 0:C4], ALU.mult).then_inc(*dve_.step("qn"))
                eng.tensor_tensor(d_qk[:, C4:2 * C4], d_cv[:, C4:2 * C4], d_pb[:, C4:2 * C4], ALU.mult).then_inc(*dve_.step("kn"))
                neg = cst[0:N, CC_NEGS:CC_NEGS + N] if sample else cst[:, CC_NEGP:CC_NEGP + N]
                if not sample:
                    eng.wait_ge(gd_rows, lin(64, 64, n))
                eng.tensor_tensor(sq(d_de), GBC[0:N], neg.unsqueeze(1).to_broadcast([N, H, N]), ALU.add).then_inc(*dve_.step("ga"))
                slot()
                eng.wait_ge(*act_.after("de3", n))
                eng.wait_ge(*pe_.after("kkqk", n))
                eng.tensor_tensor(sq(d_at), sq(M[3]), sq(d_de), ALU.mult).then_inc(*dve_.step("qkd"))
                eng.tensor_tensor(sq(d_lt), sq(M[2]), sq(d_de), ALU.mult).then_inc(*dve_.step("lt"))
                eng.wait_ge(*dve_.after("lt", n))
                eng.tensor_tensor(sq(d_lt), sq(d_lt), BBC[0:N], ALU.mult).then_inc(*dve_.step("lb"))
                eng.wait_ge(*dve_.after("lb", n))
                eng.tensor_tensor(sq(d_tt), sq(d_lt), cst[0:N, CC_LEV:CC_LEV + N].unsqueeze(1).to_broadcast([N, H, N]), ALU.mult).then_inc(*dve_.step("m0"))
                eng.wait_ge(*dve_.after("m0", n))
                eng.tensor_tensor(sq(d_tt), cst[0:N, CC_ID:CC_ID + N].unsqueeze(1).to_broadcast([N, H, N]), sq(d_tt),
                                  ALU.subtract).then_inc(inv0, 1)
                eng.wait_ge(*pe_.after("vk", n))
                eng.tensor_tensor(tk(d_vb), tk(M[4]), tokc[0:N, TOK_BETA, :].unsqueeze(2).to_broadcast([N, H, HD]), ALU.mult).then_inc(*dve_.step("vb"))
                eng.tensor_tensor(tk(d_kd), tk(M[5]), tokc[0:N, TOK_KD, :].unsqueeze(2).to_broadcast([N, H, HD]), ALU.mult).then_inc(*dve_.step("kd"))
                slot()
                slot()
                eng.wait_ge(*pe_.after("kst" if sample else "ks", n))
                eng.wait_ge(*dve_.after("vb", n))
                eng.tensor_tensor(tk(d_r), tk(d_vb), tk(M[4]), ALU.subtract).then_inc(*dve_.step("r"))
                for j in range(1, J):
                    slot()
                    eng.wait_ge(*pe_.after(f"y{j}", n))
                    eng.tensor_tensor(sq(d_tt), sq(d_tt), sq(M[2]), ALU.subtract).then_inc(*dve_.step(f"tt{j}"))
                    if j < J - 1:
                        eng.tensor_tensor(sq(d_t), sq(d_t), sq(M[3]), ALU.subtract).then_inc(*dve_.step(f"tm{j}"))
                    slot()
                slot()
                if not sample:
                    eng.wait_ge(*pe_.after("o", n))
                    eng.tensor_tensor(hn(d_S), hn(d_S), EGB[:, :, N - 1:N].to_broadcast([P, H, HD]), ALU.mult).then_inc(*dve_.step("s1"))
                    eng.wait_ge(*dve_.after("s1", n))
                    eng.wait_ge(*pe_.after("su", n))
                    eng.tensor_tensor(d_S[:, :], d_S[:, :], M[4][:, :], ALU.add).then_inc(*dve_.step("s2"))
                slot()
                eng.wait_ge(*act_.after("rr", n))
                eng.tensor_tensor(d_xs[:, 0:C4], M[5][:, 0:C4], d_pa[:, 0:C4], ALU.mult).then_inc(*dve_.step("y1"))
                eng.wait_ge(*dve_.after("y1", n))
                eng.tensor_tensor(d_xs[:, 0:C4], d_xs[:, 0:C4], d_pb[:, 2 * C4:3 * C4], ALU.mult).then_inc(*dve_.step("y2"))
                slot()
                if sample:
                    for h in range(H):
                        if h:
                            eng.wait_ge(*pe_.after(f"su{h - 1}"))
                        eng.tensor_tensor(d_vx[0:NS, :].rearrange("p (b v) -> p b v", v=HD),
                                          tk(d_vn, h).unsqueeze(1).to_broadcast([NS, DEC_BATCH, HD]),
                                          cst[0:NS, CC_IND:CC_IND + DEC_BATCH].unsqueeze(2).to_broadcast([NS, DEC_BATCH, HD]),
                                          ALU.mult).then_inc(*dve_.step(f"vx{h}"))
                        last = EGB[:, h, DEC_SEQ - 1::DEC_SEQ].unsqueeze(2).to_broadcast([P, DEC_BATCH, HD])
                        eng.tensor_tensor(d_Ss[:, :, h, :], d_Ss[:, :, h, :], last, ALU.mult).then_inc(*dve_.step(f"s1{h}"))
                        eng.wait_ge(*dve_.after(f"s1{h}"))
                        eng.wait_ge(*pe_.after(f"su{h}"))
                        for q, x in enumerate("ab"):
                            eng.tensor_tensor(d_Ss[:, 4 * q:4 * q + 4, h, :], d_Ss[:, 4 * q:4 * q + 4, h, :],
                                              M[q][:, :].rearrange("p (b v) -> p b v", v=HD), ALU.add).then_inc(*dve_.step(f"s2{h}{x}"))
                slot()
            if kind == "pool":
                eng.wait_ge(*loaded)
                if sample:
                    eng.wait_ge(*dve_.after("sx2"))
                eng.tensor_tensor(conv(d_pa), tap(1), weight(1), ALU.mult).then_inc(*pool_.step("c1"))
                eng.tensor_tensor(conv(d_mt), tap(3), weight(3), ALU.mult).then_inc(*pool_.step("c3"))
                eng.wait_ge(*pool_.after("c3", n))
                eng.tensor_tensor(d_pa[:, 0:C12], d_pa[:, 0:C12], d_mt[:, 0:C12], ALU.add).then_inc(*pool_.step("a"))
                slot()
                slot()
                eng.wait_ge(*dve_.after("ga", n))
                eng.tensor_tensor(d_pb[:, 2 * C4:3 * C4], d_cv[:, 3 * C4:4 * C4], prm[:, PC_GDN:PC_GDN + 1].to_broadcast([P, C4]),
                                  ALU.mult).then_inc(*pool_.step("zw"))
                eng.tensor_tensor(hn(d_pb, 0), hn(d_qk, C4), BEGB, ALU.mult).then_inc(*pool_.step("kb"))
                eng.tensor_tensor(hn(d_pb, C4), hn(d_qk, 0), EGB, ALU.mult).then_inc(*pool_.step("qg"))
                slot()
                eng.wait_ge(*dve_.after("lb", n))
                for j in range(1, J):
                    eng.tensor_tensor(sq(d_mt, None, j * N4), sq(d_lt), cst[0:N, CC_LEV + j * P:CC_LEV + j * P + N].unsqueeze(1).to_broadcast([N, H, N]),
                                      ALU.mult).then_inc(*pool_.step(f"mt{j}"))
                slot()
                for _ in range(2 * (J - 1) + 5):
                    slot()
            if kind == "act":
                eng.wait_ge(*dve_.after("cl", n))
                eng.activation(d_pa[:, 0:C16], d_pa[:, 0:C16], ACT.Exp, scale=-1.0).then_inc(*act_.step("e"))
                eng.wait_ge(*act_.after("e", n))
                eng.activation(d_pa[:, 0:C16], d_pa[:, 0:C16], ACT.Ln, bias=1.0).then_inc(*act_.step("l"))
                eng.wait_ge(*act_.after("l", n))
                eng.activation(d_pa[:, 0:C16], d_pa[:, 0:C16], ACT.Exp, scale=-1.0).then_inc(*act_.step("s"))
                slot()
                eng.wait_ge(*dve_.after("cs", n))
                eng.activation(d_pb[:, 0:2 * C4], d_cv[:, 0:2 * C4], ACT.Square).then_inc(*act_.step("sq"))
                slot()
                eng.wait_ge(*pe_.after("nq", n))
                eng.activation(d_pb[:, 0:C4], M[0][:, 0:C4], ACT.Ln, bias=EPS).then_inc(*act_.step("lq"))
                eng.activation(d_pb[:, C4:2 * C4], M[1][:, 0:C4], ACT.Ln, bias=EPS).then_inc(*act_.step("lk"))
                eng.wait_ge(*act_.after("lq", n))
                eng.activation(d_pb[:, 0:C4], d_pb[:, 0:C4], ACT.Exp, scale=-0.5, bias=-0.5 * math.log(HD)).then_inc(*act_.step("rq"))
                eng.wait_ge(*act_.after("lk", n))
                eng.activation(d_pb[:, C4:2 * C4], d_pb[:, C4:2 * C4], ACT.Exp, scale=-0.5).then_inc(*act_.step("rk"))
                eng.wait_ge(*dve_.after("ga", n))
                for h in range(H):
                    eng.activation(sq(d_de, h), sq(d_de, h), ACT.Exp, bias=tokc[0:N, TOK_NG, h:h + 1]).then_inc(*act_.step(f"de{h}"))
                slot()
                if sample:
                    eng.wait_ge(*pe_.after("ks"))
                    eng.activation(d_pa[:, 0:C4], M[0][:, 0:C4], ACT.Copy).then_inc(*act_.step("kst"))
                slot()
                eng.wait_ge(*pe_.after("tr", n))
                eng.activation(sq(d_t), sq(M[0]), ACT.Copy).then_inc(*act_.step("tr"))
                slot()
                for j in range(1, J):
                    eng.wait_ge(*pe_.after(f"x{j}", n))
                    eng.activation(sq(d_xs), sq(M[1]), ACT.Copy).then_inc(*act_.step(f"x{j}"))
                    slot()
                    slot()
                eng.wait_ge(*pe_.after("vn", n))
                eng.activation(d_vn[0:N, :], M[1][0:N, :], ACT.Copy).then_inc(*act_.step("vn"))
                slot()
                eng.wait_ge(*pe_.after("o", n))
                eng.activation(d_pa[:, 0:C4], M[5][:, 0:C4], ACT.Square).then_inc(*act_.step("sq2"))
                eng.wait_ge(*pe_.after("ss", n))
                eng.activation(d_pa[:, 0:C4], M[0][:, 0:C4], ACT.Ln, bias=EPS, scale=1.0 / HD).then_inc(*act_.step("rl"))
                eng.wait_ge(*act_.after("rl", n))
                eng.activation(d_pa[:, 0:C4], d_pa[:, 0:C4], ACT.Exp, scale=-0.5).then_inc(*act_.step("rr"))
                slot()
                eng.wait_ge(*dve_.after("y2", n))
                eng.dma_start(ycols(GD, col0, N), hn(d_xs)).then_inc(gx_st if sample else gd_out, 16)
                slot()
                slot()
            if kind == "pe":
                slot()
                eng.wait_ge(*act_.after("sq", n))
                for q in range(2):
                    i = eng.matmul(M[q][:, 0:C4], ones, d_pb[:, q * C4:(q + 1) * C4], start=True, stop=True)
                i.then_inc(*pe_.step("nq"))
                slot()
                eng.wait_ge(*dve_.after("kn", n))
                for h in range(H):
                    for q in range(2):
                        i = eng.matmul(M[2 + q][0:N, h * N:(h + 1) * N], hn(d_qk, C4)[:, h, :], hn(d_qk, (1 - q) * C4)[:, h, :], start=True, stop=True)
                i.then_inc(*pe_.step("kkqk"))
                for h in range(H):
                    eng.transpose(M[4][0:N, h * HD:(h + 1) * HD], hn(d_cv, 2 * C4)[:, h, :], ident)
                    i = eng.transpose(M[5][0:N, h * HD:(h + 1) * HD], hn(d_qk, C4)[:, h, :], ident)
                i.then_inc(*pe_.step("vk"))
                slot()
                eng.wait_ge(*pool_.after("kb", n))
                if sample:
                    for h in range(H):
                        for b in range(DEC_BATCH):
                            c = h * N + b * DEC_SEQ
                            i = eng.matmul(M[0][:, c:c + DEC_SEQ], d_Ss[:, b, h, :], d_pb[:, c:c + DEC_SEQ], start=True, stop=True)
                    i.then_inc(*pe_.step("ks"))
                    eng.wait_ge(*act_.after("kst"))
                    eng.wait_ge(*dve_.after("vb"))
                    for h in range(H):
                        i = eng.transpose(M[4][0:N, h * HD:(h + 1) * HD], d_pa[:, h * N:(h + 1) * N], ident)
                    i.then_inc(*pe_.step("kst"))
                else:
                    eng.wait_ge(*dve_.after("vb", n))
                    for h in range(H):
                        i = eng.matmul(M[4][0:N, h * HD:(h + 1) * HD], d_pb[:, h * N:(h + 1) * N], d_S[:, h * HD:(h + 1) * HD], start=True, stop=True)
                    i.then_inc(*pe_.step("ks"))
                slot()
                eng.wait_ge(inv0, NCH + 1 if sample else lin(1, 1, n))
                for h in range(H):
                    i = eng.transpose(sq(M[0], h), sq(d_tt, h), ident[0:N, 0:N])
                i.then_inc(*pe_.step("tr"))
                slot()
                for j in range(1, J):
                    eng.wait_ge(*pool_.after(f"mt{j}", n))
                    if j == 1:
                        eng.wait_ge(*act_.after("tr", n))
                    else:
                        eng.wait_ge(*dve_.after(f"tm{j - 1}", n))
                    for h in range(H):
                        i = eng.matmul(sq(M[1], h), sq(d_mt, h, j * N4), sq(d_t, h), start=True, stop=True)
                    i.then_inc(*pe_.step(f"x{j}"))
                    slot()
                    eng.wait_ge(*act_.after(f"x{j}", n))
                    for h in range(H):
                        i = eng.matmul(sq(M[2], h), sq(d_xs, h), sq(d_tt, h), start=True, stop=True)
                    if j < J - 1:
                        for h in range(H):
                            i = eng.matmul(sq(M[3], h), sq(d_tt, h), sq(d_xs, h), start=True, stop=True)
                    i.then_inc(*pe_.step(f"y{j}"))
                    slot()
                eng.wait_ge(*dve_.after(f"tt{J - 1}", n))
                eng.wait_ge(*dve_.after("r", n))
                for h in range(H):
                    i = eng.matmul(M[1][0:N, h * HD:(h + 1) * HD], sq(d_tt, h), tk(d_r, h), start=True, stop=True)
                i.then_inc(*pe_.step("vn"))
                slot()
                eng.wait_ge(*act_.after("vn", n))
                eng.wait_ge(*pool_.after("qg", n))
                for h in range(H):
                    i = eng.matmul(M[5][:, h * N:(h + 1) * N], tk(d_vn, h), sq(d_at, h), start=(not sample or h == 0), stop=False, skip_group_check=sample)
                    if sample:
                        for b in range(DEC_BATCH):
                            c = h * N + b * DEC_SEQ
                            i = eng.matmul(M[5][:, c:c + DEC_SEQ], d_Ss[:, b, h, :], d_pb[:, C4 + c:C4 + c + DEC_SEQ],
                                           start=False, stop=(h == H - 1 and b == DEC_BATCH - 1), skip_group_check=True)
                    else:
                        i = eng.matmul(M[5][:, h * N:(h + 1) * N], d_S[:, h * HD:(h + 1) * HD], d_pb[:, C4 + h * N:C4 + (h + 1) * N],
                                       start=False, stop=True)
                i.then_inc(*pe_.step("o"))
                if not sample:
                    for h in range(H):
                        i = eng.matmul(M[4][:, h * HD:(h + 1) * HD], tk(d_kd, h), tk(d_vn, h), start=True, stop=True)
                    i.then_inc(*pe_.step("su"))
                eng.wait_ge(*act_.after("sq2", n))
                i = eng.matmul(M[0][:, 0:C4], ones, d_pa[:, 0:C4], start=True, stop=True)
                i.then_inc(*pe_.step("ss"))
                slot()
                if sample:
                    for h in range(H):
                        eng.wait_ge(*dve_.after(f"vx{h}"))
                        if h:
                            eng.wait_ge(*dve_.after(f"s2{h - 1}b"))
                        eng.wait_ge(*act_.after("rl"))
                        for q in range(2):
                            i = eng.matmul(M[q][:, :], tk(d_kd, h), d_vx[0:NS, q * 512:(q + 1) * 512], start=True, stop=True)
                        i.then_inc(*pe_.step(f"su{h}"))
                slot()
                slot()
        ml_in, ml_out = sem("ml_in"), sem("ml_out")
        mx_in, mx_st = sem("mx_in"), sem("mx_st")
        ml_pe = steps("ml_pe", "vt kq kt num den kv kn ss", credit=1)
        ml_act = steps("ml_act", "ks e0 e1 e2 e3 s1 s2 s3 vt sq rl rr", credit=1)
        ml_dve = steps("ml_dve", "tc ga cl qw pt kt dn dm rd h c1 c2 n1 n2 y1 y2", credit=1)
        ml_pool = steps("ml_pool", "gw", credit=1)
        mx_pe = steps("mx_pe", "vt kq kt num den kn ss " + " ".join(f"kv{h}" for h in range(H)))
        mx_act = steps("mx_act", "ks e0 e1 e2 e3 s1 s2 s3 vt sq rl rr")
        mx_dve = steps("mx_dve", "nb tc ga cl qw pt kt dn dm rd h y1 y2 n1 n2 " + " ".join(f"vx{h} s1{h} s2{h}a s2{h}b" for h in range(H)))
        mx_pool = steps("mx_pool", "gw")

        def mlstm(kind, eng, n, slot, sample):
            N = NS if sample else CH
            C4 = H * N
            pe_, act_, dve_, pool_ = (mx_pe, mx_act, mx_dve, mx_pool) if sample else (ml_pe, ml_act, ml_dve, ml_pool)
            col0 = SEQ if sample else None if n is None else n * CH

            def hn(x, o=0):
                return x[:, o:o + C4].rearrange("p (h n) -> p h n", n=N)

            def sq(x, h=None):
                v = x[0:N, 0:C4].rearrange("p (h n) -> p h n", n=N)
                return v if h is None else v[:, h, :]

            def tk(x, h=None):
                v = x[0:N, :].rearrange("p (h n) -> p h n", n=HD)
                return v if h is None else v[:, h, :]

            if kind == "sp":
                sm = mx_in if sample else ml_in
                if sample:
                    for s in (ml_pe, ml_act, ml_dve, ml_pool):
                        eng.wait_ge(*s.all_of(NCH))
                    eng.wait_ge(ml_out, 16 * (NCH + 1))
                else:
                    n, col0 = next_chunk(n)
                    prefetch(eng, n, (dve_, "qw"))
                    prefetch(eng, n, (pe_, "kq"))
                for k in range(4):
                    eng.dma_start(hn(m_in, k * C4), pcols(ML_TILE + 4 * k, 4, lin(HALO, 1, col0), N)).then_inc(sm, 16)
                if not sample:
                    prefetch(eng, n, (dve_, "n1"))
                for k, q in enumerate((ROW_U, ROW_ELW, ROW_EM)):
                    eng.dma_start(hn(m_bc, k * C4), rowd[q:q + 1][:, :, bass.ds(col0, N)].rearrange("a h t -> (a h) t").unsqueeze(0).to_broadcast([P, H, N])).then_inc(sm, 16)
                return
            loaded = (mx_in, 112) if sample else None if n is None else (ml_in, lin(112, 112, n))
            if not sample:
                after_chunks(eng, n, [x for k, x in (("pe", pe_), ("act", act_), ("dve", dve_), ("pool", pool_)) if k != kind], ml_out)
            UB, ELW, EM = (hn(m_bc, k * C4) for k in range(3))
            if kind == "dve":
                eng.wait_ge(*loaded)
                if sample:
                    eng.wait_ge(*ml_dve.all_of(NCH))
                    eng.tensor_copy(m_no[:, :], m_N[:, ::HD]).then_inc(n_out, 1)
                    eng.wait_ge(mxs_ld, 32)
                    eng.tensor_copy(m_Nb[:, :, :, :].rearrange("p b h v -> p (b h) v"),
                                    m_Ns[:, :, :].rearrange("p b h -> p (b h)").unsqueeze(2).to_broadcast([P, DEC_BATCH * H, HD])).then_inc(*dve_.step("nb"))
                tok_at = tok[:, :, NCH, :] if sample else tok[:, :, bass.ds(n, 1), :].squeeze(2)
                eng.tensor_scalar(tokc[0:N, :, :], tok_at[0:N], 0.0, None, ALU.add).then_inc(*dve_.step("tc"))
                neg = cst[0:N, CC_NEGS:CC_NEGS + N] if sample else cst[:, CC_NEGP:CC_NEGP + N]
                eng.tensor_tensor(sq(m_e), UB[0:N], neg.unsqueeze(1).to_broadcast([N, H, N]), ALU.add).then_inc(*dve_.step("ga"))
                eng.tensor_scalar(m_so[:, 0:C4], m_in[:, 3 * C4:4 * C4], CLAMP, None, ALU.max).then_inc(*dve_.step("cl"))
                eng.tensor_tensor(m_qw[:, 0:C4], m_in[:, 0:C4], m_bc[:, C4:2 * C4], ALU.mult).then_inc(*dve_.step("qw"))
                slot()
                eng.wait_ge(*act_.after("e3", n))
                eng.wait_ge(*pe_.after("kq", n))
                eng.tensor_tensor(sq(m_pt), sq(M[0]), sq(m_e), ALU.mult).then_inc(*dve_.step("pt"))
                eng.wait_ge(*pe_.after("kt", n))
                eng.tensor_tensor(tk(m_kt), tk(M[4]), tokc[0:N, TOK_EWS, :].unsqueeze(2).to_broadcast([N, H, HD]), ALU.mult).then_inc(*dve_.step("kt"))
                slot()
                eng.wait_ge(*pe_.after("den", n))
                eng.tensor_tensor(m_dn[:, 0:C4], M[2][:, 0:C4], m_bc[:, 2 * C4:3 * C4], ALU.max).then_inc(*dve_.step("dn"))
                eng.wait_ge(*dve_.after("dn", n))
                eng.scalar_tensor_tensor(m_dn[:, 0:C4], M[2][:, 0:C4], -1.0, m_dn[:, 0:C4], ALU.mult, ALU.max).then_inc(*dve_.step("dm"))
                eng.wait_ge(*dve_.after("dm", n))
                eng.reciprocal(m_rd[:, 0:C4], m_dn[:, 0:C4]).then_inc(*dve_.step("rd"))
                eng.wait_ge(*dve_.after("rd", n))
                eng.tensor_tensor(m_h[:, 0:C4], M[1][:, 0:C4], m_rd[:, 0:C4], ALU.mult).then_inc(*dve_.step("h"))
                slot()
                if not sample:
                    last = ELW[:, :, N - 1:N].to_broadcast([P, H, HD])
                    for k, (st, ps, done) in enumerate(((m_C, M[3], "kv"), (m_N, M[0], "kn"))):
                        eng.tensor_tensor(hn(st), hn(st), last, ALU.mult).then_inc(*dve_.step("cn"[k] + "1"))
                        eng.wait_ge(*dve_.after("cn"[k] + "1", n))
                        eng.wait_ge(*pe_.after(done, n))
                        eng.tensor_tensor(st[:, :], st[:, :], ps[:, :], ALU.add).then_inc(*dve_.step("cn"[k] + "2"))
                slot()
                eng.wait_ge(*act_.after("rr", n))
                eng.tensor_tensor(m_y[:, 0:C4], m_h[:, 0:C4], m_sq[:, 0:C4], ALU.mult).then_inc(*dve_.step("y1"))
                eng.wait_ge(*dve_.after("y1", n))
                eng.wait_ge(*pool_.after("gw", n))
                eng.tensor_tensor(m_y[:, 0:C4], m_y[:, 0:C4], m_gw[:, 0:C4], ALU.mult).then_inc(*dve_.step("y2"))
                slot()
                if sample:
                    ends = m_bc[:, C4:2 * C4].rearrange("p (h b c) -> p b h c", b=DEC_BATCH, c=DEC_SEQ)[:, :, :, DEC_SEQ - 1]
                    eng.tensor_tensor(m_Ns[:, :, :], m_Ns[:, :, :], ends, ALU.mult).then_inc(*dve_.step("n1"))
                    eng.wait_ge(*dve_.after("n1"))
                    eng.tensor_tensor(m_Ns[:, :, :], m_Ns[:, :, :], M[0][:, 0:H * DEC_BATCH].rearrange("p (h b) -> p b h", b=DEC_BATCH),
                                      ALU.add).then_inc(*dve_.step("n2"))
                    for h in range(H):
                        if h:
                            eng.wait_ge(*pe_.after(f"kv{h - 1}"))
                        eng.tensor_tensor(m_vx[:, :].rearrange("p (b v) -> p b v", v=HD),
                                          tk(m_vt, h).unsqueeze(1).to_broadcast([NS, DEC_BATCH, HD]),
                                          cst[0:NS, CC_IND:CC_IND + DEC_BATCH].unsqueeze(2).to_broadcast([NS, DEC_BATCH, HD]),
                                          ALU.mult).then_inc(*dve_.step(f"vx{h}"))
                        last = ELW[:, h, DEC_SEQ - 1::DEC_SEQ].unsqueeze(2).to_broadcast([P, DEC_BATCH, HD])
                        eng.tensor_tensor(m_Cs[:, :, h, :], m_Cs[:, :, h, :], last, ALU.mult).then_inc(*dve_.step(f"s1{h}"))
                        eng.wait_ge(*dve_.after(f"s1{h}"))
                        eng.wait_ge(*pe_.after(f"kv{h}"))
                        for q, x in enumerate("ab"):
                            eng.tensor_tensor(m_Cs[:, 4 * q:4 * q + 4, h, :], m_Cs[:, 4 * q:4 * q + 4, h, :],
                                              M[2 + q][:, :].rearrange("p (b v) -> p b v", v=HD), ALU.add).then_inc(*dve_.step(f"s2{h}{x}"))
                slot()
            if kind == "pool":
                eng.wait_ge(*act_.after("s3", n))
                eng.tensor_tensor(hn(m_gw), hn(m_so), prm[:, PC_MLN:PC_MLN + H].unsqueeze(2).to_broadcast([P, H, N]), ALU.mult).then_inc(*pool_.step("gw"))
                for _ in range(6):
                    slot()
            if kind == "act":
                eng.wait_ge(*loaded)
                eng.activation(m_ks[:, 0:C4], m_in[:, C4:2 * C4], ACT.Copy, scale=HD ** -0.5).then_inc(*act_.step("ks"))
                eng.wait_ge(*dve_.after("ga", n))
                for h in range(H):
                    eng.activation(sq(m_e, h), sq(m_e, h), ACT.Exp, bias=tokc[0:N, TOK_W, h:h + 1]).then_inc(*act_.step(f"e{h}"))
                eng.wait_ge(*dve_.after("cl", n))
                eng.activation(m_so[:, 0:C4], m_so[:, 0:C4], ACT.Exp, scale=-1.0).then_inc(*act_.step("s1"))
                eng.wait_ge(*act_.after("s1", n))
                eng.activation(m_so[:, 0:C4], m_so[:, 0:C4], ACT.Ln, bias=1.0).then_inc(*act_.step("s2"))
                eng.wait_ge(*act_.after("s2", n))
                eng.activation(m_so[:, 0:C4], m_so[:, 0:C4], ACT.Exp, scale=-1.0).then_inc(*act_.step("s3"))
                slot()
                eng.wait_ge(*pe_.after("vt", n))
                eng.activation(m_vt[0:N, :], M[5][0:N, :], ACT.Copy).then_inc(*act_.step("vt"))
                slot()
                eng.wait_ge(*dve_.after("h", n))
                eng.activation(m_sq[:, 0:C4], m_h[:, 0:C4], ACT.Square).then_inc(*act_.step("sq"))
                slot()
                eng.wait_ge(*pe_.after("ss", n))
                eng.activation(m_sq[:, 0:C4], M[4][:, 0:C4], ACT.Ln, bias=EPS, scale=1.0 / HD).then_inc(*act_.step("rl"))
                eng.wait_ge(*act_.after("rl", n))
                eng.activation(m_sq[:, 0:C4], m_sq[:, 0:C4], ACT.Exp, scale=-0.5).then_inc(*act_.step("rr"))
                slot()
                eng.wait_ge(*dve_.after("y2", n))
                eng.dma_start(ycols(ML, col0, N), hn(m_y)).then_inc(mx_st if sample else ml_out, 16)
                slot()
                slot()
            if kind == "pe":
                eng.wait_ge(*loaded)
                for h in range(H):
                    i = eng.transpose(M[5][0:N, h * HD:(h + 1) * HD], hn(m_in, 2 * C4)[:, h, :], ident)
                i.then_inc(*pe_.step("vt"))
                slot()
                eng.wait_ge(*act_.after("ks", n))
                for h in range(H):
                    i = eng.matmul(sq(M[0], h), hn(m_ks)[:, h, :], hn(m_in)[:, h, :], start=True, stop=True)
                i.then_inc(*pe_.step("kq"))
                for h in range(H):
                    i = eng.transpose(M[4][0:N, h * HD:(h + 1) * HD], hn(m_ks)[:, h, :], ident)
                i.then_inc(*pe_.step("kt"))
                slot()
                eng.wait_ge(*dve_.after("kt", n))
                eng.wait_ge(*act_.after("vt", n))
                for h in range(H):
                    i = eng.matmul(M[1][:, h * N:(h + 1) * N], tk(m_vt, h), sq(m_pt, h), start=(not sample or h == 0), stop=False, skip_group_check=sample)
                    if sample:
                        for b in range(DEC_BATCH):
                            c = h * N + b * DEC_SEQ
                            i = eng.matmul(M[1][:, c:c + DEC_SEQ], m_Cs[:, b, h, :], m_qw[:, c:c + DEC_SEQ],
                                           start=False, stop=(h == H - 1 and b == DEC_BATCH - 1), skip_group_check=True)
                    else:
                        i = eng.matmul(M[1][:, h * N:(h + 1) * N], m_C[:, h * HD:(h + 1) * HD], m_qw[:, h * N:(h + 1) * N],
                                       start=False, stop=True)
                i.then_inc(*pe_.step("num"))
                for h in range(H):
                    i = eng.matmul(M[2][:, h * N:(h + 1) * N], cst[0:N, CC_ONE:CC_ONE + P], sq(m_pt, h), start=(not sample or h == 0), stop=False, skip_group_check=sample)
                    if sample:
                        for b in range(DEC_BATCH):
                            c = h * N + b * DEC_SEQ
                            i = eng.matmul(M[2][:, c:c + DEC_SEQ], m_Nb[:, b, h, :], m_qw[:, c:c + DEC_SEQ],
                                           start=False, stop=(h == H - 1 and b == DEC_BATCH - 1), skip_group_check=True)
                    else:
                        i = eng.matmul(M[2][:, h * N:(h + 1) * N], m_N[:, h * HD:(h + 1) * HD], m_qw[:, h * N:(h + 1) * N],
                                       start=False, stop=True)
                i.then_inc(*pe_.step("den"))
                if sample:
                    for h in range(H):
                        i = eng.matmul(M[0][:, h * DEC_BATCH:(h + 1) * DEC_BATCH], tk(m_kt, h), cst[0:NS, CC_IND:CC_IND + DEC_BATCH],
                                       start=True, stop=True)
                    i.then_inc(*pe_.step("kn"))
                else:
                    for h in range(H):
                        i = eng.matmul(M[3][:, h * HD:(h + 1) * HD], tk(m_kt, h), tk(m_vt, h), start=True, stop=True)
                    i.then_inc(*pe_.step("kv"))
                    for h in range(H):
                        i = eng.matmul(M[0][:, h * HD:(h + 1) * HD], tk(m_kt, h), ones, start=True, stop=True)
                    i.then_inc(*pe_.step("kn"))
                slot()
                eng.wait_ge(*act_.after("sq", n))
                i = eng.matmul(M[4][:, 0:C4], ones, m_sq[:, 0:C4], start=True, stop=True)
                i.then_inc(*pe_.step("ss"))
                slot()
                slot()
                if sample:
                    for h in range(H):
                        eng.wait_ge(*dve_.after(f"vx{h}"))
                        if h:
                            eng.wait_ge(*dve_.after(f"s2{h - 1}b"))
                        for q in range(2):
                            i = eng.matmul(M[2 + q][:, :], tk(m_kt, h), m_vx[:, q * 512:(q + 1) * 512], start=True, stop=True)
                        i.then_inc(*pe_.step(f"kv{h}"))
                slot()

        nm_act = {w: steps(f"nm{w}_act", " ".join(f"q{k}" for k in range(KT)) + " l r " + " ".join(f"h{k}" for k in range(KT))) for w in "12"}
        nm_dve = {w: steps(f"nm{w}_dve", " ".join(f"a{k}" for k in range(KT)) + " " + " ".join(f"s{k} l{k}" for k in range(KT))) for w in "12"}
        nm_pe = {w: steps(f"nm{w}_pe", "s") for w in "123"}
        fn_act = steps("fn_act", " ".join(f"q{k}" for k in range(KT)) + " l r")
        fn_dve = steps("fn_dve", " ".join(f"a{k}" for k in range(KT)) + " " + " ".join(f"s{k}" for k in range(KT)))

        def norm(kind, eng, which, x, sqs, total, rs, tmp, col, ready):
            act_, dve_, pe_ = (nm_act.get(which), nm_dve.get(which), nm_pe[which]) if which != "3" else (fn_act, fn_dve, nm_pe["3"])
            if kind == "act":
                ready(eng)
                for k in range(KT):
                    if k >= 2:
                        eng.wait_ge(*dve_.after(f"a{k - 2}"))
                    eng.activation(sqs[k % 2], x[:, k, :], ACT.Square).then_inc(*act_.step(f"q{k}"))
                eng.wait_ge(*pe_.after("s"))
                for g in range(TG):
                    i = eng.activation(rs[:, g * GN:(g + 1) * GN], M[g][:, 0:GN], ACT.Ln, bias=EPS, scale=1.0 / D_MODEL)
                i.then_inc(*act_.step("l"))
                eng.wait_ge(*act_.after("l"))
                eng.activation(rs, rs, ACT.Exp, scale=-0.5).then_inc(*act_.step("r"))
                if which != "3":
                    for k in range(KT):
                        eng.wait_ge(*dve_.after(f"s{k}"))
                        eng.activation(xn_hi[:, k, :], tmp[k % 2], ACT.Copy).then_inc(*act_.step(f"h{k}"))
            if kind == "dve":
                for k in range(KT):
                    eng.wait_ge(*act_.after(f"q{k}"))
                    if k == 0:
                        eng.tensor_copy(total, sqs[0]).then_inc(*dve_.step("a0"))
                    else:
                        eng.wait_ge(*dve_.after(f"a{k - 1}"))
                        eng.tensor_tensor(total, total, sqs[k % 2], ALU.add).then_inc(*dve_.step(f"a{k}"))
                eng.wait_ge(*act_.after("r"))

                def scaled(k):
                    out = x[:, k, :] if which == "3" else tmp[k % 2]
                    eng.scalar_tensor_tensor(out, x[:, k, :], prm[:, col + k:col + k + 1], rs, ALU.mult, ALU.mult).then_inc(*dve_.step(f"s{k}"))

                for k in range(KT):
                    if k >= 2 and which != "3":
                        eng.wait_ge(*dve_.after(f"l{k - 2}"))
                    scaled(k)
                    if which != "3":
                        eng.wait_ge(*act_.after(f"h{k}"))
                        eng.tensor_tensor(xn_lo[:, k, :], tmp[k % 2], xn_hi[:, k, :].bitcast(F32), ALU.subtract).then_inc(*dve_.step(f"l{k}"))
            if kind == "pe":
                eng.wait_ge(*dve_.after(f"a{KT - 1}"))
                for g in range(TG):
                    i = eng.matmul(M[g][:, 0:GN], ones, total[:, g * GN:(g + 1) * GN], start=True, stop=True)
                i.then_inc(*pe_.step("s"))

        MERGE0 = NPROJ
        OUT0 = MERGE0 + 24
        FFN0 = OUT0 + KT
        ORDER = [HG, GD, ML]
        Y_AT = {HG: (xn_hi[:, 4:8, :], xn_lo[:, 4:8, :]), GD: (xn_hi[:, 0:4, :], xn_lo[:, 0:4, :]), ML: (y_hi[:, :, :], y_lo[:, :, :])}
        y_ld = [sem(f"y_ld{s}") for s in range(2)]
        y_high, y_low = sem("y_high"), sem("y_low")
        gate_ld = [sem(f"gate_ld{s}") for s in range(2)]
        gate_sig, merged = sem("gate_sig"), sem("merged")
        mg_hi, mg_lo, resid_ld, added = sem("mg_hi"), sem("mg_lo"), sem("resid_ld"), sem("added")
        f_relu, f_sq, f_hi, f_lo, f_acc = sem("f_relu"), sem("f_sq"), sem("f_hi"), sem("f_lo"), sem("f_acc")
        y_st = sem("y_st")
        mxs_ld, hss_ld, gxs_ld = sem("mxs_ld"), sem("hss_ld"), sem("gxs_ld")
        st_out = sem("st_out")
        ybuf = (e_a, e_b)

        def split_y(kind, eng):
            for j in range(12):
                b, k = ORDER[j // 4], j % 4
                if kind == "sp":
                    if j == 0:
                        for s in (mx_pe, mx_act, mx_dve, mx_pool):
                            eng.wait_ge(*s.all_of(1))
                        for s_, v in ((hg_out, 16 * (NCH + 1)), (gd_out, 16 * (NCH + 1)), (ml_out, 16 * (NCH + 1)), (hs_st, 16), (gx_st, 16), (mx_st, 16)):
                            eng.wait_ge(s_, v)
                        eng.wait_ge(st_out, 16 * (2 + 3 + 5))
                    if j >= 2:
                        eng.wait_ge(y_low, j - 1)
                    eng.dma_start(ybuf[j % 2][:, :], yd[4 * b + k]).then_inc(y_ld[j % 2], 16)
                if kind == "act":
                    if j == 0:
                        eng.wait_ge(groups_done, TG * NPROJ)
                    eng.wait_ge(y_ld[j % 2], 16 * (j // 2 + 1))
                    eng.activation(Y_AT[b][0][:, k, :], ybuf[j % 2][:, :], ACT.Copy).then_inc(y_high, 1)
                if kind == "dve":
                    eng.wait_ge(y_high, j + 1)
                    eng.tensor_tensor(Y_AT[b][1][:, k, :], ybuf[j % 2][:, :], Y_AT[b][0][:, k, :].bitcast(F32), ALU.subtract).then_inc(y_low, 1)

        def merge_pair(kind, eng, j0, i=0, next_kt=4):
            nb = j0 // KT
            b = ORDER[nb]
            for s in range(2):
                t = Tile(MERGE0 + j0 + s, 2, i)
                j = lin(j0 + s, 2, i)
                d = lin(j0 % KT + s, 2, i)
                if kind == "gates":
                    if j0:
                        eng.wait_ge(merged, lin(TG * (j0 + s - 1), 2 * TG, i))
                    eng.dma_start(stage[:, s, :], proj[lin(GATE_TILE + KT * b + j0 % KT + s, 2, i), :, HALO:HALO + T]).then_inc(gate_ld[s], 16)
                if kind == "act":
                    make_hi(eng, t.next(), next_kt if s == 1 else 4)
                    eng.wait_ge(gate_ld[s], lin(16 * (j0 // 2 + 1), 16, i))
                    eng.activation(stage[:, s, :], stage[:, s, :], ACT.Sigmoid).then_inc(gate_sig, 1)
                if kind == "pool":
                    make_lo(eng, t.next(), next_kt if s == 1 else 4)
                if kind == "pe":
                    for g in range(TG):
                        dense(eng, t, g, None, 4, Y_AT[b])
                if kind == "dve":
                    eng.wait_ge(gate_sig, lin(j0 + s + 1, 2, i))
                    for g in range(TG):
                        cols = slice(g * GN, (g + 1) * GN)
                        eng.wait_ge(groups_done, t.number(TG, g + 1))
                        eng.tensor_tensor(e_c[:, cols], D[t.bank(g)][:, 0:GN], stage[:, s, cols], ALU.mult).then_inc(bank_free[t.bank(g)], 1)
                        eng.wait_ge(bank_free[t.bank(g)], t.bank_uses(g, 2))
                        if j0 + s + g:
                            eng.wait_ge(merged, lin(TG * (j0 + s) + g, 2 * TG, i))
                        a = acc[:, bass.ds(d, 1), cols].squeeze(1)
                        eng.tensor_tensor(a, a, e_c[:, cols], ALU.add).then_inc(merged, 1)

        def out_proj(kind, eng, t, d):
            if kind == "dve":
                for g in range(TG):
                    cols = slice(g * GN, (g + 1) * GN)
                    eng.wait_ge(groups_done, t.number(TG, g + 1))
                    a = acc[:, bass.ds(d, 1), cols].squeeze(1)
                    eng.tensor_tensor(a, a, D[t.bank(g)][:, 0:GN], ALU.add).then_inc(bank_free[t.bank(g)], 1)

        def ffn_block(kind, eng, i, last):
            for m in range(FT + KT):
                t = Tile(FFN0 + m, FT + KT, i) if not isinstance(i, int) else Tile(FFN0 + m + (FT + KT) * i)
                kt, nkt = (KT, KT if m < FT - 1 else FT) if m < FT else (FT, FT if m < FT + KT - 1 else KT)
                more = not (last and m == FT + KT - 1)
                blk_groups = TG * FT
                if kind == "sp":
                    if m < FT:
                        load_w(eng, t, w_full[lin(KT + m, FT, i)])
                    else:
                        load_w(eng, t, w_half[lin(24 + m - FT, KT, i)], FT)
                if kind == "pool" and more:
                    make_lo(eng, t.next(), nkt)
                if kind == "act" and more:
                    make_hi(eng, t.next(), nkt)
                if kind == "pe":
                    for g in range(TG):
                        if m == 0 and g == 0 and isinstance(i, int) and i == 0:
                            eng.wait_ge(*nm_dve["2"].after(f"l{KT - 1}"))
                        if m == FT:
                            eng.wait_ge(f_lo, lin(blk_groups - TG + g + 3, blk_groups, i))
                        dense(eng, t, g, None, kt, None if m < FT else (y_hi, y_lo))
                if m < FT and kind in ("act", "dve"):
                    for g in range(TG):
                        cols = slice(g * GN, (g + 1) * GN)
                        c = TG * m + g
                        u, v = (e_a, e_b) if c % 2 == 0 else (e_c, stage[:, 0, :])
                        u, v = u[:, cols], v[:, cols]
                        if kind == "act":
                            eng.wait_ge(f_lo, lin(c + 1, blk_groups, i))
                            eng.wait_ge(groups_done, t.number(TG, g + 1))
                            eng.activation(u, D[t.bank(g)][:, 0:GN], ACT.Relu).then_inc(bank_free[t.bank(g)], 1)
                            eng.wait_ge(bank_free[t.bank(g)], t.bank_uses(g, 2))
                            eng.activation(v, u, ACT.Square).then_inc(f_sq, 1)
                            eng.wait_ge(f_sq, lin(c + 1, blk_groups, i))
                            eng.activation(y_hi[:, m, cols], v, ACT.Copy).then_inc(f_hi, 1)
                        else:
                            eng.wait_ge(f_hi, lin(c + 1, blk_groups, i))
                            eng.tensor_tensor(y_lo[:, m, cols], v, y_hi[:, m, cols].bitcast(F32), ALU.subtract).then_inc(f_lo, 1)
                if m >= FT and kind == "dve":
                    for g in range(TG):
                        cols = slice(g * GN, (g + 1) * GN)
                        eng.wait_ge(groups_done, t.number(TG, g + 1))
                        eng.tensor_tensor(acc[:, m - FT, cols], acc[:, m - FT, cols], D[t.bank(g)][:, 0:GN], ALU.add).then_inc(bank_free[t.bank(g)], 1)

        ready, halo_st, acc_clear, n_out = sem("ready"), sem("halo_st"), sem("acc_clear"), sem("n_out")

        def of_state(x):
            return x.rearrange("b h k v -> k (b h) v")

        def flat_bh(x):
            return x[:, :, :, :].rearrange("k b h v -> k (b h) v")

        GD0 = GD_TILE
        SEG_ROW, SEG_HG = 1, 3
        LOOP_HG, LOOP_GD, LOOP_ML = GD0, GD0 + 18, GD0 + 36
        ROW_SLOTS, HG_SLOTS, GD_SLOTS, GX_SLOTS, ML_SLOTS = 6, 8, 21, 11, 6
        chunk_credit = {("hg", "pe"): hg_pe.sem, ("hg", "act"): hg_act.sem, ("hg", "dve"): hg_dve.sem, ("hg", "pool"): hg_pool.sem, ("hg", "out"): hg_out,
                        ("gd", "pe"): gd_pe.sem, ("gd", "act"): gd_act.sem, ("gd", "dve"): gd_dve.sem, ("gd", "pool"): gd_pool.sem, ("gd", "out"): gd_out,
                        ("ml", "pe"): ml_pe.sem, ("ml", "act"): ml_act.sem, ("ml", "dve"): ml_dve.sem, ("ml", "pool"): ml_pool.sem, ("ml", "out"): ml_out}
        mixers = (("hg", hgrn, LOOP_HG, HG_SLOTS, HG_SLOTS, 2), ("gd", gdn, LOOP_GD, GD_SLOTS, GX_SLOTS, 2), ("ml", mlstm, LOOP_ML, ML_SLOTS, ML_SLOTS, 4))

        def mix_program(kind, eng):
            f = Filler(kind, eng, Tile(0), 1, 1)
            f()
            f = Filler(kind, eng, Tile(SEG_ROW), 2, ROW_SLOTS)
            rows(kind, eng, f)
            f.done()
            with eng.Fori(0, (GD0 - SEG_HG) // 2) as i:
                Filler(kind, eng, Tile(SEG_HG, 2, i), 2, 1)()
            for name, mixer, first, slots, slots_s, tiles_s in mixers:
                if kind == "dve":
                    clear[name](eng)
                eng.sem_inc(chunk_credit[name, kind], 1)
                if kind == "act":
                    eng.sem_inc(chunk_credit[name, "out"], 16)
                with eng.Fori(0, NCH) as n:
                    f = Filler(kind, eng, Tile(first, 2, n), 2, slots)
                    mixer(kind, eng, n, f, False)
                    f.done()
                f = Filler(kind, eng, Tile(first + 2 * NCH), tiles_s, slots_s, 4 if name == "ml" else KT)
                mixer(kind, eng, 0, f, True)
                f.done()

        def clear_hg(eng):
            for s in (rw_pe, rw_act, rw_dve):
                eng.wait_ge(*s.all_of(1))
            eng.wait_ge(rw_out, 16)
            eng.wait_ge(rw_mo, 32)
            eng.memset(g_S[:, :], 0.0).then_inc(ready, 1)
            eng.memset(g_kl[:, :], 0.0).then_inc(ready, 1)

        def clear_gd(eng):
            eng.wait_ge(st_out, 16 * 2)
            for s in (hs_pe, hs_act, hs_dve, hs_pool):
                eng.wait_ge(*s.all_of(1))
            eng.wait_ge(hs_st, 16)
            eng.memset(d_S[:, :], 0.0).then_inc(ready, 1)

        def clear_ml(eng):
            eng.wait_ge(st_out, 16 * 5)
            for s in (gx_pe, gx_act, gx_dve, gx_pool):
                eng.wait_ge(*s.all_of(1))
            eng.wait_ge(gx_st, 16)
            eng.memset(m_C[:, :], 0.0).then_inc(ready, 1)
            eng.memset(m_N[:, :], 0.0).then_inc(ready, 1)

        clear = {"hg": clear_hg, "gd": clear_gd, "ml": clear_ml}
        BANKS_BEFORE_FFN = TG * FFN0
        ALL_GROUPS = TG * (FFN0 + FB * (FT + KT))

        def evacuated_all(eng, n_groups):
            eng.wait_ge(bank_free[0], (n_groups + 1) // 2 + 1)
            eng.wait_ge(bank_free[1], n_groups // 2 + 1)

        def mixer_loads(sp, name, mixer, first, slots, slots_s, tiles_s):
            mixer("sp", sp, None, None, False)
            with sp.Fori(0, NCH - 1) as n:
                for s in range(2):
                    load_w(sp, Tile(first + 2 + s, 2, n), w_proj[lin(first + 2 + s, 2, n)])
                mixer("sp", sp, n, None, False)
            for s in range(2):
                load_w(sp, Tile(first + 2 * NCH + s), w_proj[first + 2 * NCH + s])
            mixer("sp", sp, 0, None, True)
            for s in range(2):
                load_w(sp, Tile(first + 2 * NCH + 2 + s), w_proj[first + 2 * NCH + 2 + s]) if first + 2 * NCH + 2 + s < NPROJ - 2 or tiles_s == 2 else None

        block = ctx.enter_context(nc.Block())

        @block.sync
        def _(sp):
            sp.dma_start(cst[:, :], con).then_inc(const_ld, 16)
            sp.dma_start(prm[:, :], par).then_inc(const_ld, 16)
            sp.dma_start(xin[:, :, :], xT.rearrange("k p t -> p k t")).then_inc(x_ld, 16)
            load_w(sp, Tile(0), w_proj[0])
            load_w(sp, Tile(1), w_proj[1])
            sp.wait_ge(ready, 1)
            sp.dma_start(proj[GD_TILE:GD_TILE + 12, :, 0:HALO].rearrange("t p c -> p t c"), halo0[:, :].rearrange("p (t c) -> p t c", c=HALO)).then_inc(halo_st, 16)
            load_w(sp, Tile(2), w_proj[2])
            sp.wait_ge(*nm_dve["1"].all_of(1))
            sp.wait_ge(*nm_act["1"].all_of(1))
            load_w(sp, Tile(3), w_proj[3])
            rows("sp", sp, None)
            load_w(sp, Tile(4), w_proj[4])
            with sp.Fori(0, (GD0 - SEG_HG) // 2) as i:
                for s in range(2):
                    load_w(sp, Tile(SEG_HG + 2 + s, 2, i), w_proj[lin(SEG_HG + 2 + s, 2, i)])
            sp.wait_ge(halo_st, 16)
            sp.wait_ge(ready, 3)
            sp.dma_start(flat_bh(g_Ss), of_state(st_hg)).then_inc(hss_ld, 16)
            sp.wait_ge(hss_ld, 16)
            stored_all(sp, GD_TILE)
            mixer_loads(sp, *mixers[0])
            sp.wait_ge(*hg_dve.all_of(NCH))
            sp.dma_start(p_H.rearrange("h k v -> k h v"), g_S[:, :].rearrange("p (h v) -> p h v", v=HD)).then_inc(st_out, 16)
            sp.wait_ge(*hs_dve.all_of(1))
            sp.dma_start(of_state(s_H), flat_bh(g_Ss)).then_inc(st_out, 16)
            sp.wait_ge(ready, 4)
            sp.dma_start(flat_bh(d_Ss), of_state(st_gd)).then_inc(gxs_ld, 16)
            sp.wait_ge(gxs_ld, 16)
            stored_all(sp, ML_TILE)
            mixer_loads(sp, *mixers[1])
            sp.dma_start(p_S.rearrange("h k v -> k h v"), d_S[:, :].rearrange("p (h v) -> p h v", v=HD)).then_inc(st_out, 16)
            sp.wait_ge(*gx_dve.after("sx3"))
            sp.dma_start(s_conv, d_ch[:, 12 * NS:12 * NS + 12 * DEC_BATCH * HALO]).then_inc(st_out, 16)
            sp.wait_ge(*gx_dve.all_of(1))
            sp.dma_start(of_state(s_S), flat_bh(d_Ss)).then_inc(st_out, 16)
            sp.wait_ge(ready, 6)
            sp.dma_start(flat_bh(m_Cs), of_state(st_ml)).then_inc(mxs_ld, 16)
            sp.dma_start(m_Ns[:, :, :].rearrange("p b h -> p (b h)"), st_mn).then_inc(mxs_ld, 16)
            sp.wait_ge(mxs_ld, 32)
            stored_all(sp, GATE_TILE)
            mixer_loads(sp, *mixers[2])
            for s in range(2):
                load_w(sp, Tile(NPROJ - 2 + s), w_proj[NPROJ - 2 + s])
            sp.dma_start(p_conv, proj[GD_TILE:GD_TILE + 12, :, SEQ:SEQ + HALO]).then_inc(st_out, 16)
            sp.dma_start(p_C.rearrange("h k v -> k h v"), m_C[:, :].rearrange("p (h v) -> p h v", v=HD)).then_inc(st_out, 16)
            sp.wait_ge(n_out, 1)
            sp.dma_start(p_n, m_no[:, :]).then_inc(st_out, 16)
            sp.wait_ge(*mx_dve.all_of(1))
            sp.dma_start(s_n, m_Ns[:, :, :].rearrange("p b h -> p (b h)")).then_inc(st_out, 16)
            sp.dma_start(of_state(s_C), flat_bh(m_Cs)).then_inc(st_out, 16)
            for s in range(2):
                load_w(sp, Tile(MERGE0 + s), w_half[s], 4)
            stored_all(sp, NPROJ)
            merge_pair("gates", sp, 0)
            split_y("sp", sp)
            for s in range(2):
                load_w(sp, Tile(MERGE0 + 2 + s), w_half[2 + s], 4)
            for j0, count in ((2, 3), (8, 4), (16, 3)):
                with sp.Fori(0, count) as i:
                    merge_pair("gates", sp, j0, i)
                    for s in range(2):
                        load_w(sp, Tile(MERGE0 + j0 + 2 + s, 2, i), w_half[lin(j0 + 2 + s, 2, i)], 4)
            merge_pair("gates", sp, 22)
            for s in range(2):
                load_w(sp, Tile(OUT0 + s), w_full[s])
            sp.wait_ge(mg_lo, KT)
            sp.dma_start(acc[:, :, :], xT.rearrange("k p t -> p k t")).then_inc(resid_ld, 16)
            with sp.Fori(0, KT // 2 - 1) as i:
                for s in range(2):
                    load_w(sp, Tile(OUT0 + 2 + s, 2, i), w_full[lin(2 + s, 2, i)])
            with sp.Fori(0, FB) as i:
                ffn_block("sp", sp, i, False)
            for k in range(KT):
                sp.wait_ge(*fn_dve.after(f"s{k}"))
                sp.dma_start(yT[k], acc[:, k, :]).then_inc(y_st, 16)
            sp.wait_ge(y_st, 16 * KT)

        @block.gpsimd
        def _(pool):
            pool.memset(halo0[:, :], 0.0).then_inc(ready, 1)
            make_lo(pool, Tile(0))
            mix_program("pool", pool)
            for s in (mx_pe, mx_act, mx_dve, mx_pool):
                pool.wait_ge(*s.all_of(1))
            pool.wait_ge(mx_st, 16)
            pool.wait_ge(st_out, 16 * 10)
            pool.memset(acc[:, :, :], 0.0).then_inc(acc_clear, 1)
            merge_pair("pool", pool, 0)
            for j0, count in ((2, 3), (8, 4), (16, 3)):
                with pool.Fori(0, count) as i:
                    merge_pair("pool", pool, j0, i)
            merge_pair("pool", pool, 22, 0, KT)
            with pool.Fori(0, KT // 2) as i:
                for s in range(2):
                    make_lo(pool, Tile(OUT0 + s, 2, i).next())
            with pool.Fori(0, FB - 1) as i:
                ffn_block("pool", pool, i, False)
            ffn_block("pool", pool, FB - 1, True)

        @block.scalar
        def _(act):
            for b in range(2):
                act.sem_inc(bank_free[b], 1)
            act.wait_ge(*lb_dve.after("d"))
            act.activation(lbt[:, 1, :], lbt[:, 0, :], ACT.Exp).then_inc(*lb_act.step("e"))
            make_hi(act, Tile(0))
            norm("act", act, "1", xin, (nsq[:, :], ntmp[:, :]), stage[:, 0, :], nrs[:, :], (nsq[:, :], ntmp[:, :]), PC_N1, lambda e: e.wait_ge(x_ld, 16))
            mix_program("act", act)
            split_y("act", act)
            merge_pair("act", act, 0)
            for j0, count in ((2, 3), (8, 4), (16, 3)):
                with act.Fori(0, count) as i:
                    merge_pair("act", act, j0, i)
            merge_pair("act", act, 22, 0, KT)
            act.wait_ge(groups_done, TG * OUT0)
            act.wait_ge(merged, TG * 24)
            for k in range(KT):
                act.activation(xn_hi[:, k, :], acc[:, k, :], ACT.Copy).then_inc(mg_hi, 1)
            with act.Fori(0, KT // 2) as i:
                for s in range(2):
                    make_hi(act, Tile(OUT0 + s, 2, i).next())
            norm("act", act, "2", acc, (e_a[:, :], e_b[:, :]), e_c[:, :], stage[:, 0, :], (e_a[:, :], e_b[:, :]), PC_N2,
                 lambda e: evacuated_all(e, BANKS_BEFORE_FFN))
            with act.Fori(0, FB - 1) as i:
                ffn_block("act", act, i, False)
            ffn_block("act", act, FB - 1, True)
            norm("act", act, "3", acc, (e_a[:, :], e_b[:, :]), e_c[:, :], stage[:, 0, :], None, PC_NF,
                 lambda e: evacuated_all(e, ALL_GROUPS))

        @block.vector
        def _(dve):
            dve.wait_ge(const_ld, 32)
            logits = prm[:, PC_LB:PC_LB + H]
            dve.tensor_tensor(lbt[:, 0, :], logits, logits, ALU.subtract).then_inc(*lb_dve.step("d"))
            dve.wait_ge(*lb_act.after("e"))
            dve.reciprocal(lbt[:, 2, :], lbt[:, 1, :]).then_inc(*lb_dve.step("r"))
            dve.wait_ge(*lb_dve.after("r"))
            dve.tensor_tensor(lbt[:, 3, :], lbt[:, 1, :], lbt[:, 2, :], ALU.mult).then_inc(*lb_dve.step("n"))
            dve.wait_ge(*lb_dve.after("n"))
            dve.tensor_tensor(lbt[:, 4, :], lbt[:, 3, :], lbt[:, 3, :], ALU.subtract).then_inc(*lb_dve.step("lb"))
            dve.wait_ge(*lb_dve.after("lb"))
            dve.tensor_scalar(lbt[:, 5, :], lbt[:, 4, :], -1.0, 1.0, ALU.mult, ALU.add).then_inc(*lb_dve.step("om"))
            dve.wait_ge(*lb_dve.after("om"))
            norm("dve", dve, "1", xin, (nsq[:, :], ntmp[:, :]), stage[:, 0, :], nrs[:, :], (nsq[:, :], ntmp[:, :]), PC_N1, None)
            mix_program("dve", dve)
            split_y("dve", dve)
            dve.wait_ge(acc_clear, 1)
            merge_pair("dve", dve, 0)
            for j0, count in ((2, 3), (8, 4), (16, 3)):
                with dve.Fori(0, count) as i:
                    merge_pair("dve", dve, j0, i)
            merge_pair("dve", dve, 22, 0)
            for k in range(KT):
                dve.wait_ge(mg_hi, k + 1)
                dve.tensor_tensor(xn_lo[:, k, :], acc[:, k, :], xn_hi[:, k, :].bitcast(F32), ALU.subtract).then_inc(mg_lo, 1)
            dve.wait_ge(resid_ld, 16)
            with dve.Fori(0, KT // 2) as i:
                for s in range(2):
                    out_proj("dve", dve, Tile(OUT0 + s, 2, i), lin(s, 2, i))
            dve.sem_inc(f_lo, 2)
            norm("dve", dve, "2", acc, (e_a[:, :], e_b[:, :]), e_c[:, :], stage[:, 0, :], (e_a[:, :], e_b[:, :]), PC_N2, None)
            with dve.Fori(0, FB - 1) as i:
                ffn_block("dve", dve, i, False)
            ffn_block("dve", dve, FB - 1, True)
            norm("dve", dve, "3", acc, (e_a[:, :], e_b[:, :]), e_c[:, :], stage[:, 0, :], None, PC_NF, None)

        @block.tensor
        def _(pe):
            pe.wait_ge(const_ld, 32)
            norm("pe", pe, "1", xin, None, stage[:, 0, :], None, None, PC_N1, None)
            pe.wait_ge(*nm_dve["1"].after(f"l{KT - 1}"))
            mix_program("pe", pe)
            pe.wait_ge(y_low, 4)
            merge_pair("pe", pe, 0)
            for j0, count in ((2, 3), (8, 4), (16, 3)):
                if j0 > 2:
                    pe.wait_ge(y_low, 4 * (j0 // KT + 1))
                with pe.Fori(0, count) as i:
                    merge_pair("pe", pe, j0, i)
            merge_pair("pe", pe, 22, 0)
            pe.wait_ge(mg_lo, KT)
            with pe.Fori(0, KT // 2) as i:
                for s in range(2):
                    for g in range(TG):
                        dense(pe, Tile(OUT0 + s, 2, i), g, None)
            norm("pe", pe, "2", acc, None, e_c[:, :], None, None, PC_N2, None)
            pe.wait_ge(*nm_dve["2"].after(f"l{KT - 1}"))
            with pe.Fori(0, FB - 1) as i:
                ffn_block("pe", pe, i, False)
            ffn_block("pe", pe, FB - 1, True)
            norm("pe", pe, "3", acc, None, e_c[:, :], None, None, PC_NF, None)


def constants():
    s, t = np.arange(P)[:, None], np.arange(P)[None, :]
    seq = np.arange(NS) // DEC_SEQ
    c = np.zeros((P, CC_ALL), np.float32)
    c[:, CC_ID:CC_ID + P] = s == t
    c[:, CC_ONE:CC_ONE + P] = 1
    c[:, CC_NEGP:CC_NEGP + P] = np.where(s <= t, 0, MASKED)
    c[:NS, CC_NEGS:CC_NEGS + NS] = np.where((s <= t)[:NS, :NS] & (seq[:, None] == seq[None, :]), 0, MASKED)
    for j, hf in enumerate(HALVES):
        lev = (s // (2 * hf) == t // (2 * hf)) & (s % (2 * hf) < hf) & (t % (2 * hf) >= hf)
        c[:, CC_LEV + j * P:CC_LEV + (j + 1) * P] = lev
        for n, at, rows_ in ((CH, CC_HGP, P), (NS, CC_HGS, NS)):
            if n == NS and j > 1:
                continue
            part = lev[:rows_, :n][:, np.arange(n) % (2 * hf) >= hf]
            w = H * n // 2
            c[:rows_, at + j * w:at + (j + 1) * w] = np.tile(part, (1, H))
    c[:, CC_SEGP:CC_SEGP + 512] = np.arange(512) % CH != 0
    c[:, CC_SEGS:CC_SEGS + 128] = np.arange(128) % DEC_SEQ != 0
    c[:NS, CC_IND:CC_IND + DEC_BATCH] = seq[:, None] == np.arange(DEC_BATCH)
    at = np.arange(T)
    row = np.where(at < SEQ, at % CH != 0, (at - SEQ) % DEC_SEQ != 0)
    return c, np.tile(row.astype(np.float32), (H, 1))


def tiles(w, k_tiles):
    n = w.shape[1] // P
    return w.reshape(k_tiles, P, n, P).transpose(2, 1, 0, 3).reshape(n, P, k_tiles * P)


def kernel(**inputs):
    import concourse.bacc as _bacc
    from concourse import mybir as _mybir
    from concourse.bass_utils import run_bass_kernel_spmd as _run

    a = {k: np.asarray(v) for k, v in inputs.items()}
    x = np.concatenate([a["x_prompt"].reshape(SEQ, D_MODEL), a["x_sample"].reshape(NS, D_MODEL)], 0)
    w = a["w_in"][0]
    cuts = np.cumsum([0] + [W_MIX] * 4 + [H] * 2 + [W_MIX] * 4 + [H] * 2 + [W_MIX] * 4 + [D_MODEL] * 3)
    (ml_q, ml_k, ml_v, ml_o, ml_i, ml_f, gd_q, gd_k, gd_v, gd_z, gd_b, gd_a, hg_q, hg_f, hg_i, hg_g, ga, gb, gc) = (
        w[:, p:q] for p, q in zip(cuts[:-1], cuts[1:]))
    gates = np.concatenate([ml_i, ml_f, gd_b, gd_a, np.zeros((D_MODEL, P - 4 * H), w.dtype)], 1)
    w_cols = np.concatenate([gates, hg_q, hg_f, hg_i, hg_g, gd_q, gd_k, gd_v, gd_z, ml_q, ml_k, ml_v, ml_o, ga, gb, gc], 1)
    w_proj = tiles(w_cols, KT)
    wb = a["w_branch"][0]
    half = [tiles(wb[b], 4) for b in (HG, GD, ML)]
    down = a["w_down"][0].reshape(FB, FT * P, D_MODEL)
    half += [tiles(down[f], FT) for f in range(FB)]
    w_half = np.concatenate(half, 0)
    w_full = np.concatenate([tiles(a["w_out"][0], KT), tiles(a["w_up"][0], KT)], 0)

    def col(v):
        return v.reshape(-1, P).T

    con, segrow = constants()
    conv_w = a["gd_conv_w"][0].reshape(CONV_W * 12, P).T
    par = np.concatenate([col(a["norm1_w"][0]), col(a["norm2_w"][0]), col(a["final_norm_w"]), col(a["ml_norm_w"][0]),
                          col(a["gd_norm_w"][0]), col(a["hg_norm_w"][0]), col(a["hg_lb_logits"][0]), conv_w], 1)
    rowpar = np.stack([a["ml_i_bias"][0], a["ml_f_bias"][0], a["gd_A_log"][0], a["gd_dt_bias"][0]], 1)
    conv0 = a["state_gdn_conv"][0].reshape(DEC_BATCH, HALO, 12, P).transpose(3, 2, 0, 1).reshape(P, -1)
    ins = {
        "xT": x.T.reshape(KT, P, T), "w_proj": w_proj, "w_half": w_half, "w_full": w_full, "par": par, "con": con,
        "rowpar": rowpar, "segrow": segrow, "m0": a["state_mlstm_m"][0].T, "conv0": conv0, "st_ml": a["state_mlstm_C"][0],
        "st_mn": a["state_mlstm_n"][0].reshape(DEC_BATCH * H, HD).T, "st_gd": a["state_gdn_S"][0], "st_hg": a["state_hgrn_S"][0],
    }
    outs = {
        "yT": (KT, P, T), "p_C": (H, HD, HD), "p_n": (P, H), "p_m": (H, 1), "p_S": (H, HD, HD), "p_conv": (12, P, HALO),
        "p_H": (H, HD, HD), "s_C": (DEC_BATCH, H, HD, HD), "s_n": (P, DEC_BATCH * H), "s_m": (H, DEC_BATCH),
        "s_S": (DEC_BATCH, H, HD, HD), "s_conv": (P, 12 * DEC_BATCH * HALO), "s_H": (DEC_BATCH, H, HD, HD),
    }
    nc = _bacc.Bacc("TRN2", target_bir_lowering=False, num_devices=1)
    arrays, aps = {}, {}
    for k, v in ins.items():
        arrays[f"in_{k}"] = np.ascontiguousarray(v)
        aps[k] = nc.dram_tensor(f"in_{k}", v.shape, _mybir.dt.from_np(v.dtype), kind="ExternalInput").ap()
    for k, shape in outs.items():
        aps[k] = nc.dram_tensor(f"out_{k}", shape, F32, kind="ExternalOutput").ap()
    build(nc, **aps)
    r = _run(nc, [arrays], core_ids=[0]).results[0]
    o = {k: r[f"out_{k}"] for k in outs}
    y = o["yT"].reshape(D_MODEL, T).T
    one = (1, 1)
    return (
        np.ascontiguousarray(y[:SEQ]).reshape(1, SEQ, D_MODEL), np.ascontiguousarray(y[SEQ:]).reshape(DEC_BATCH, DEC_SEQ, D_MODEL),
        o["p_C"].reshape(*one, H, HD, HD), np.ascontiguousarray(o["p_n"].T).reshape(*one, H, HD), o["p_m"].reshape(*one, H),
        o["p_S"].reshape(*one, H, HD, HD), np.ascontiguousarray(o["p_conv"].transpose(2, 0, 1)).reshape(*one, HALO, 3 * W_MIX),
        o["p_H"].reshape(*one, H, HD, HD),
        o["s_C"].reshape(1, DEC_BATCH, H, HD, HD), np.ascontiguousarray(o["s_n"].T).reshape(1, DEC_BATCH, H, HD),
        np.ascontiguousarray(o["s_m"].T).reshape(1, DEC_BATCH, H), o["s_S"].reshape(1, DEC_BATCH, H, HD, HD),
        np.ascontiguousarray(o["s_conv"].reshape(P, 12, DEC_BATCH, HALO).transpose(2, 3, 1, 0)).reshape(1, DEC_BATCH, HALO, 3 * W_MIX),
        o["s_H"].reshape(1, DEC_BATCH, H, HD, HD),
    )
```

```python
import math
from contextlib import ExitStack

import numpy as np

import concourse.bass as bass
from concourse import mybir

ALU = mybir.AluOpType
ACT = mybir.ActivationFunctionType
F32 = mybir.dt.float32
F32R = mybir.dt.float32r

P = 128
D_MODEL = 1024
SEQ = 1024
DEC_BATCH = 8
DEC_SEQ = 4
NS = DEC_BATCH * DEC_SEQ
T = SEQ + NS
W_MIX = D_MODEL // 2
H = 4
HD = 128
CONV_W = 4
HALO = CONV_W - 1
D_FF = 4 * D_MODEL
EPS = 1e-6
KT = D_MODEL // P
CH = 128
NCH = SEQ // CH
TG = 3
GN = T // TG
NPIECE = 3
ROWS_TILE = 0
HG_TILE = 1
GD_TILE = HG_TILE + 16
ML_TILE = GD_TILE + 16
GATE_TILE = ML_TILE + 16
NPROJ = GATE_TILE + 24
MERGE0 = NPROJ
OUT0 = MERGE0 + 24
FFN0 = OUT0 + KT
FB = 8
FT = D_FF // P // FB
CLAMP = -44.0
MASKED = -1e30
HALVES = [1, 2, 4, 8, 16, 32, 64]
ML, GD, HG = range(3)
ROW_U, ROW_ELW, ROW_EM, ROW_G, ROW_BETA, ROW_EG, ROW_BEG = range(7)
TOK_W, TOK_EWS, TOK_NG, TOK_BETA, TOK_KD = range(5)
PC_N1, PC_N2, PC_NF, PC_MLN, PC_GDN, PC_HGN, PC_LB, PC_CONV = 0, 8, 16, 24, 28, 29, 33, 37
PC_ALL = PC_CONV + CONV_W * 12
CC_ID, CC_ONE, CC_NEGP, CC_NEGS, CC_LEV, CC_SEGP, CC_SEGS, CC_IND = 0, 128, 256, 384, 416, 1312, 1824, 1952
CC_HGP = 1960
CC_HGS = CC_HGP + 7 * 256
CC_ALL = CC_HGS + 2 * 64


def lin(const, step, i):
    return i * step + const


class Steps:

    def __init__(self, sem, names, credit=0):
        self.sem, self.names, self.credit, self.at = sem, names, credit, 0

    def step(self, name):
        assert self.names[self.at % len(self.names)] == name, (name, self.names[self.at % len(self.names)])
        self.at += 1
        return self.sem, 1

    def after(self, name, n=0, ahead=0):
        return self.sem, lin(self.names.index(name) + 1 + self.credit + len(self.names) * ahead, len(self.names), n)

    def all_of(self, n):
        return self.sem, lin(self.credit, len(self.names), n)


class Tile:

    def __init__(self, base, step=0, i=0):
        self.base, self.stride, self.i = base, step, i

    def next(self, k=1):
        return Tile(self.base + k, self.stride, self.i)

    @property
    def slot(self):
        return self.base % 2

    def number(self, times=1, plus=0):
        return lin(self.base * times + plus, self.stride * times, self.i)

    def uses(self, plus=0):
        return lin(self.base // 2 + plus, self.stride // 2, self.i)

    def bank(self, g):
        return (TG * self.base + g) % 2

    def bank_uses(self, g, plus=0):
        return lin((TG * self.base + g) // 2 + plus, TG * self.stride // 2, self.i)


def build(nc, xT, w_proj, w_half, w_full, par, con, rowpar, segrow, m0, conv0, st_ml, st_mn, st_gd, st_hg,
          yT, p_C, p_n, p_m, p_S, p_conv, p_H, s_C, s_n, s_m, s_S, s_conv, s_H):
    proj = nc.dram_tensor("proj", (NPROJ, P, HALO + T), F32, kind="Internal").ap()
    rowd = nc.dram_tensor("rowd", (7, H, T), F32, kind="Internal").ap()
    yd = nc.dram_tensor("yd", (12, P, T), F32, kind="Internal").ap()
    with ExitStack() as ctx:
        def sb(name, shape, dt=F32):
            return ctx.enter_context(nc.sbuf_tensor(name, shape, dt))

        def sem(name):
            return ctx.enter_context(nc.semaphore(name))

        xn_hi, xn_lo = sb("xn_hi", [P, KT, T], F32R), sb("xn_lo", [P, KT, T], F32R)
        w_raw = sb("w_raw", [P, 2, KT * P])
        w_hi, w_lo = [sb(f"w_hi{s}", [P, KT, P], F32R) for s in range(2)], [sb(f"w_lo{s}", [P, KT, P], F32R) for s in range(2)]
        stage = sb("stage", [P, 2, T])
        cst = sb("cst", [P, CC_ALL])
        prm = sb("prm", [P, PC_ALL])
        tok = sb("tok", [P, 5, NCH + 1, H])
        tokc = sb("tokc", [P, 5, H])
        lbt = sb("lbt", [P, 6, H])
        halo0 = sb("halo0", [P, 12 * HALO])
        ident, ones = cst[:, CC_ID:CC_ID + P], cst[:, CC_ONE:CC_ONE + P]

        arena_of = {}

        def arena(stack, name, shape, dt=F32):
            arena_of[name] = stack.enter_context(nc.sbuf_tensor(name, shape, dt))
            return arena_of[name]

        with ExitStack() as a:
            xin = arena(a, "xin", [P, KT, T])
            nsq = arena(a, "nsq", [P, T])
            ntmp = arena(a, "ntmp", [P, T])
            nrs = arena(a, "nrs", [P, T])
        with ExitStack() as a:
            r_in = arena(a, "r_in", [H, 4, T])
            r_a = arena(a, "r_a", [H, 3, T])
            r_b = arena(a, "r_b", [H, 2, T])
            r_m = arena(a, "r_m", [H, T])
            r_row = arena(a, "r_row", [H, 7, T])
            r_tok = arena(a, "r_tok", [H, 5, T])
            r_mp = arena(a, "r_mp", [H, 2 * NCH])
            r_t8 = arena(a, "r_t8", [H, DEC_BATCH])
            r_mo = arena(a, "r_mo", [H, 1 + DEC_BATCH])
            r_par = arena(a, "r_par", [H, 5])
        N4 = H * CH
        with ExitStack() as a:
            g_Ss = arena(a, "g_Ss", [P, DEC_BATCH, H, HD])
            g_in = arena(a, "g_in", [P, 3 * N4])
            g_v = arena(a, "g_v", [P, N4])
            g_x = arena(a, "g_x", [P, 3 * N4])
            g_sg = arena(a, "g_sg", [P, 3 * N4])
            g_sl = arena(a, "g_sl", [P, 2 * N4])
            g_k = arena(a, "g_k", [P, N4])
            g_lf = arena(a, "g_lf", [P, N4])
            g_b = arena(a, "g_b", [P, N4])
            g_dq = arena(a, "g_dq", [P, 7 * 256])
            g_dk = arena(a, "g_dk", [P, 7 * 256])
            g_e2 = arena(a, "g_e2", [P, 2, N4])
            g_ql = arena(a, "g_ql", [P, 7 * 256])
            g_kl = arena(a, "g_kl", [P, 7 * N4])
            g_vt = arena(a, "g_vt", [P, N4])
            g_rr = arena(a, "g_rr", [P, CH])
            g_S = arena(a, "g_S", [P, N4])
            g_mm, g_vx = g_dq, g_kl
            g_long = [[g_Ss[:, 4 * k:4 * k + 4].rearrange("p a h v -> p (a h v)")[:, m * N4:(m + 1) * N4] for k in range(2) for m in range(3)],
                      [g_x[:, 0:N4], g_sg[:, N4 // 4:N4], g_k, g_lf, g_b, g_v]]
        with ExitStack() as a:
            d_Ss = arena(a, "d_Ss", [P, DEC_BATCH, H, HD])
            d_ch = arena(a, "d_ch", [P, 12 * (CH + HALO)])
            d_sx = arena(a, "d_sx", [P, 12, DEC_BATCH, HALO + DEC_SEQ])
            d_cv = arena(a, "d_cv", [P, 16 * CH])
            d_pa = arena(a, "d_pa", [P, 16 * CH])
            d_pb = arena(a, "d_pb", [P, 16 * CH])
            d_qk = arena(a, "d_qk", [P, 2 * N4])
            d_bc = arena(a, "d_bc", [P, 4 * N4])
            d_de = arena(a, "d_de", [P, N4])
            d_at = arena(a, "d_at", [P, N4])
            d_lt = arena(a, "d_lt", [P, N4])
            d_mt = arena(a, "d_mt", [P, 7 * N4])
            d_tt = arena(a, "d_tt", [P, N4])
            d_t = arena(a, "d_t", [P, N4])
            d_vb = arena(a, "d_vb", [P, N4])
            d_kd = arena(a, "d_kd", [P, N4])
            d_r = arena(a, "d_r", [P, N4])
            d_S = arena(a, "d_S", [P, N4])
            d_xs, d_vn = d_de, d_lt
            d_sc = d_Ss[:, :, :, :].rearrange("p b h v -> p (b h v)")
        with ExitStack() as a:
            m_Cs = arena(a, "m_Cs", [P, DEC_BATCH, H, HD])
            m_in = arena(a, "m_in", [P, 4 * N4])
            m_bc = arena(a, "m_bc", [P, 3 * N4])
            m_ks = arena(a, "m_ks", [P, N4])
            m_e = arena(a, "m_e", [P, N4])
            m_pt = arena(a, "m_pt", [P, N4])
            m_so = arena(a, "m_so", [P, N4])
            m_gw = arena(a, "m_gw", [P, N4])
            m_qw = arena(a, "m_qw", [P, N4])
            m_vt = arena(a, "m_vt", [P, N4])
            m_kt = arena(a, "m_kt", [P, N4])
            m_dn = arena(a, "m_dn", [P, N4])
            m_rd = arena(a, "m_rd", [P, N4])
            m_h = arena(a, "m_h", [P, N4])
            m_sq = arena(a, "m_sq", [P, N4])
            m_y = arena(a, "m_y", [P, N4])
            m_C = arena(a, "m_C", [P, N4])
            m_N = arena(a, "m_N", [P, H])
            m_no = arena(a, "m_no", [P, H])
            m_Ns = arena(a, "m_Ns", [P, DEC_BATCH, H])
            m_qn = arena(a, "m_qn", [P, N4])
            m_vx = arena(a, "m_vx", [NS, 2 * DEC_BATCH * HD])
        with ExitStack() as a:
            acc = arena(a, "acc", [P, KT, T])
            y_hi = arena(a, "y_hi", [P, 4, T], F32R)
            y_lo = arena(a, "y_lo", [P, 4, T], F32R)
            e_a = arena(a, "e_a", [P, T])
            e_b = arena(a, "e_b", [P, T])
            e_c = arena(a, "e_c", [P, T])
            e_3 = arena(a, "e_3", [P, 3, T])

        D = [ctx.enter_context(nc.psum_tensor(f"D{i}", [P, 512], F32)) for i in range(2)]
        M = [ctx.enter_context(nc.psum_tensor(f"M{i}", [P, 512], F32)) for i in range(6)]

        const_ld, masks_ld = sem("const_ld"), sem("masks_ld")
        x_ld = [sem(f"x_ld{k}") for k in range(KT)]
        w_loaded = [sem(f"w_loaded{s}") for s in range(2)]
        w_hi_made, w_lo_made, groups_done = sem("w_hi_made"), sem("w_lo_made"), sem("groups_done")
        bank_free = [sem(f"bank_free{b}") for b in range(2)]
        evacuated = sem("evacuated")
        stage_stored = [sem(f"stage_stored{s}") for s in range(2)]

        def steps(name, names, credit=0):
            return Steps(sem(name), names.split(), credit)

        def load_w(sp, t, src, kt=KT):
            if not (isinstance(t.i, int) and t.base < 2):
                sp.wait_ge(w_lo_made, t.number(plus=-1))
            sp.dma_start(w_raw[:, t.slot, 0:kt * P], src).then_inc(w_loaded[t.slot], 16)

        def load_f(sp, t, src, kt=KT):
            buf, loaded, _ = raw(t)
            sp.wait_ge(w_lo_made, t.number(plus=-2))
            sp.dma_start(buf[:, 0:kt * P], src).then_inc(loaded, 16)

        def raw(t):
            if t.base >= FFN0:
                s, use = (t.base - FFN0) % 3, (t.base - FFN0) // 3
                return e_3[:, s, 0:KT * P], f_loaded[s], lin(16 * (use + 1), 16 * t.stride // 3, t.i)
            return w_raw[:, t.slot, :], w_loaded[t.slot], lin(16 * (t.base // 2 + 1), 8 * t.stride, t.i)

        def make_hi(act, t, kt=KT):
            if not (isinstance(t.i, int) and t.base < 2):
                act.wait_ge(groups_done, t.number(TG, -TG))
            buf, loaded, value = raw(t)
            act.wait_ge(loaded, value)
            nc.scalar.activation(w_hi[t.slot][:, 0:kt, :], buf[:, 0:kt * P].rearrange("p (k m) -> p k m", m=P),
                                 ACT.Copy).then_inc(w_hi_made, 1)

        def make_lo(pool, t, kt=KT):
            pool.wait_ge(w_hi_made, t.number(plus=1))
            nc.gpsimd.tensor_tensor(w_lo[t.slot][:, 0:kt, :], raw(t)[0][:, 0:kt * P].rearrange("p (k m) -> p k m", m=P),
                                    w_hi[t.slot][:, 0:kt, :].bitcast(F32), ALU.subtract).then_inc(w_lo_made, 1)

        def dense(pe, t, g, third, kt=KT, src=None, before=None):
            hi, lo = src or (xn_hi, xn_lo)
            b = t.bank(g)
            ks = range(kt) if third is None else range(kt * third // NPIECE, kt * (third + 1) // NPIECE)
            if ks[0] == 0:
                if g == 0:
                    pe.wait_ge(w_lo_made, t.number(plus=1))
                pe.wait_ge(bank_free[b], t.bank_uses(g, 1))
            cols = slice(g * GN, (g + 1) * GN)
            for k in ks:
                if before is not None:
                    before(g, k)
                last = None
                for n, (w, x) in enumerate(((w_hi, hi), (w_hi, lo), (w_lo, hi))):
                    last = nc.tensor.matmul(D[b][:, 0:GN], w[t.slot][:, k, :], x[:, k, cols],
                                            start=(k == 0 and n == 0), stop=(k == kt - 1 and n == 2))
                if k == kt - 1:
                    last.then_inc(groups_done, 1)

        def evac_proj(act, t, g):
            if g == 0 and not (isinstance(t.i, int) and t.base < 2):
                act.wait_ge(stage_stored[t.slot], lin(16 * (t.base // 2), 8 * t.stride, t.i))
            act.wait_ge(groups_done, t.number(TG, g + 1))
            nc.scalar.activation(stage[:, t.slot, g * GN:(g + 1) * GN], D[t.bank(g)][:, 0:GN],
                                 ACT.Copy).then_inc(bank_free[t.bank(g)], 1)
            if g == TG - 1:
                act.wait_ge(bank_free[t.bank(2)], t.bank_uses(2, 2))
                act.wait_ge(bank_free[t.bank(1)], t.bank_uses(1, 2))
                act.dma_start(proj[t.number(), :, HALO:HALO + T], stage[:, t.slot, :]).then_inc(stage_stored[t.slot], 16)

        def stored_all(eng, n_tiles):
            eng.wait_ge(stage_stored[0], 16 * ((n_tiles + 1) // 2))
            eng.wait_ge(stage_stored[1], 16 * (n_tiles // 2))

        class Filler:
            def __init__(self, kind, eng, tile, n_tiles, slots, last_kt=KT):
                self.last_kt, self.kind, self.eng, self.tile, self.n, self.at = last_kt, kind, eng, tile, n_tiles, 0
                self.weights = [1] * slots if isinstance(slots, int) else slots
                self.late, self.before = [], None

            def evacuate(self):
                for t, g, kt in self.late:
                    if g is None:
                        (make_hi if self.kind == "act" else make_lo)(self.eng, t, kt)
                    else:
                        evac_proj(self.eng, t, g)
                self.late = []

            def __call__(self):
                pieces = self.n * TG * NPIECE
                a, b = (pieces * sum(self.weights[:self.at + k]) // sum(self.weights) for k in range(2))
                self.at += 1
                self.evacuate()
                for j in range(a, b):
                    t = self.tile.next(j // (TG * NPIECE))
                    next_kt = self.last_kt if j // (TG * NPIECE) == self.n - 1 else KT
                    g, third = j % (TG * NPIECE) // NPIECE, j % NPIECE
                    if self.kind == "pe":
                        dense(self.eng, t, g, third, before=self.before)
                    elif self.kind == "act":
                        if g == 0 and third == 0:
                            self.late.append((t.next(), None, next_kt))
                        if third == NPIECE - 1:
                            self.late.append((t, g, None))
                        if b - a > NPIECE + 1:
                            self.evacuate()
                    elif self.kind == "pool":
                        if g == 0 and third == 0:
                            self.late.append((t.next(), None, next_kt))
                        if b - a > NPIECE + 1:
                            self.evacuate()

            def done(self):
                self.evacuate()
                assert self.at == len(self.weights), (self.at, len(self.weights))

        STATE_STEPS = "vx0 vx1 s20a s20b vx2 s21a s21b vx3 s22a s22b s23a s23b"
        DECAY_STEPS = " s10 s11 s12 s13"
        hg_in = sem("hg_in")
        hg_pe = steps("hg_pe", "vt diag lev kt o kv ss", credit=1)
        hf_act, hf_dve, hf_pool = steps("hf_act", "e l s lf"), steps("hf_dve", "cl sl g1 g2 b"), steps("hf_pool", "k1 k2")
        hg_act = steps("hg_act", "eq ek eb ed vt kt sq rl rr", credit=1)
        hg_dve = steps("hg_dve", " ".join(f"dq{j}" for j in range(7)) + " "
                       + " ".join(f"ql{j}" for j in range(7)) + " qe at mk0 mk1 mk2 mk3 "
                       + " ".join(f"ad{j}" for j in range(7)) + " s1 s2 y1 y2", credit=1)
        hg_pool = steps("hg_pool", " ".join(f"dk{j}" for j in range(7)) + " dl "
                        + " ".join(f"kl{j}" for j in range(7)) + " kd gw", credit=1)
        hg_v = sem("hg_v")
        hg_out = sem("hg_out")
        hs_in = sem("hs_in")
        hs_st = sem("hs_st")
        hs_pe = steps("hs_pe", "vt diag lev kt o ss " + " ".join(f"kv{h}" for h in range(H)))
        hsf_act, hsf_dve, hsf_pool = steps("hsf_act", "e l s lf"), steps("hsf_dve", "cl sl g1 g2 b"), steps("hsf_pool", "k1 k2")
        hs_act = steps("hs_act", "eq ek eb ed vt kt sq rl rr")
        hs_dve = steps("hs_dve", "dq0 dq1 ql0 ql1 qe at mk0 ad0 ad1 y1 y2 "
                       + STATE_STEPS)
        hs_pool = steps("hs_pool", "dk0 dk1 dl kl0 kl1 kd gw" + DECAY_STEPS)
        lb_dve, lb_act = steps("lb_dve", "d r n lb om"), steps("lb_act", "e")

        def pcols(tile, ntile, col, n):
            v = proj[tile:tile + ntile].rearrange("t p c -> p t c")
            return v[:, :, bass.ds(col, n)]

        def ycols(branch, col, n):
            return yd[4 * branch:4 * branch + 4].rearrange("t p c -> p t c")[:, :, bass.ds(col, n)]

        def next_chunk(n):
            return (None, 0) if n is None else (n, n * CH + CH)

        def prefetch(eng, prev, step):
            if prev is not None:
                eng.wait_ge(*step[0].after(step[1], prev))

        def after_chunks(eng, n, of, out=None):
            for s in of:
                eng.wait_ge(*s.all_of(n))
            if out is not None:
                eng.wait_ge(out, lin(16, 16, n))

        def sample_states(kind, eng, steps_of, kv, read, S, decay, vt, vx, kt, banks):
            pe_, dve_, pool_ = steps_of
            if kind == "pool":
                eng.wait_ge(*pe_.after(read))
                for h in range(H):
                    eng.tensor_tensor(S[:, :, h, :], S[:, :, h, :], decay(h).unsqueeze(2).to_broadcast([P, DEC_BATCH, HD]),
                                      ALU.mult).then_inc(*pool_.step(f"s1{h}"))

            def spread(h):
                n = DEC_BATCH * HD
                eng.tensor_tensor(vx[0:NS, h % 2 * n:(h % 2 + 1) * n].rearrange("p (b v) -> p b v", v=HD),
                                  vt[0:NS, h * HD:(h + 1) * HD].unsqueeze(1).to_broadcast([NS, DEC_BATCH, HD]),
                                  cst[0:NS, CC_IND:CC_IND + DEC_BATCH].unsqueeze(2).to_broadcast([NS, DEC_BATCH, HD]),
                                  ALU.mult).then_inc(*dve_.step(f"vx{h}"))

            if kind == "dve":
                spread(0)
                spread(1)
                for h in range(H):
                    eng.wait_ge(*pool_.after(f"s1{h}"))
                    eng.wait_ge(*pe_.after(f"{kv}{h}"))
                    for q, x in enumerate("ab"):
                        eng.tensor_tensor(S[:, 4 * q:4 * q + 4, h, :], S[:, 4 * q:4 * q + 4, h, :],
                                          M[banks[h % 2][q]][:, :].rearrange("p (b v) -> p b v", v=HD), ALU.add).then_inc(*dve_.step(f"s2{h}{x}"))
                    if h + 2 < H:
                        spread(h + 2)
            if kind == "pe":
                for h in range(H):
                    eng.wait_ge(*dve_.after(f"vx{h}"))
                    if h >= 2:
                        eng.wait_ge(*dve_.after(f"s2{h - 2}b"))
                    for q in range(2):
                        at = h % 2 * DEC_BATCH * HD + q * 512
                        i = eng.matmul(M[banks[h % 2][q]][:, :], kt[0:NS, h * HD:(h + 1) * HD], vx[0:NS, at:at + 512], start=True, stop=True)
                    i.then_inc(*pe_.step(f"{kv}{h}"))

        def hgrn_front(kind, eng, n, ahead, sample):
            N = NS if sample else CH
            C4 = H * N
            act_, dve_, pool_ = (hsf_act, hsf_dve, hsf_pool) if sample else (hf_act, hf_dve, hf_pool)

            def hn(x, o=0):
                return x[:, o:o + C4].rearrange("p (h n) -> p h n", n=N)

            def per_head(x):
                return x.unsqueeze(2).to_broadcast([P, H, N])

            if kind == "act":
                eng.wait_ge(*dve_.after("cl", n, ahead))
                eng.activation(g_x[:, 0:3 * C4], g_x[:, 0:3 * C4], ACT.Exp, scale=-1.0).then_inc(*act_.step("e"))
                eng.wait_ge(*act_.after("e", n, ahead))
                eng.activation(g_sg[:, 0:3 * C4], g_x[:, 0:3 * C4], ACT.Ln, bias=1.0).then_inc(*act_.step("l"))
                eng.wait_ge(*act_.after("l", n, ahead))
                eng.activation(g_sg[:, 0:3 * C4], g_sg[:, 0:3 * C4], ACT.Exp, scale=-1.0).then_inc(*act_.step("s"))
                eng.wait_ge(*dve_.after("g2", n, ahead))
                eng.activation(g_lf[:, 0:C4], g_lf[:, 0:C4], ACT.Ln).then_inc(*act_.step("lf"))
            if kind == "dve":
                eng.wait_ge(hs_in if sample else hg_in, 64 if sample else lin(48 + 48 * ahead, 48, n))
                if ahead:
                    eng.wait_ge(*pool_.after("k1", n))
                eng.tensor_scalar(g_x[:, 0:3 * C4], g_in[:, 0:3 * C4], CLAMP, None, ALU.max).then_inc(*dve_.step("cl"))
                eng.wait_ge(*act_.after("s", n, ahead))
                if ahead:
                    eng.wait_ge(*hg_pe.after("diag", n))
                    eng.wait_ge(*hg_pool.after("gw", n))
                    eng.wait_ge(*hg_dve.after("qe", n))
                eng.tensor_tensor(g_sl[:, 0:2 * C4], g_in[:, 0:2 * C4], g_sg[:, 0:2 * C4], ALU.mult).then_inc(*dve_.step("sl"))
                eng.tensor_tensor(hn(g_lf), hn(g_sg, 2 * C4), per_head(lbt[:, 5, :]), ALU.mult).then_inc(*dve_.step("g1"))
                eng.wait_ge(*dve_.after("g1", n, ahead))
                eng.tensor_tensor(hn(g_lf), hn(g_lf), per_head(lbt[:, 4, :]), ALU.add).then_inc(*dve_.step("g2"))
                eng.wait_ge(*act_.after("lf", n, ahead))
                if ahead:
                    eng.wait_ge(*hg_act.after("eb", n))
                seg = cst[:, CC_SEGS:CC_SEGS + C4] if sample else cst[:, CC_SEGP:CC_SEGP + C4]
                eng.tensor_tensor_scan(g_b[:, 0:C4], seg, g_lf[:, 0:C4], 0.0, ALU.mult, ALU.add).then_inc(*dve_.step("b"))
            if kind == "pool":
                eng.wait_ge(*act_.after("s", n, ahead))
                if ahead:
                    eng.wait_ge(*hg_pe.after("diag", n))
                    eng.wait_ge(*hg_pool.after("kd", n))
                eng.tensor_tensor(g_k[:, 0:C4], g_x[:, 2 * C4:3 * C4], g_sg[:, 2 * C4:3 * C4], ALU.mult).then_inc(*pool_.step("k1"))
                eng.wait_ge(*pool_.after("k1", n, ahead))
                eng.tensor_tensor(hn(g_k), hn(g_k), per_head(lbt[:, 5, :]), ALU.mult).then_inc(*pool_.step("k2"))

        def hgrn(kind, eng, n, slot, sample, with_next=False):
            N = NS if sample else CH
            C4 = H * N
            halves = HALVES[:2] if sample else HALVES
            L = len(halves)
            HF = C4 // 2
            pe_, act_, dve_, pool_ = (hs_pe, hs_act, hs_dve, hs_pool) if sample else (hg_pe, hg_act, hg_dve, hg_pool)
            col0 = SEQ if sample else None if n is None else n * CH

            def hn(x, o=0):
                return x[:, o:o + C4].rearrange("p (h n) -> p h n", n=N)

            def blk(x, hf, o=0):
                return x[:, o:o + C4].rearrange("p (b c) -> p b c", c=2 * hf)

            def cb(x, hf, o):
                return x[:, o:o + HF].rearrange("p (b c) -> p b c", c=hf)

            def tk(x, h=None):
                v = x[0:N, :].rearrange("p (h n) -> p h n", n=HD)
                return v if h is None else v[:, h, :]

            df, pf = (hsf_dve, hsf_pool) if sample else (hf_dve, hf_pool)
            g_qe, g_gw, g_y, g_kd, g_kt, g_at = g_long[sample]

            states = (kind, eng, (hs_pe, hs_dve, hs_pool), "kv", "o", g_Ss, lambda h: g_e2[:, 0, h * N + DEC_SEQ - 1:(h + 1) * N:DEC_SEQ],
                      g_vt, g_vx, g_kt, ((4, 5), (0, 2)))

            def front():
                if with_next:
                    hgrn_front(kind, eng, n, 1, False)

            if kind == "sp":
                sm = hs_in if sample else hg_in
                if sample:
                    for s in (hg_pe, hg_act, hg_dve, hg_pool):
                        eng.wait_ge(*s.all_of(NCH))
                    eng.wait_ge(hg_out, 16 * (NCH + 1))
                else:
                    n, col0 = next_chunk(n)
                    prefetch(eng, n, (hf_dve, "sl"))
                for i, tile in enumerate((0, 12, 4)):
                    eng.dma_start(hn(g_in, i * C4), pcols(HG_TILE + tile, 4, lin(HALO, 1, col0), N)).then_inc(sm, 16)
                if not sample:
                    prefetch(eng, n, (pe_, "vt"))
                eng.dma_start(hn(g_v), pcols(HG_TILE + 8, 4, lin(HALO, 1, col0), N)).then_inc(sm if sample else hg_v, 16)
                if sample:
                    eng.dma_start(flat_bh(g_Ss), of_state(st_hg)).then_inc(hss_ld, 16)
                else:
                    slot()
                return
            loaded = (hs_in, 64) if sample else None if n is None else (hg_v, lin(16, 16, n))
            if not sample and kind != "pe":
                after_chunks(eng, n, [x for k, x in (("pe", pe_), ("act", act_), ("dve", dve_), ("pool", pool_)) if k != kind])
            if kind == "act":
                slot()
                slot()
                eng.wait_ge(*dve_.after(f"dq{L - 1}", n))
                eng.activation(g_dq[:, 0:L * HF], g_dq[:, 0:L * HF], ACT.Exp).then_inc(*act_.step("eq"))
                slot()
                eng.wait_ge(*pool_.after("dl", n))
                eng.activation(g_dk[:, 0:L * HF], g_dk[:, 0:L * HF], ACT.Exp).then_inc(*act_.step("ek"))
                eng.activation(g_e2[:, 0, 0:C4], g_b[:, 0:C4], ACT.Exp).then_inc(*act_.step("eb"))
                eng.activation(g_e2[:, 1, 0:C4], g_e2[:, 1, 0:C4], ACT.Exp).then_inc(*act_.step("ed"))
                eng.wait_ge(*pe_.after("vt", n))
                eng.activation(g_vt[0:N, :], M[5][0:N, :], ACT.Copy).then_inc(*act_.step("vt"))
                slot()
                front()
                eng.wait_ge(*pe_.after("kt", n))
                eng.activation(g_kt[0:N, 0:H * HD], M[0][0:N, :], ACT.Copy).then_inc(*act_.step("kt"))
                slot()
                slot()
                if not sample:
                    eng.wait_ge(hg_out, lin(16, 16, n))
                eng.wait_ge(*pe_.after("o", n))
                eng.activation(g_y[:, 0:C4], M[1][:, 0:C4], ACT.Square).then_inc(*act_.step("sq"))
                slot()
                eng.wait_ge(*pe_.after("ss", n))
                eng.activation(g_rr[:, 0:N], M[3][:, 0:N], ACT.Ln, bias=EPS, scale=1.0 / W_MIX).then_inc(*act_.step("rl"))
                eng.wait_ge(*act_.after("rl", n))
                eng.activation(g_rr[:, 0:N], g_rr[:, 0:N], ACT.Exp, scale=-0.5).then_inc(*act_.step("rr"))
                eng.wait_ge(*dve_.after("y2", n))
                eng.dma_start(ycols(HG, col0, N), hn(g_y)).then_inc(hs_st if sample else hg_out, 16)
                slot()
            if kind == "dve":
                eng.wait_ge(*df.after("b", n))
                for j, hf in enumerate(halves):
                    b = blk(g_b, hf)
                    eng.tensor_tensor(cb(g_dq, hf, j * HF), b[:, :, hf:2 * hf],
                                      b[:, :, hf - 1:hf].to_broadcast([P, C4 // (2 * hf), hf]),
                                      ALU.subtract).then_inc(*dve_.step(f"dq{j}"))
                slot()
                slot()
                slot()
                eng.wait_ge(*act_.after("eq", n))
                for j, hf in enumerate(halves):
                    eng.tensor_tensor(cb(g_ql, hf, j * HF), blk(g_sl, hf)[:, :, hf:2 * hf], cb(g_dq, hf, j * HF),
                                      ALU.mult).then_inc(*dve_.step(f"ql{j}"))
                eng.wait_ge(*act_.after("eb", n))
                eng.tensor_tensor(g_qe[:, 0:C4], g_sl[:, 0:C4], g_e2[:, 0, 0:C4], ALU.mult).then_inc(*dve_.step("qe"))
                slot()
                eng.wait_ge(*pe_.after("diag", n))
                eng.tensor_tensor(g_at[0:N, 0:C4].rearrange("p (h n) -> p h n", n=N), M[0][0:N, 0:C4].rearrange("p (h n) -> p h n", n=N),
                                  cst[0:N, CC_ID:CC_ID + N].unsqueeze(1).to_broadcast([N, H, N]), ALU.mult).then_inc(*dve_.step("at"))
                front()
                eng.wait_ge(*pe_.after("lev", n))
                msk = CC_HGS if sample else CC_HGP
                for q in range((L + 1) // 2):
                    w = min(2, L - 2 * q) * HF
                    eng.tensor_tensor(g_mm[0:N, 2 * q * HF:2 * q * HF + w], M[1 + q][0:N, 0:w],
                                      cst[0:N, msk + 2 * q * HF:msk + 2 * q * HF + w], ALU.mult).then_inc(*dve_.step(f"mk{q}"))
                for j, hf in enumerate(halves):
                    eng.wait_ge(*(dve_.after(f"mk{(L + 1) // 2 - 1}" if j == 0 else f"ad{j - 1}", n)))
                    a = g_at[0:N, 0:C4].rearrange("p (b c) -> p b c", c=2 * hf)[:, :, hf:2 * hf]
                    eng.tensor_tensor(a, a, g_mm[0:N, j * HF:(j + 1) * HF].rearrange("p (b c) -> p b c", c=hf),
                                      ALU.add).then_inc(*dve_.step(f"ad{j}"))
                slot()
                slot()
                if not sample:
                    eng.wait_ge(*pe_.after("o", n))
                    eng.tensor_tensor(hn(g_S), hn(g_S), hn(g_e2[:, 0, :])[:, :, N - 1:N].to_broadcast([P, H, HD]),
                                      ALU.mult).then_inc(*dve_.step("s1"))
                    eng.wait_ge(*dve_.after("s1", n))
                    eng.wait_ge(*pe_.after("kv", n))
                    eng.tensor_tensor(g_S[:, :], g_S[:, :], M[2][:, :], ALU.add).then_inc(*dve_.step("s2"))
                slot()
                eng.wait_ge(*act_.after("rr", n))
                eng.tensor_tensor(hn(g_y), hn(M[1]), g_rr[:, 0:N].unsqueeze(1).to_broadcast([P, H, N]),
                                  ALU.mult).then_inc(*dve_.step("y1"))
                eng.wait_ge(*dve_.after("y1", n))
                eng.wait_ge(*pool_.after("gw", n))
                eng.tensor_tensor(g_y[:, 0:C4], g_y[:, 0:C4], g_gw[:, 0:C4], ALU.mult).then_inc(*dve_.step("y2"))
                if sample:
                    sample_states(*states)
                slot()
            if kind == "pool":
                eng.wait_ge(*df.after("b", n))
                for j, hf in enumerate(halves):
                    b = blk(g_b, hf)
                    eng.tensor_tensor(cb(g_dk, hf, j * HF), b[:, :, hf - 1:hf].to_broadcast([P, C4 // (2 * hf), hf]),
                                      b[:, :, 0:hf], ALU.subtract).then_inc(*pool_.step(f"dk{j}"))
                if sample:
                    bb = g_b[:, 0:C4].rearrange("p (g c) -> p g c", c=DEC_SEQ)
                    eng.tensor_tensor(g_e2[:, 1, 0:C4].rearrange("p (g c) -> p g c", c=DEC_SEQ),
                                      bb[:, :, DEC_SEQ - 1:DEC_SEQ].to_broadcast([P, C4 // DEC_SEQ, DEC_SEQ]), bb,
                                      ALU.subtract).then_inc(*pool_.step("dl"))
                else:
                    eng.tensor_tensor(hn(g_e2[:, 1, :]), hn(g_b)[:, :, N - 1:N].to_broadcast([P, H, N]), hn(g_b),
                                      ALU.subtract).then_inc(*pool_.step("dl"))
                slot()
                slot()
                eng.wait_ge(*act_.after("ek", n))
                for j, hf in enumerate(halves):
                    eng.tensor_tensor(blk(g_kl, hf, j * N4)[:, :, 0:hf], blk(g_k, hf)[:, :, 0:hf], cb(g_dk, hf, j * HF),
                                      ALU.mult).then_inc(*pool_.step(f"kl{j}"))
                eng.wait_ge(*act_.after("ed", n))
                eng.tensor_tensor(g_kd[:, 0:C4], g_k[:, 0:C4], g_e2[:, 1, 0:C4], ALU.mult).then_inc(*pool_.step("kd"))
                eng.tensor_tensor(hn(g_gw), hn(g_sl, C4), prm[:, PC_HGN:PC_HGN + H].unsqueeze(2).to_broadcast([P, H, N]),
                                  ALU.mult).then_inc(*pool_.step("gw"))
                front()
                for _ in range(5):
                    slot()
                if sample:
                    sample_states(*states)
                slot()
            if kind == "pe":
                slot()
                if not sample:
                    after_chunks(eng, n, [act_])
                eng.wait_ge(*loaded)
                for h in range(H):
                    i = eng.transpose(M[5][0:N, h * HD:(h + 1) * HD], hn(g_v)[:, h, :], ident)
                i.then_inc(*pe_.step("vt"))
                eng.wait_ge(*df.after("sl", n))
                eng.wait_ge(*pf.after("k2", n))
                for h in range(H):
                    i = eng.matmul(M[0][0:N, h * N:(h + 1) * N], hn(g_k)[:, h, :], hn(g_sl)[:, h, :], start=True, stop=True)
                i.then_inc(*pe_.step("diag"))
                slot()
                slot()
                slot()
                if not sample:
                    after_chunks(eng, n, [dve_])
                eng.wait_ge(*dve_.after(f"ql{L - 1}", n))
                eng.wait_ge(*pool_.after(f"kl{L - 1}", n))
                for j in range(L):
                    for h in range(H):
                        o = (j % 2) * HF + h * (N // 2)
                        i = eng.matmul(M[1 + j // 2][0:N, o:o + N // 2], hn(g_kl, j * N4)[:, h, :],
                                       g_ql[:, j * HF + h * (N // 2):j * HF + (h + 1) * (N // 2)], start=True, stop=True)
                i.then_inc(*pe_.step("lev"))
                eng.wait_ge(*dve_.after("at", n))
                eng.wait_ge(*pool_.after("kd", n))
                for h in range(H):
                    i = eng.transpose(M[0][0:N, h * HD:(h + 1) * HD], hn(g_kd)[:, h, :], ident)
                i.then_inc(*pe_.step("kt"))
                slot()
                slot()
                eng.wait_ge(*act_.after("vt", n))
                eng.wait_ge(*dve_.after(f"ad{L - 1}", n))
                for h in range(H):
                    if sample and h == 0:
                        eng.wait_ge(hss_ld, 16)
                    i = eng.matmul(M[1][:, h * N:(h + 1) * N], tk(g_vt, h), g_at[0:N, h * N:(h + 1) * N], start=(not sample or h == 0), stop=False, skip_group_check=sample)
                    if sample:
                        for b in range(DEC_BATCH):
                            c = h * N + b * DEC_SEQ
                            i = eng.matmul(M[1][:, c:c + DEC_SEQ], g_Ss[:, b, h, :], g_qe[:, c:c + DEC_SEQ],
                                           start=False, stop=(h == H - 1 and b == DEC_BATCH - 1), skip_group_check=True)
                    else:
                        i = eng.matmul(M[1][:, h * N:(h + 1) * N], g_S[:, h * HD:(h + 1) * HD], g_qe[:, h * N:(h + 1) * N],
                                       start=False, stop=True)
                i.then_inc(*pe_.step("o"))
                if not sample:
                    eng.wait_ge(*act_.after("kt", n))
                    for h in range(H):
                        i = eng.matmul(M[2][:, h * HD:(h + 1) * HD], tk(g_kt, h), tk(g_vt, h), start=True, stop=True)
                    i.then_inc(*pe_.step("kv"))
                slot()
                eng.wait_ge(*act_.after("sq", n))
                for h in range(H):
                    i = eng.matmul(M[3][:, 0:N], ones, g_y[:, h * N:(h + 1) * N], start=(h == 0), stop=(h == H - 1))
                i.then_inc(*pe_.step("ss"))
                if sample:
                    sample_states(*states)
                slot()

        rw_in, rw_out, rw_mo, seg_ld = sem("rw_in"), sem("rw_out"), sem("rw_mo"), sem("seg_ld")
        rw_act = steps("rw_act", "e l ea be bl bs em elw ews kd eg tok toks")
        rw_dve = steps("rw_dve", "i z az x ax bc mn fl mx sp g bcum gcum m "
                       + " ".join(f"t{k} m{k}" for k in range(DEC_SEQ))
                       + " mp0 mp1 mp2 u w lw1 lw2 em ew1 ew2 ng kd1 kd2 beg mo1 mo2")
        rw_pe = steps("rw_pe", "tok")

        def rows(kind, eng, slot):
            def ends(x):
                return x[:, CH - 1:SEQ:CH], x[:, SEQ + DEC_SEQ - 1:T:DEC_SEQ]

            def cut(x):
                return (x[:, 0:SEQ].rearrange("h (c n) -> h c n", n=CH), x[:, SEQ:T].rearrange("h (c n) -> h c n", n=DEC_SEQ))

            if kind == "sp":
                eng.dma_start(r_mp[:, NCH:2 * NCH], m0).then_inc(rw_in, 16)
                eng.dma_start(r_tok[:, TOK_KD, :], segrow).then_inc(seg_ld, 16)
                eng.dma_start(r_par[:, 0:4], rowpar).then_inc(rw_in, 16)
                stored_rows(eng)
                eng.dma_start(r_in[:, :, :], proj[ROWS_TILE, 0:4 * H, HALO:HALO + T].rearrange("(q h) t -> h q t", h=H)).then_inc(rw_in, 16)
                return
            if kind == "dve":
                eng.wait_ge(rw_in, 48)

                def ts(name, out, in_, s1, s2, o0, o1=None):
                    a = (o0,) if o1 is None else (o0, o1)
                    eng.tensor_scalar(out, in_, s1, s2, *a).then_inc(*rw_dve.step(name))
                    eng.wait_ge(*rw_dve.after(name))

                def tt(name, out, a, b, op):
                    eng.tensor_tensor(out, a, b, op).then_inc(*rw_dve.step(name))
                    eng.wait_ge(*rw_dve.after(name))

                def mag(name, out, x):
                    eng.scalar_tensor_tensor(out, x, -1.0, x, ALU.mult, ALU.max).then_inc(*rw_dve.step(name))
                    eng.wait_ge(*rw_dve.after(name))
                ts("i", r_in[:, 0, :], r_in[:, 0, :], r_par[:, 0:1], None, ALU.add)
                ts("z", r_in[:, 1, :], r_in[:, 1, :], r_par[:, 1:2], None, ALU.add)
                mag("az", r_a[:, 0, :], r_in[:, 1, :])
                ts("x", r_in[:, 3, :], r_in[:, 3, :], r_par[:, 3:4], None, ALU.add)
                mag("ax", r_a[:, 1, :], r_in[:, 3, :])
                ts("bc", r_a[:, 2, :], r_in[:, 2, :], CLAMP, None, ALU.max)
                slot()
                eng.wait_ge(*rw_act.after("l"))
                ts("mn", r_m[:, :], r_in[:, 1, :], 0.0, None, ALU.min)
                tt("fl", r_in[:, 1, :], r_m[:, :], r_a[:, 0, :], ALU.subtract)
                ts("mx", r_m[:, :], r_in[:, 3, :], 0.0, None, ALU.max)
                tt("sp", r_m[:, :], r_m[:, :], r_a[:, 1, :], ALU.add)
                eng.wait_ge(*rw_act.after("ea"))
                ts("g", r_in[:, 3, :], r_m[:, :], r_par[:, 4:5], -1.0, ALU.mult, ALU.mult)
                seg = r_tok[:, TOK_KD, :]
                eng.wait_ge(seg_ld, 16)
                eng.tensor_tensor_scan(r_a[:, 0, :], seg, r_in[:, 1, :], 0.0, ALU.mult, ALU.add).then_inc(*rw_dve.step("bcum"))
                eng.tensor_tensor_scan(r_row[:, ROW_G, :], seg, r_in[:, 3, :], 0.0, ALU.mult, ALU.add).then_inc(*rw_dve.step("gcum"))
                slot()
                eng.tensor_tensor_scan(r_m[:, 0:SEQ], r_in[:, 1, 0:SEQ], r_in[:, 0, 0:SEQ], 0.0, ALU.add,
                                       ALU.max).then_inc(*rw_dve.step("m"))
                for k in range(DEC_SEQ):
                    at = slice(SEQ + k, T, DEC_SEQ)
                    prev = r_mp[:, NCH:2 * NCH] if k == 0 else r_m[:, SEQ + k - 1:T:DEC_SEQ]
                    tt(f"t{k}", r_t8[:, :], r_in[:, 1, at], prev, ALU.add)
                    tt(f"m{k}", r_m[:, at], r_t8[:, :], r_in[:, 0, at], ALU.max)
                eng.memset(r_mp[:, 0:1], 0.0).then_inc(*rw_dve.step("mp0"))
                ts("mp1", r_mp[:, 1:NCH], r_m[:, CH - 1:SEQ - CH:CH], 0.0, None, ALU.add)
                ts("mp2", r_mo[:, 0:1], r_m[:, SEQ - 1:SEQ], 0.0, None, ALU.add)
                slot()
                tt("u", r_row[:, ROW_U, :], r_a[:, 0, :], r_m[:, :], ALU.subtract)
                tt("w", r_tok[:, TOK_W, :], r_in[:, 0, :], r_a[:, 0, :], ALU.subtract)
                prev = (r_mp[:, 0:NCH].unsqueeze(2).to_broadcast([H, NCH, CH]),
                        r_mp[:, NCH:2 * NCH].unsqueeze(2).to_broadcast([H, DEC_BATCH, DEC_SEQ]))
                for k, (o, u, m_) in enumerate(zip(cut(r_row[:, ROW_ELW, :]), cut(r_row[:, ROW_U, :]), prev)):
                    tt(f"lw{k + 1}", o, u, m_, ALU.add)
                ts("em", r_row[:, ROW_EM, :], r_m[:, :], -1.0, None, ALU.mult)
                for k, (o, w, u) in enumerate(zip(cut(r_tok[:, TOK_EWS, :]), cut(r_tok[:, TOK_W, :]), cut(r_row[:, ROW_U, :]))):
                    n = (CH, DEC_SEQ)[k]
                    tt(f"ew{k + 1}", o, w, u[:, :, n - 1:n].to_broadcast([H, 8, n]), ALU.add)
                ts("ng", r_tok[:, TOK_NG, :], r_row[:, ROW_G, :], -1.0, None, ALU.mult)
                for k, (o, gg) in enumerate(zip(cut(r_tok[:, TOK_KD, :]), cut(r_row[:, ROW_G, :]))):
                    n = (CH, DEC_SEQ)[k]
                    tt(f"kd{k + 1}", o, gg[:, :, n - 1:n].to_broadcast([H, 8, n]), gg, ALU.subtract)
                slot()
                eng.wait_ge(*rw_act.after("eg"))
                tt("beg", r_row[:, ROW_BEG, :], r_row[:, ROW_BETA, :], r_row[:, ROW_EG, :], ALU.mult)
                ts("mo1", r_mo[:, 1:1 + DEC_BATCH], r_m[:, SEQ + DEC_SEQ - 1:T:DEC_SEQ], 0.0, None, ALU.add)
                ts("mo2", r_tok[:, TOK_BETA, :], r_row[:, ROW_BETA, :], 0.0, None, ALU.add)
                slot()
                slot()
            if kind == "act":
                eng.wait_ge(*rw_dve.after("bc"))
                eng.activation(r_b[:, :, :], r_a[:, 0:2, :], ACT.Exp, scale=-1.0).then_inc(*rw_act.step("e"))
                eng.wait_ge(*rw_act.after("e"))
                eng.activation(r_a[:, 0:2, :], r_b[:, :, :], ACT.Ln, bias=1.0).then_inc(*rw_act.step("l"))
                eng.activation(r_par[:, 4:5], r_par[:, 2:3], ACT.Exp).then_inc(*rw_act.step("ea"))
                eng.activation(r_a[:, 2, :], r_a[:, 2, :], ACT.Exp, scale=-1.0).then_inc(*rw_act.step("be"))
                eng.wait_ge(*rw_act.after("be"))
                eng.activation(r_a[:, 2, :], r_a[:, 2, :], ACT.Ln, bias=1.0).then_inc(*rw_act.step("bl"))
                eng.wait_ge(*rw_act.after("bl"))
                eng.activation(r_row[:, ROW_BETA, :], r_a[:, 2, :], ACT.Exp, scale=-1.0).then_inc(*rw_act.step("bs"))
                slot()
                slot()
                slot()
                eng.wait_ge(*rw_dve.after("em"))
                eng.activation(r_row[:, ROW_EM, :], r_row[:, ROW_EM, :], ACT.Exp).then_inc(*rw_act.step("em"))
                eng.activation(r_row[:, ROW_ELW, :], r_row[:, ROW_ELW, :], ACT.Exp).then_inc(*rw_act.step("elw"))
                eng.wait_ge(*rw_dve.after("kd2"))
                eng.activation(r_tok[:, TOK_EWS, :], r_tok[:, TOK_EWS, :], ACT.Exp).then_inc(*rw_act.step("ews"))
                eng.activation(r_tok[:, TOK_KD, :], r_tok[:, TOK_KD, :], ACT.Exp).then_inc(*rw_act.step("kd"))
                eng.activation(r_row[:, ROW_EG, :], r_row[:, ROW_G, :], ACT.Exp).then_inc(*rw_act.step("eg"))
                slot()
                eng.wait_ge(*rw_dve.after("mo2"))
                eng.wait_ge(*rw_act.after("eg"))
                eng.dma_start(rowd.rearrange("q h t -> h q t"), r_row[:, :, :]).then_inc(rw_out, 16)
                eng.dma_start(p_m, r_mo[:, 0:1]).then_inc(rw_mo, 16)
                eng.dma_start(s_m, r_mo[:, 1:1 + DEC_BATCH]).then_inc(rw_mo, 16)
                slot()
                eng.wait_ge(*rw_pe.after("tok"))
                eng.activation(tok[:, :, 0:NCH, :].rearrange("p q c h -> p q (c h)"),
                               M[0][:, 0:5 * NCH * H].rearrange("p (q c) -> p q c", q=5), ACT.Copy).then_inc(*rw_act.step("tok"))
                eng.activation(tok[0:NS, :, NCH, :], M[1][0:NS, 0:5 * H].rearrange("p (q h) -> p q h", q=5),
                               ACT.Copy).then_inc(*rw_act.step("toks"))
                slot()
            if kind == "pool":
                for _ in range(6):
                    slot()
            if kind == "pe":
                for _ in range(5):
                    slot()
                eng.wait_ge(*rw_dve.after("mo2"))
                eng.wait_ge(*rw_act.after("eg"))
                for q in range(5):
                    for c in range(NCH):
                        i = eng.transpose(M[0][:, (q * NCH + c) * H:(q * NCH + c + 1) * H], r_tok[:, q, c * CH:(c + 1) * CH], ident[0:H, 0:H])
                    i = eng.transpose(M[1][0:NS, q * H:(q + 1) * H], r_tok[:, q, SEQ:T], ident[0:H, 0:H])
                i.then_inc(*rw_pe.step("tok"))
                slot()

        def stored_rows(eng):
            eng.wait_ge(stage_stored[0], 16)

        gd_in, gd_rows, gd_out = sem("gd_in"), sem("gd_rows"), sem("gd_out")
        gx_in, gx_st = sem("gx_in"), sem("gx_st")
        inv0 = sem("inv0")
        d_vx = d_mt[:, 0:2 * DEC_BATCH * HD]
        gd_pe = steps("gd_pe", "nq kkqk vk ks tr " + " ".join(f"x{j} y{j}" for j in range(1, 7)) + " vn o su ss", credit=1)
        gf_act = steps("gf_act", "e l s sq")
        gf_dve = steps("gf_dve", "c0 c2 a1 a2 cl cs")
        gf_pool = steps("gf_pool", "c1 c3 a")
        gd_act = steps("gd_act", "lq lk rq rk de0 de1 de2 de3 tr " + " ".join(f"x{j}" for j in range(1, 7)) + " vn sq2 rl rr", credit=1)
        gd_dve = steps("gd_dve", "tc qn kn ga lt lb m0 vb kd qkd r " + " ".join(f"tm{j} tt{j}" for j in range(1, 6))
                       + " tt6 s1 s2 y1 y2", credit=1)
        gd_pool = steps("gd_pool", "kb qg zw " + " ".join(f"mt{j}" for j in range(1, 7)), credit=1)
        gx_pe = steps("gx_pe", "nq kkqk vk ks kst tr x1 y1 vn o ss " + " ".join(f"su{h}" for h in range(H)))
        gxf_act = steps("gxf_act", "e l s sq")
        gxf_dve = steps("gxf_dve", "sx1 sx2 sx3 c0 c2 a1 a2 cl cs")
        gxf_pool = steps("gxf_pool", "c1 c3 a")
        gx_act = steps("gx_act", "lq lk rq rk de0 de1 de2 de3 kst tr x1 vn sq2 rl rr")
        gx_dve = steps("gx_dve", "tc qn kn ga lt lb m0 vb kd qkd r tt1 y1 y2 "
                       + STATE_STEPS)
        gx_pool = steps("gx_pool", "kb qg zw mt1" + DECAY_STEPS)

        def gdn_front(kind, eng, n, ahead, part, sample):
            N = NS if sample else CH
            C4, C12, C16 = H * N, 12 * N, 16 * N
            act_, dve_, pool_ = (gxf_act, gxf_dve, gxf_pool) if sample else (gf_act, gf_dve, gf_pool)
            scratch = d_sc if ahead else d_mt
            tap2, tap3, squares = scratch[:, C12:2 * C12], scratch[:, 0:C12], d_mt if sample else d_sc

            def tap(j):
                if sample:
                    return d_sx[:, :, :, j:j + DEC_SEQ]
                return d_ch[:, :].rearrange("p (t c) -> p t c", c=CH + HALO)[:, :, j:j + CH]

            def conv(x):
                if sample:
                    return x[:, 0:C12].rearrange("p (t b c) -> p t b c", b=DEC_BATCH, c=DEC_SEQ)
                return x[:, 0:C12].rearrange("p (t c) -> p t c", c=CH)

            def weight(j):
                w = prm[:, PC_CONV + 12 * j:PC_CONV + 12 * (j + 1)].unsqueeze(2)
                return w.unsqueeze(3).to_broadcast([P, 12, DEC_BATCH, DEC_SEQ]) if sample else w.to_broadcast([P, 12, CH])

            loaded = (gx_in, 16 * 7) if sample else (gd_in, lin(32 + 32 * ahead, 32, n))
            if kind == "dve":
                if part == 0:
                    eng.wait_ge(*loaded)
                    if sample:
                        before = d_ch[:, C12:C12 + 12 * DEC_BATCH * HALO].rearrange("p (t b c) -> p t b c", b=DEC_BATCH, c=HALO)
                        eng.tensor_copy(d_sx[:, :, :, HALO:], d_ch[:, 0:C12].rearrange("p (t b c) -> p t b c", b=DEC_BATCH, c=DEC_SEQ)).then_inc(*dve_.step("sx1"))
                        eng.tensor_copy(d_sx[:, :, :, 0:HALO], before).then_inc(*dve_.step("sx2"))
                        eng.wait_ge(*dve_.after("sx2"))
                        eng.tensor_copy(before, d_sx[:, :, :, DEC_SEQ:]).then_inc(*dve_.step("sx3"))
                    if ahead:
                        eng.wait_ge(*gd_pe.after("vk", n))
                        eng.wait_ge(*gd_pool.after("zw", n))
                    eng.tensor_tensor(conv(d_cv), tap(0), weight(0), ALU.mult).then_inc(*dve_.step("c0"))
                if part == 1:
                    eng.tensor_tensor(conv(tap2), tap(2), weight(2), ALU.mult).then_inc(*dve_.step("c2"))
                if part == 2:
                    eng.wait_ge(*dve_.after("c2", n, ahead))
                    eng.tensor_tensor(d_cv[:, 0:C12], d_cv[:, 0:C12], tap2[:, 0:C12], ALU.add).then_inc(*dve_.step("a1"))
                if part == 3:
                    eng.wait_ge(*dve_.after("a1", n, ahead))
                    eng.wait_ge(*pool_.after("a", n, ahead))
                    eng.tensor_tensor(d_cv[:, 0:C12], d_cv[:, 0:C12], d_pa[:, 0:C12], ALU.add).then_inc(*dve_.step("a2"))
                    eng.wait_ge(*dve_.after("a2", n, ahead))
                    eng.tensor_scalar(d_pa[:, 0:C16], d_cv[:, 0:C16], CLAMP, None, ALU.max).then_inc(*dve_.step("cl"))
                if part == 4:
                    eng.wait_ge(*act_.after("s", n, ahead))
                    eng.tensor_tensor(d_cv[:, 0:C16], d_cv[:, 0:C16], d_pa[:, 0:C16], ALU.mult).then_inc(*dve_.step("cs"))
            if kind == "pool":
                eng.wait_ge(*loaded)
                if sample:
                    eng.wait_ge(*dve_.after("sx2"))
                if ahead:
                    eng.wait_ge(*gd_pe.after("nq", n))
                    eng.wait_ge(*dve_.after("cs", n))
                eng.tensor_tensor(conv(d_pa), tap(1), weight(1), ALU.mult).then_inc(*pool_.step("c1"))
                eng.tensor_tensor(conv(tap3), tap(3), weight(3), ALU.mult).then_inc(*pool_.step("c3"))
                eng.wait_ge(*pool_.after("c3", n, ahead))
                eng.tensor_tensor(d_pa[:, 0:C12], d_pa[:, 0:C12], tap3[:, 0:C12], ALU.add).then_inc(*pool_.step("a"))
            if kind == "act":
                if part == 0:
                    eng.wait_ge(*dve_.after("cl", n, ahead))
                    eng.activation(d_pa[:, 0:C16], d_pa[:, 0:C16], ACT.Exp, scale=-1.0).then_inc(*act_.step("e"))
                if part == 1:
                    eng.wait_ge(*act_.after("e", n, ahead))
                    eng.activation(d_pa[:, 0:C16], d_pa[:, 0:C16], ACT.Ln, bias=1.0).then_inc(*act_.step("l"))
                if part == 2:
                    eng.wait_ge(*act_.after("l", n, ahead))
                    eng.activation(d_pa[:, 0:C16], d_pa[:, 0:C16], ACT.Exp, scale=-1.0).then_inc(*act_.step("s"))
                if part == 3:
                    eng.wait_ge(*dve_.after("cs", n, ahead))
                    if not ahead and not sample:
                        eng.wait_ge(states_out, 16)
                    eng.activation(squares[:, 0:2 * C4], d_cv[:, 0:2 * C4], ACT.Square).then_inc(*act_.step("sq"))

        def gdn(kind, eng, n, slot, sample, with_next=False):
            N = NS if sample else CH
            C4 = H * N
            J = 2 if sample else 7
            pe_, act_, dve_, pool_ = (gx_pe, gx_act, gx_dve, gx_pool) if sample else (gd_pe, gd_act, gd_dve, gd_pool)
            col0 = SEQ if sample else None if n is None else n * CH
            C12, C16 = 12 * N, 16 * N

            def hn(x, o=0):
                return x[:, o:o + C4].rearrange("p (h n) -> p h n", n=N)

            def sq(x, h=None, o=0):
                v = x[0:N, o:o + C4].rearrange("p (h n) -> p h n", n=N)
                return v if h is None else v[:, h, :]

            def half(x, j, side, h=None):
                x = x[0:N, 0:C4] if h is None else x[0:N, h * N:(h + 1) * N]
                return x.rearrange("p (g c) -> p g c", c=2 << j)[:, :, side << j:(side + 1) << j]

            def tk(x, h=None):
                v = x[0:N, :].rearrange("p (h n) -> p h n", n=HD)
                return v if h is None else v[:, h, :]

            af = gxf_act if sample else gf_act
            squares = d_mt if sample else d_sc

            states = (kind, eng, (gx_pe, gx_dve, gx_pool), "su", "o", d_Ss,
                      lambda h: d_bc[:, 2 * C4 + h * N + DEC_SEQ - 1:2 * C4 + (h + 1) * N:DEC_SEQ], d_vn, d_vx, d_kd, ((0, 1), (2, 3)))

            def front(part=0):
                if with_next:
                    gdn_front(kind, eng, n, 1, part, False)

            if kind == "sp":
                sm = gx_in if sample else gd_in
                if sample:
                    for s in (gd_pe, gd_act, gd_dve, gd_pool):
                        eng.wait_ge(*s.all_of(NCH))
                    eng.wait_ge(gd_out, 16 * (NCH + 1))
                    eng.dma_start(d_ch[:, 0:C12].rearrange("p (t c) -> p t c", c=N), pcols(GD_TILE, 12, col0 + HALO, N)).then_inc(sm, 16)
                    eng.dma_start(d_ch[:, C12:C12 + 12 * DEC_BATCH * HALO], conv0).then_inc(sm, 16)
                else:
                    n, col0 = next_chunk(n)
                    prefetch(eng, n, (gf_dve, "c2"))
                    prefetch(eng, n, (gf_pool, "c3"))
                    eng.dma_start(d_ch[:, :].rearrange("p (t c) -> p t c", c=CH + HALO), pcols(GD_TILE, 12, col0, CH + HALO)).then_inc(sm, 16)
                    prefetch(eng, n, (pool_, "zw"))
                eng.dma_start(d_cv[:, C12:C16].rearrange("p (t c) -> p t c", c=N), pcols(GD_TILE + 12, 4, lin(HALO, 1, col0), N)).then_inc(sm, 16)
                if not sample:
                    slot()
                    prefetch(eng, n, (dve_, "s1"))
                for k, q in enumerate((ROW_G, ROW_BETA, ROW_EG, ROW_BEG)):
                    eng.dma_start(hn(d_bc, k * C4), rowd[q:q + 1][:, :, bass.ds(col0, N)].rearrange("a h t -> (a h) t").unsqueeze(0).to_broadcast([P, H, N])).then_inc(sm if sample else gd_rows, 16)
                if sample:
                    eng.dma_start(flat_bh(d_Ss), of_state(st_gd)).then_inc(gxs_ld, 16)
                return
            loaded = (gx_in, 16 * 7) if sample else None if n is None else (gd_in, lin(32, 32, n))
            if not sample:
                after_chunks(eng, n, {"pe": [act_], "act": [pe_], "dve": [pe_, act_, pool_], "pool": [pe_, dve_]}[kind])
            GBC, BBC, EGB, BEGB = (hn(d_bc, k * C4) for k in range(4))
            if kind == "dve":
                tok_at = tok[:, :, NCH, :] if sample else tok[:, :, bass.ds(n, 1), :].squeeze(2) if not isinstance(n, int) else tok[:, :, n, :]
                eng.tensor_scalar(tokc[0:N, :, :], tok_at[0:N], 0.0, None, ALU.add).then_inc(*dve_.step("tc"))
                slot()
                slot()
                eng.wait_ge(*act_.after("rk", n))
                eng.tensor_tensor(d_qk[:, 0:C4], d_cv[:, 0:C4], d_pb[:, 0:C4], ALU.mult).then_inc(*dve_.step("qn"))
                eng.tensor_tensor(d_qk[:, C4:2 * C4], d_cv[:, C4:2 * C4], d_pb[:, C4:2 * C4], ALU.mult).then_inc(*dve_.step("kn"))
                neg = cst[0:N, CC_NEGS:CC_NEGS + N] if sample else cst[:, CC_NEGP:CC_NEGP + N]
                if not sample:
                    eng.wait_ge(gd_rows, lin(64, 64, n))
                    eng.wait_ge(gd_out, lin(16, 16, n))
                eng.tensor_tensor(sq(d_de), GBC[0:N], neg.unsqueeze(1).to_broadcast([N, H, N]), ALU.add).then_inc(*dve_.step("ga"))
                slot()
                eng.wait_ge(*act_.after("de3", n))
                eng.wait_ge(*pe_.after("kkqk", n))
                eng.tensor_tensor(sq(d_lt), sq(M[2]), sq(d_de), ALU.mult).then_inc(*dve_.step("lt"))
                eng.wait_ge(*dve_.after("lt", n))
                eng.tensor_tensor(sq(d_lt), sq(d_lt), BBC[0:N], ALU.mult).then_inc(*dve_.step("lb"))
                eng.wait_ge(*dve_.after("lb", n))
                eng.tensor_tensor(sq(d_tt), sq(d_lt), cst[0:N, CC_LEV:CC_LEV + N].unsqueeze(1).to_broadcast([N, H, N]), ALU.mult).then_inc(*dve_.step("m0"))
                eng.wait_ge(*dve_.after("m0", n))
                eng.tensor_tensor(sq(d_tt), cst[0:N, CC_ID:CC_ID + N].unsqueeze(1).to_broadcast([N, H, N]), sq(d_tt),
                                  ALU.subtract).then_inc(inv0, 1)
                eng.wait_ge(*pe_.after("vk", n))
                eng.tensor_tensor(tk(d_vb), tk(M[4]), tokc[0:N, TOK_BETA, :].unsqueeze(2).to_broadcast([N, H, HD]), ALU.mult).then_inc(*dve_.step("vb"))
                eng.tensor_tensor(tk(d_kd), tk(M[5]), tokc[0:N, TOK_KD, :].unsqueeze(2).to_broadcast([N, H, HD]), ALU.mult).then_inc(*dve_.step("kd"))
                eng.tensor_tensor(sq(d_at), sq(M[3]), sq(d_de), ALU.mult).then_inc(*dve_.step("qkd"))
                slot()
                slot()
                eng.wait_ge(*pe_.after("kst" if sample else "ks", n))
                eng.wait_ge(*dve_.after("vb", n))
                eng.tensor_tensor(tk(d_r), tk(d_vb), tk(M[4]), ALU.subtract).then_inc(*dve_.step("r"))
                front(0)
                front(1)
                for j in range(1, J):
                    slot()
                    eng.wait_ge(*pe_.after(f"y{j}", n))
                    if j < J - 1:
                        eng.tensor_tensor(half(d_t, j, 0), half(d_t, j, 0), half(M[3], j, 0), ALU.subtract).then_inc(*dve_.step(f"tm{j}"))
                    eng.tensor_tensor(half(d_tt, j, 1), half(d_tt, j, 1), half(M[2], j, 1), ALU.subtract).then_inc(*dve_.step(f"tt{j}"))
                    if j in (1, 3):
                        front(2 if j == 1 else 3)
                    slot()
                slot()
                front(4)
                if not sample:
                    eng.wait_ge(*pe_.after("o", n))
                    eng.tensor_tensor(hn(d_S), hn(d_S), EGB[:, :, N - 1:N].to_broadcast([P, H, HD]), ALU.mult).then_inc(*dve_.step("s1"))
                    eng.wait_ge(*dve_.after("s1", n))
                    eng.wait_ge(*pe_.after("su", n))
                    eng.tensor_tensor(d_S[:, :], d_S[:, :], M[4][:, :], ALU.add).then_inc(*dve_.step("s2"))
                slot()
                eng.wait_ge(*act_.after("rr", n))
                eng.tensor_tensor(d_xs[:, 0:C4], M[5][:, 0:C4], d_t[:, 0:C4], ALU.mult).then_inc(*dve_.step("y1"))
                eng.wait_ge(*dve_.after("y1", n))
                eng.tensor_tensor(d_xs[:, 0:C4], d_xs[:, 0:C4], d_pb[:, 2 * C4:3 * C4], ALU.mult).then_inc(*dve_.step("y2"))
                slot()
                if sample:
                    sample_states(*states)
                slot()
            if kind == "pool":
                slot()
                slot()
                eng.wait_ge(*dve_.after("kn", n))
                if not sample:
                    eng.wait_ge(gd_rows, lin(64, 64, n))
                eng.tensor_tensor(hn(d_pb, 0), hn(d_qk, C4), BEGB, ALU.mult).then_inc(*pool_.step("kb"))
                eng.tensor_tensor(hn(d_pb, C4), hn(d_qk, 0), EGB, ALU.mult).then_inc(*pool_.step("qg"))
                eng.tensor_tensor(d_pb[:, 2 * C4:3 * C4], d_cv[:, 3 * C4:4 * C4], prm[:, PC_GDN:PC_GDN + 1].to_broadcast([P, C4]),
                                  ALU.mult).then_inc(*pool_.step("zw"))
                slot()
                eng.wait_ge(*dve_.after("lb", n))
                for j in range(1, J):
                    eng.tensor_tensor(sq(d_mt, None, j * N4), sq(d_lt), cst[0:N, CC_LEV + j * P:CC_LEV + j * P + N].unsqueeze(1).to_broadcast([N, H, N]),
                                      ALU.mult).then_inc(*pool_.step(f"mt{j}"))
                slot()
                slot()
                front()
                for _ in range(2 * (J - 1) + 3):
                    slot()
                if sample:
                    sample_states(*states)
                slot()
            if kind == "act":
                slot()
                slot()
                eng.wait_ge(*pe_.after("nq", n))
                eng.activation(d_pb[:, 0:C4], M[0][:, 0:C4], ACT.Ln, bias=EPS).then_inc(*act_.step("lq"))
                eng.activation(d_pb[:, C4:2 * C4], M[1][:, 0:C4], ACT.Ln, bias=EPS).then_inc(*act_.step("lk"))
                eng.wait_ge(*act_.after("lq", n))
                eng.activation(d_pb[:, 0:C4], d_pb[:, 0:C4], ACT.Exp, scale=-0.5, bias=-0.5 * math.log(HD)).then_inc(*act_.step("rq"))
                eng.wait_ge(*act_.after("lk", n))
                eng.activation(d_pb[:, C4:2 * C4], d_pb[:, C4:2 * C4], ACT.Exp, scale=-0.5).then_inc(*act_.step("rk"))
                eng.wait_ge(*dve_.after("ga", n))
                for h in range(H):
                    eng.activation(sq(d_de, h), sq(d_de, h), ACT.Exp, bias=tokc[0:N, TOK_NG, h:h + 1]).then_inc(*act_.step(f"de{h}"))
                slot()
                if sample:
                    eng.wait_ge(*pe_.after("ks"))
                    eng.activation(d_pa[:, 0:C4], M[0][:, 0:C4], ACT.Copy).then_inc(*act_.step("kst"))
                slot()
                eng.wait_ge(*pe_.after("tr", n))
                eng.activation(sq(d_t), sq(M[0]), ACT.Copy).then_inc(*act_.step("tr"))
                slot()
                eng.wait_ge(*dve_.after("qkd", n))
                for j in range(1, J):
                    eng.wait_ge(*pe_.after(f"x{j}", n))
                    eng.activation(sq(d_xs), sq(M[1]), ACT.Copy).then_inc(*act_.step(f"x{j}"))
                    if j >= 4:
                        front(j - 4)
                    slot()
                    slot()
                eng.wait_ge(*pe_.after("vn", n))
                eng.activation(d_vn[0:N, :], M[1][0:N, :], ACT.Copy).then_inc(*act_.step("vn"))
                front(3)
                slot()
                eng.wait_ge(*pe_.after("o", n))
                eng.activation(d_t[:, 0:C4], M[5][:, 0:C4], ACT.Square).then_inc(*act_.step("sq2"))
                eng.wait_ge(*pe_.after("ss", n))
                eng.activation(d_t[:, 0:C4], M[0][:, 0:C4], ACT.Ln, bias=EPS, scale=1.0 / HD).then_inc(*act_.step("rl"))
                eng.wait_ge(*act_.after("rl", n))
                eng.activation(d_t[:, 0:C4], d_t[:, 0:C4], ACT.Exp, scale=-0.5).then_inc(*act_.step("rr"))
                slot()
                eng.wait_ge(*dve_.after("y2", n))
                eng.dma_start(ycols(GD, col0, N), hn(d_xs)).then_inc(gx_st if sample else gd_out, 16)
                slot()
                slot()
            if kind == "pe":
                slot()
                eng.wait_ge(*af.after("sq", n))
                for q in range(2):
                    i = eng.matmul(M[q][:, 0:C4], ones, squares[:, q * C4:(q + 1) * C4], start=True, stop=True)
                i.then_inc(*pe_.step("nq"))
                slot()
                eng.wait_ge(*dve_.after("kn", n))
                for h in range(H):
                    for q in range(2):
                        i = eng.matmul(M[2 + q][0:N, h * N:(h + 1) * N], hn(d_qk, C4)[:, h, :], hn(d_qk, (1 - q) * C4)[:, h, :], start=True, stop=True)
                i.then_inc(*pe_.step("kkqk"))
                for h in range(H):
                    eng.transpose(M[4][0:N, h * HD:(h + 1) * HD], hn(d_cv, 2 * C4)[:, h, :], ident)
                    i = eng.transpose(M[5][0:N, h * HD:(h + 1) * HD], hn(d_qk, C4)[:, h, :], ident)
                i.then_inc(*pe_.step("vk"))
                slot()
                eng.wait_ge(*pool_.after("kb", n))
                if sample:
                    eng.wait_ge(gxs_ld, 16)
                    for h in range(H):
                        for b in range(DEC_BATCH):
                            c = h * N + b * DEC_SEQ
                            i = eng.matmul(M[0][:, c:c + DEC_SEQ], d_Ss[:, b, h, :], d_pb[:, c:c + DEC_SEQ], start=True, stop=True)
                    i.then_inc(*pe_.step("ks"))
                    eng.wait_ge(*act_.after("kst"))
                    eng.wait_ge(*dve_.after("vb"))
                    for h in range(H):
                        i = eng.transpose(M[4][0:N, h * HD:(h + 1) * HD], d_pa[:, h * N:(h + 1) * N], ident)
                    i.then_inc(*pe_.step("kst"))
                else:
                    eng.wait_ge(*dve_.after("vb", n))
                    for h in range(H):
                        i = eng.matmul(M[4][0:N, h * HD:(h + 1) * HD], d_pb[:, h * N:(h + 1) * N], d_S[:, h * HD:(h + 1) * HD], start=True, stop=True)
                    i.then_inc(*pe_.step("ks"))
                slot()
                eng.wait_ge(inv0, NCH + 1 if sample else lin(1, 1, n))
                for h in range(H):
                    i = eng.transpose(sq(M[0], h), sq(d_tt, h), ident[0:N, 0:N])
                i.then_inc(*pe_.step("tr"))
                slot()
                for j in range(1, J):
                    eng.wait_ge(*pool_.after(f"mt{j}", n))
                    if j == 1:
                        eng.wait_ge(*act_.after("tr", n))
                    else:
                        eng.wait_ge(*dve_.after(f"tm{j - 1}", n))
                    for h in range(H):
                        i = eng.matmul(sq(M[1], h), sq(d_mt, h, j * N4), sq(d_t, h), start=True, stop=True)
                    i.then_inc(*pe_.step(f"x{j}"))
                    slot()
                    eng.wait_ge(*act_.after(f"x{j}", n))
                    if j > 1:
                        eng.wait_ge(*dve_.after(f"tt{j - 1}", n))
                    for h in range(H):
                        i = eng.matmul(half(M[2], j, 1, h), sq(d_xs, h), half(d_tt, j, 1, h), start=True, stop=True)
                    if j < J - 1:
                        for h in range(H):
                            i = eng.matmul(half(M[3], j, 0, h), sq(d_tt, h), half(d_xs, j, 0, h), start=True, stop=True)
                    i.then_inc(*pe_.step(f"y{j}"))
                    slot()
                eng.wait_ge(*dve_.after(f"tt{J - 1}", n))
                eng.wait_ge(*dve_.after("r", n))
                for h in range(H):
                    i = eng.matmul(M[1][0:N, h * HD:(h + 1) * HD], sq(d_tt, h), tk(d_r, h), start=True, stop=True)
                i.then_inc(*pe_.step("vn"))
                slot()
                eng.wait_ge(*act_.after("vn", n))
                eng.wait_ge(*pool_.after("qg", n))
                for h in range(H):
                    i = eng.matmul(M[5][:, h * N:(h + 1) * N], tk(d_vn, h), sq(d_at, h), start=(not sample or h == 0), stop=False, skip_group_check=sample)
                    if sample:
                        for b in range(DEC_BATCH):
                            c = h * N + b * DEC_SEQ
                            i = eng.matmul(M[5][:, c:c + DEC_SEQ], d_Ss[:, b, h, :], d_pb[:, C4 + c:C4 + c + DEC_SEQ],
                                           start=False, stop=(h == H - 1 and b == DEC_BATCH - 1), skip_group_check=True)
                    else:
                        i = eng.matmul(M[5][:, h * N:(h + 1) * N], d_S[:, h * HD:(h + 1) * HD], d_pb[:, C4 + h * N:C4 + (h + 1) * N],
                                       start=False, stop=True)
                i.then_inc(*pe_.step("o"))
                if not sample:
                    for h in range(H):
                        i = eng.matmul(M[4][:, h * HD:(h + 1) * HD], tk(d_kd, h), tk(d_vn, h), start=True, stop=True)
                    i.then_inc(*pe_.step("su"))
                eng.wait_ge(*act_.after("sq2", n))
                i = eng.matmul(M[0][:, 0:C4], ones, d_t[:, 0:C4], start=True, stop=True)
                i.then_inc(*pe_.step("ss"))
                slot()
                if sample:
                    eng.wait_ge(*act_.after("rl"))
                    sample_states(*states)
                slot()
                slot()
        ml_in, ml_out = sem("ml_in"), sem("ml_out")
        mx_in, mx_st = sem("mx_in"), sem("mx_st")
        ml_pe = steps("ml_pe", "vt kq kt num den kv kn ss", credit=1)
        ml_act = steps("ml_act", "ks e0 e1 e2 e3 s1 s2 s3 vt sq rl rr", credit=1)
        ml_dve = steps("ml_dve", "tc ga cl qw qn pt qp kt dn dm rd h c1 n1 c2 n2 y1 y2", credit=1)
        ml_pool = steps("ml_pool", "gw", credit=1)
        mx_pe = steps("mx_pe", "vt kq kt num den kn ss " + " ".join(f"kv{h}" for h in range(H)))
        mx_act = steps("mx_act", "ks e0 e1 e2 e3 s1 s2 s3 vt sq rl rr")
        mx_dve = steps("mx_dve", "tc ga cl qw qn pt kt dn dm rd h y1 y2 n1 n2 " + STATE_STEPS)
        mx_pool = steps("mx_pool", "gw" + DECAY_STEPS)

        def mlstm(kind, eng, n, slot, sample):
            N = NS if sample else CH
            C4 = H * N
            pe_, act_, dve_, pool_ = (mx_pe, mx_act, mx_dve, mx_pool) if sample else (ml_pe, ml_act, ml_dve, ml_pool)
            col0 = SEQ if sample else None if n is None else n * CH

            def hn(x, o=0):
                return x[:, o:o + C4].rearrange("p (h n) -> p h n", n=N)

            def sq(x, h=None):
                v = x[0:N, 0:C4].rearrange("p (h n) -> p h n", n=N)
                return v if h is None else v[:, h, :]

            def tk(x, h=None):
                v = x[0:N, :].rearrange("p (h n) -> p h n", n=HD)
                return v if h is None else v[:, h, :]

            if kind == "sp":
                sm = mx_in if sample else ml_in
                if sample:
                    for s in (ml_pe, ml_act, ml_dve, ml_pool):
                        eng.wait_ge(*s.all_of(NCH))
                    eng.wait_ge(ml_out, 16 * (NCH + 1))
                else:
                    n, col0 = next_chunk(n)
                    prefetch(eng, n, (dve_, "qw"))
                    prefetch(eng, n, (pe_, "kq"))
                for k in range(4):
                    eng.dma_start(hn(m_in, k * C4), pcols(ML_TILE + 4 * k, 4, lin(HALO, 1, col0), N)).then_inc(sm, 16)
                if not sample:
                    slot()
                    prefetch(eng, n, (dve_, "n1"))
                for k, q in enumerate((ROW_U, ROW_ELW, ROW_EM)):
                    eng.dma_start(hn(m_bc, k * C4), rowd[q:q + 1][:, :, bass.ds(col0, N)].rearrange("a h t -> (a h) t").unsqueeze(0).to_broadcast([P, H, N])).then_inc(sm, 16)
                if sample:
                    eng.wait_ge(states_out, 16 * 2)
                    eng.dma_start(m_Ns[:, :, :].rearrange("p b h -> p (b h)"), st_mn).then_inc(mxs_ld, 16)
                    eng.dma_start(flat_bh(m_Cs), of_state(st_ml)).then_inc(mxs_ld, 16)
                return
            states = (kind, eng, (mx_pe, mx_dve, mx_pool), "kv", "num", m_Cs,
                      lambda h: m_bc[:, C4 + h * N + DEC_SEQ - 1:C4 + (h + 1) * N:DEC_SEQ], m_vt, m_vx, m_kt, ((2, 3), (5, 0)))
            loaded = (mx_in, 112) if sample else None if n is None else (ml_in, lin(112, 112, n))
            if not sample:
                after_chunks(eng, n, [x for k, x in (("pe", pe_), ("act", act_), ("dve", dve_), ("pool", pool_)) if k != kind], ml_out if kind == "dve" else None)
            UB, ELW, EM = (hn(m_bc, k * C4) for k in range(3))
            if kind == "dve":
                eng.wait_ge(*loaded)
                if sample:
                    eng.wait_ge(*ml_dve.all_of(NCH))
                    eng.tensor_copy(m_no[:, :], m_N[:, :]).then_inc(n_out, 1)
                tok_at = tok[:, :, NCH, :] if sample else tok[:, :, bass.ds(n, 1), :].squeeze(2)
                eng.tensor_scalar(tokc[0:N, :, :], tok_at[0:N], 0.0, None, ALU.add).then_inc(*dve_.step("tc"))
                neg = cst[0:N, CC_NEGS:CC_NEGS + N] if sample else cst[:, CC_NEGP:CC_NEGP + N]
                eng.tensor_tensor(sq(m_e), UB[0:N], neg.unsqueeze(1).to_broadcast([N, H, N]), ALU.add).then_inc(*dve_.step("ga"))
                eng.tensor_scalar(m_so[:, 0:C4], m_in[:, 3 * C4:4 * C4], CLAMP, None, ALU.max).then_inc(*dve_.step("cl"))
                eng.tensor_tensor(m_qw[:, 0:C4], m_in[:, 0:C4], m_bc[:, C4:2 * C4], ALU.mult).then_inc(*dve_.step("qw"))
                eng.wait_ge(*dve_.after("qw", n))
                if sample:
                    eng.wait_ge(mxs_ld, 32)
                    eng.tensor_tensor(m_qn[:, 0:C4].rearrange("p (h b c) -> p h b c", b=DEC_BATCH, c=DEC_SEQ),
                                      m_qw[:, 0:C4].rearrange("p (h b c) -> p h b c", b=DEC_BATCH, c=DEC_SEQ),
                                      m_Ns[:, :, :].rearrange("p b h -> p h b").unsqueeze(3).to_broadcast([P, H, DEC_BATCH, DEC_SEQ]),
                                      ALU.mult).then_inc(*dve_.step("qn"))
                else:
                    eng.tensor_tensor(hn(m_qn), hn(m_qw), m_N[:, :].unsqueeze(2).to_broadcast([P, H, N]), ALU.mult).then_inc(*dve_.step("qn"))
                slot()
                eng.wait_ge(*act_.after("e3", n))
                eng.wait_ge(*pe_.after("kq", n))
                eng.tensor_tensor(sq(m_pt), sq(M[0]), sq(m_e), ALU.mult).then_inc(*dve_.step("pt"))
                if not sample:
                    eng.wait_ge(*dve_.after("pt", n))
                    eng.tensor_tensor(m_qn[:, :], m_qn[:, :], m_pt[:, :], ALU.add).then_inc(*dve_.step("qp"))
                eng.wait_ge(*pe_.after("kt", n))
                eng.tensor_tensor(tk(m_kt), tk(M[4]), tokc[0:N, TOK_EWS, :].unsqueeze(2).to_broadcast([N, H, HD]), ALU.mult).then_inc(*dve_.step("kt"))
                slot()
                eng.wait_ge(*pe_.after("den", n))
                eng.tensor_tensor(m_dn[:, 0:C4], M[2][:, 0:C4], m_bc[:, 2 * C4:3 * C4], ALU.max).then_inc(*dve_.step("dn"))
                eng.wait_ge(*dve_.after("dn", n))
                eng.scalar_tensor_tensor(m_dn[:, 0:C4], M[2][:, 0:C4], -1.0, m_dn[:, 0:C4], ALU.mult, ALU.max).then_inc(*dve_.step("dm"))
                eng.wait_ge(*dve_.after("dm", n))
                eng.reciprocal(m_rd[:, 0:C4], m_dn[:, 0:C4]).then_inc(*dve_.step("rd"))
                eng.wait_ge(*dve_.after("rd", n))
                eng.tensor_tensor(m_h[:, 0:C4], M[1][:, 0:C4], m_rd[:, 0:C4], ALU.mult).then_inc(*dve_.step("h"))
                slot()
                if not sample:
                    last = ELW[:, :, N - 1:N]
                    eng.tensor_tensor(hn(m_C), hn(m_C), last.to_broadcast([P, H, HD]), ALU.mult).then_inc(*dve_.step("c1"))
                    eng.tensor_tensor(m_N[:, :], m_N[:, :], last.squeeze(2), ALU.mult).then_inc(*dve_.step("n1"))
                    eng.wait_ge(*dve_.after("n1", n))
                    eng.wait_ge(*pe_.after("kn", n))
                    eng.tensor_tensor(m_C[:, :], m_C[:, :], M[3][:, :], ALU.add).then_inc(*dve_.step("c2"))
                    eng.tensor_tensor(m_N[:, :], m_N[:, :], M[0][:, 0:H], ALU.add).then_inc(*dve_.step("n2"))
                slot()
                eng.wait_ge(*act_.after("rr", n))
                eng.tensor_tensor(m_y[:, 0:C4], m_h[:, 0:C4], m_sq[:, 0:C4], ALU.mult).then_inc(*dve_.step("y1"))
                eng.wait_ge(*dve_.after("y1", n))
                eng.wait_ge(*pool_.after("gw", n))
                eng.tensor_tensor(m_y[:, 0:C4], m_y[:, 0:C4], m_gw[:, 0:C4], ALU.mult).then_inc(*dve_.step("y2"))
                slot()
                if sample:
                    ends = m_bc[:, C4:2 * C4].rearrange("p (h b c) -> p b h c", b=DEC_BATCH, c=DEC_SEQ)[:, :, :, DEC_SEQ - 1]
                    eng.tensor_tensor(m_Ns[:, :, :], m_Ns[:, :, :], ends, ALU.mult).then_inc(*dve_.step("n1"))
                    eng.wait_ge(*dve_.after("n1"))
                    eng.tensor_tensor(m_Ns[:, :, :], m_Ns[:, :, :], M[0][:, 0:H * DEC_BATCH].rearrange("p (h b) -> p b h", b=DEC_BATCH),
                                      ALU.add).then_inc(*dve_.step("n2"))
                    sample_states(*states)
                slot()
            if kind == "pool":
                eng.wait_ge(*act_.after("s3", n))
                eng.tensor_tensor(hn(m_gw), hn(m_so), prm[:, PC_MLN:PC_MLN + H].unsqueeze(2).to_broadcast([P, H, N]), ALU.mult).then_inc(*pool_.step("gw"))
                for _ in range(5):
                    slot()
                if sample:
                    sample_states(*states)
                slot()
            if kind == "act":
                eng.wait_ge(*loaded)
                eng.activation(m_ks[:, 0:C4], m_in[:, C4:2 * C4], ACT.Copy, scale=HD ** -0.5).then_inc(*act_.step("ks"))
                eng.wait_ge(*dve_.after("ga", n))
                for h in range(H):
                    eng.activation(sq(m_e, h), sq(m_e, h), ACT.Exp, bias=tokc[0:N, TOK_W, h:h + 1]).then_inc(*act_.step(f"e{h}"))
                eng.wait_ge(*dve_.after("cl", n))
                eng.activation(m_so[:, 0:C4], m_so[:, 0:C4], ACT.Exp, scale=-1.0).then_inc(*act_.step("s1"))
                eng.wait_ge(*act_.after("s1", n))
                eng.activation(m_so[:, 0:C4], m_so[:, 0:C4], ACT.Ln, bias=1.0).then_inc(*act_.step("s2"))
                eng.wait_ge(*act_.after("s2", n))
                eng.activation(m_so[:, 0:C4], m_so[:, 0:C4], ACT.Exp, scale=-1.0).then_inc(*act_.step("s3"))
                slot()
                eng.wait_ge(*pe_.after("vt", n))
                eng.activation(m_vt[0:N, :], M[5][0:N, :], ACT.Copy).then_inc(*act_.step("vt"))
                slot()
                eng.wait_ge(*dve_.after("h", n))
                eng.activation(m_sq[:, 0:C4], m_h[:, 0:C4], ACT.Square).then_inc(*act_.step("sq"))
                slot()
                eng.wait_ge(*pe_.after("ss", n))
                eng.activation(m_sq[:, 0:C4], M[4][:, 0:C4], ACT.Ln, bias=EPS, scale=1.0 / HD).then_inc(*act_.step("rl"))
                eng.wait_ge(*act_.after("rl", n))
                eng.activation(m_sq[:, 0:C4], m_sq[:, 0:C4], ACT.Exp, scale=-0.5).then_inc(*act_.step("rr"))
                slot()
                eng.wait_ge(*dve_.after("y2", n))
                eng.dma_start(ycols(ML, col0, N), hn(m_y)).then_inc(mx_st if sample else ml_out, 16)
                slot()
                slot()
            if kind == "pe":
                eng.wait_ge(*loaded)
                for h in range(H):
                    i = eng.transpose(M[5][0:N, h * HD:(h + 1) * HD], hn(m_in, 2 * C4)[:, h, :], ident)
                i.then_inc(*pe_.step("vt"))
                slot()
                eng.wait_ge(*act_.after("ks", n))
                for h in range(H):
                    i = eng.matmul(sq(M[0], h), hn(m_ks)[:, h, :], hn(m_in)[:, h, :], start=True, stop=True)
                i.then_inc(*pe_.step("kq"))
                for h in range(H):
                    i = eng.transpose(M[4][0:N, h * HD:(h + 1) * HD], hn(m_ks)[:, h, :], ident)
                i.then_inc(*pe_.step("kt"))
                slot()
                eng.wait_ge(*dve_.after("kt", n))
                eng.wait_ge(*act_.after("vt", n))
                if sample:
                    eng.wait_ge(mxs_ld, 32)
                for h in range(H):
                    i = eng.matmul(M[1][:, h * N:(h + 1) * N], tk(m_vt, h), sq(m_pt, h), start=(not sample or h == 0), stop=False, skip_group_check=sample)
                    if sample:
                        for b in range(DEC_BATCH):
                            c = h * N + b * DEC_SEQ
                            i = eng.matmul(M[1][:, c:c + DEC_SEQ], m_Cs[:, b, h, :], m_qw[:, c:c + DEC_SEQ],
                                           start=False, stop=(h == H - 1 and b == DEC_BATCH - 1), skip_group_check=True)
                    else:
                        i = eng.matmul(M[1][:, h * N:(h + 1) * N], m_C[:, h * HD:(h + 1) * HD], m_qw[:, h * N:(h + 1) * N],
                                       start=False, stop=True)
                i.then_inc(*pe_.step("num"))
                if sample:
                    eng.matmul(M[2][:, 0:C4], cst[0:N, CC_ONE:CC_ONE + P], m_pt[0:N, 0:C4], start=True, stop=False)
                    i = eng.matmul(M[2][:, 0:C4], ones, m_qn[:, 0:C4], start=False, stop=True)
                else:
                    i = eng.matmul(M[2][:, :], ones, m_qn[:, :], start=True, stop=True)
                i.then_inc(*pe_.step("den"))
                if sample:
                    for h in range(H):
                        i = eng.matmul(M[0][:, h * DEC_BATCH:(h + 1) * DEC_BATCH], tk(m_kt, h), cst[0:NS, CC_IND:CC_IND + DEC_BATCH],
                                       start=True, stop=True)
                    i.then_inc(*pe_.step("kn"))
                else:
                    for h in range(H):
                        i = eng.matmul(M[3][:, h * HD:(h + 1) * HD], tk(m_kt, h), tk(m_vt, h), start=True, stop=True)
                    i.then_inc(*pe_.step("kv"))
                    for h in range(H):
                        i = eng.matmul(M[0][:, h:h + 1], tk(m_kt, h), ones[:, 0:1], start=True, stop=True)
                    i.then_inc(*pe_.step("kn"))
                slot()
                eng.wait_ge(*act_.after("sq", n))
                i = eng.matmul(M[4][:, 0:C4], ones, m_sq[:, 0:C4], start=True, stop=True)
                i.then_inc(*pe_.step("ss"))
                slot()
                slot()
                if sample:
                    sample_states(*states)
                slot()

        sums = " ".join(f"q{k}" for k in range(KT))
        roots = " ".join(f"l{g} r{g}" for g in range(TG))
        PIECES = [(g, k) for g in range(TG) for k in range(KT)]
        nm_act = {w: steps(f"nm{w}_act", f"{sums} {roots}" + ("" if w == "3" else " " + " ".join(f"h{i}" for i in range(TG * KT)))) for w in "123"}
        lows = "s0 " + " ".join(f"s{i + 1} l{i}" for i in range(TG * KT - 1)) + f" l{TG * KT - 1}"
        nm_dve = {w: steps(f"nm{w}_dve", " ".join(f"a{k}" for k in range(KT)) + " " + (" ".join(f"s{k}" for k in range(KT)) if w == "3" else lows))
                  for w in "123"}
        nm_pe = {w: steps(f"nm{w}_pe", " ".join(f"s{g}" for g in range(TG))) for w in "123"}

        def norm_sum(kind, eng, which, x, sqs, total, k, ready=None):
            act_, dve_ = nm_act[which], nm_dve[which]
            if kind == "act":
                ready(eng, k)
                if k >= 2:
                    eng.wait_ge(*dve_.after(f"a{k - 2}"))
                eng.activation(sqs[k % 2], x[:, k, :], ACT.Square).then_inc(*act_.step(f"q{k}"))
            if kind == "dve":
                eng.wait_ge(*act_.after(f"q{k}"))
                if k == 0:
                    eng.tensor_copy(total, sqs[0]).then_inc(*dve_.step("a0"))
                else:
                    eng.wait_ge(*dve_.after(f"a{k - 1}"))
                    eng.tensor_tensor(total, total, sqs[k % 2], ALU.add).then_inc(*dve_.step(f"a{k}"))

        def norm_scale(kind, eng, which, x, total, rs, tmp, col):
            act_, dve_, pe_ = nm_act[which], nm_dve[which], nm_pe[which]

            def cols(g):
                return slice(g * GN, (g + 1) * GN)

            def piece(i):
                return tmp[i % 2][:, cols(i // 2 % TG)]

            if kind == "act":
                for g in range(TG):
                    eng.wait_ge(*pe_.after(f"s{g}"))
                    eng.activation(rs[:, cols(g)], M[g][:, 0:GN], ACT.Ln, bias=EPS, scale=1.0 / D_MODEL).then_inc(*act_.step(f"l{g}"))
                    eng.wait_ge(*act_.after(f"l{g}"))
                    eng.activation(rs[:, cols(g)], rs[:, cols(g)], ACT.Exp, scale=-0.5).then_inc(*act_.step(f"r{g}"))
                for i, (g, k) in enumerate(PIECES if which != "3" else ()):
                    eng.wait_ge(*dve_.after(f"s{i}"))
                    eng.activation(xn_hi[:, k, cols(g)], piece(i), ACT.Copy).then_inc(*act_.step(f"h{i}"))
            if kind == "dve" and which == "3":
                eng.wait_ge(*act_.after(f"r{TG - 1}"))
                for k in range(KT):
                    eng.scalar_tensor_tensor(x[:, k, :], x[:, k, :], prm[:, col + k:col + k + 1], rs, ALU.mult, ALU.mult).then_inc(*dve_.step(f"s{k}"))
            elif kind == "dve":
                def low(i):
                    g, k = PIECES[i]
                    eng.wait_ge(*act_.after(f"h{i}"))
                    eng.tensor_tensor(xn_lo[:, k, cols(g)], piece(i), xn_hi[:, k, cols(g)].bitcast(F32), ALU.subtract).then_inc(*dve_.step(f"l{i}"))

                for i, (g, k) in enumerate(PIECES):
                    if k == 0:
                        eng.wait_ge(*act_.after(f"r{g}"))
                    if i >= 6:
                        eng.wait_ge(*dve_.after(f"l{i - 6}"))
                    eng.scalar_tensor_tensor(piece(i), x[:, k, cols(g)], prm[:, col + k:col + k + 1], rs[:, cols(g)], ALU.mult, ALU.mult).then_inc(*dve_.step(f"s{i}"))
                    if i:
                        low(i - 1)
                low(TG * KT - 1)
            if kind == "pe":
                eng.wait_ge(*dve_.after(f"a{KT - 1}"))
                for g in range(TG):
                    eng.matmul(M[g][:, 0:GN], ones, total[:, cols(g)], start=True, stop=True).then_inc(*pe_.step(f"s{g}"))

        def normed(which, g):
            return nm_dve[which].after(f"l{(g + 1) * KT - 1}")

        ORDER = [HG, GD, ML]
        Y_AT = {HG: (y_hi[:, :, :], y_lo[:, :, :]), GD: (xn_hi[:, 0:4, :], xn_lo[:, 0:4, :]), ML: (y_hi[:, :, :], y_lo[:, :, :])}
        y_ld = [sem(f"y_ld{s}") for s in range(5)]
        resid_ld = [sem(f"resid_ld{s}") for s in range(3)]
        f_loaded = [sem(f"f_loaded{s}") for s in range(3)]
        y_high, y_low = sem("y_high"), sem("y_low")
        gate_ld = [sem(f"gate_ld{s}") for s in range(2)]
        gate_sig, merged = sem("gate_sig"), sem("merged")
        mg_hi, mg_lo = sem("mg_hi"), sem("mg_lo")
        f_relu, f_sq, f_hi, f_lo, f_acc = sem("f_relu"), sem("f_sq"), sem("f_hi"), sem("f_lo"), sem("f_acc")
        y_st = sem("y_st")
        mxs_ld, hss_ld, gxs_ld = sem("mxs_ld"), sem("hss_ld"), sem("gxs_ld")
        st_out, states_out = sem("st_out"), sem("states_out")
        ybuf = [e_a[:, :], e_b[:, :]] + [e_3[:, k, :] for k in range(3)]

        def split_y(kind, eng, j):
            b, k, buf = ORDER[j // 4], j % 4, j % 5
            if kind == "sp":
                if j == 0:
                    for s in (mx_pe, mx_act, mx_dve, mx_pool):
                        eng.wait_ge(*s.all_of(1))
                    for s_, v in ((hg_out, 16 * (NCH + 1)), (gd_out, 16 * (NCH + 1)), (ml_out, 16 * (NCH + 1)), (hs_st, 16), (gx_st, 16), (mx_st, 16)):
                        eng.wait_ge(s_, v)
                    eng.wait_ge(st_out, 16 * (1 + 2 + 4))
                if j >= 5:
                    eng.wait_ge(y_low, j - 4)
                eng.dma_start(ybuf[buf], yd[4 * b + k]).then_inc(y_ld[buf], 16)
            if kind == ("dve" if j < 4 else "act"):
                if j == 4 or j == 8:
                    eng.wait_ge(groups_done, TG * (NPROJ if j == 4 else MERGE0 + KT))
                eng.wait_ge(y_ld[buf], 16 * (j // 5 + 1))
                if j < 4:
                    eng.tensor_copy(Y_AT[b][0][:, k, :], ybuf[buf]).then_inc(y_high, 1)
                else:
                    eng.activation(Y_AT[b][0][:, k, :], ybuf[buf], ACT.Copy).then_inc(y_high, 1)
            if kind == "dve":
                eng.wait_ge(y_high, j + 1)
                eng.tensor_tensor(Y_AT[b][1][:, k, :], ybuf[buf], Y_AT[b][0][:, k, :].bitcast(F32), ALU.subtract).then_inc(y_low, 1)

        def split_merged(kind, eng, d):
            if kind == "act":
                eng.wait_ge(groups_done, TG * (MERGE0 + 16))
                eng.wait_ge(merged, TG * (16 + d + 1))
                eng.activation(xn_hi[:, d, :], acc[:, d, :], ACT.Copy).then_inc(mg_hi, 1)
            if kind == "dve":
                eng.wait_ge(mg_hi, d + 1)
                eng.tensor_tensor(xn_lo[:, d, :], acc[:, d, :], xn_hi[:, d, :].bitcast(F32), ALU.subtract).then_inc(mg_lo, 1)

        def merge_all(kind, eng):
            if kind == "sp":
                merge_pair("gates", eng, 0)
            for j in range(4 if kind != "sp" else 0):
                split_y(kind, eng, j)
            for j0 in range(0, 24, 2):
                if kind == "sp":
                    for s in range(2):
                        if j0 < 22:
                            load_w(eng, Tile(MERGE0 + j0 + 2 + s), w_half[j0 + 2 + s], 4)
                        else:
                            load_w(eng, Tile(OUT0 + s), w_full[s])
                    if j0 < 16:
                        split_y(kind, eng, 4 + j0 // 2)
                    if j0 < 22:
                        merge_pair("gates", eng, j0 + 2)
                    continue
                if kind == "pe" and j0 % KT == 0:
                    eng.wait_ge(y_low, 4 * (j0 // KT + 1))
                merge_pair(kind, eng, j0, 0, KT if j0 == 22 else 4)
                if j0 < 16:
                    split_y(kind, eng, 4 + j0 // 2)
                elif j0 > 16:
                    split_merged(kind, eng, j0 - 18)
                    split_merged(kind, eng, j0 - 17)
            for d in (KT - 2, KT - 1):
                split_merged(kind, eng, d)

        def merge_pair(kind, eng, j0, i=0, next_kt=4):
            nb = j0 // KT
            b = ORDER[nb]
            for s in range(2):
                t = Tile(MERGE0 + j0 + s, 2, i)
                j = lin(j0 + s, 2, i)
                d = lin(j0 % KT + s, 2, i)
                if kind == "gates":
                    if j0:
                        eng.wait_ge(merged, lin(TG * (j0 + s - 1), 2 * TG, i))
                    eng.dma_start(stage[:, s, :], proj[lin(GATE_TILE + KT * b + j0 % KT + s, 2, i), :, HALO:HALO + T]).then_inc(gate_ld[s], 16)
                if kind == "act":
                    make_hi(eng, t.next(), next_kt if s == 1 else 4)
                    eng.wait_ge(gate_ld[s], lin(16 * (j0 // 2 + 1), 16, i))
                    eng.activation(stage[:, s, :], stage[:, s, :], ACT.Sigmoid).then_inc(gate_sig, 1)
                if kind == "pool":
                    make_lo(eng, t.next(), next_kt if s == 1 else 4)
                if kind == "pe":
                    for g in range(TG):
                        dense(eng, t, g, None, 4, Y_AT[b])
                if kind == "dve":
                    eng.wait_ge(gate_sig, lin(j0 + s + 1, 2, i))
                    for g in range(TG):
                        cols = slice(g * GN, (g + 1) * GN)
                        eng.wait_ge(groups_done, t.number(TG, g + 1))
                        if nb == 0:
                            if j0 + s + g == 0:
                                eng.wait_ge(states_out, 16 * 3)
                            eng.tensor_tensor(acc[:, j0 % KT + s, cols], D[t.bank(g)][:, 0:GN], stage[:, s, cols], ALU.mult).then_inc(bank_free[t.bank(g)], 1)
                            eng.wait_ge(bank_free[t.bank(g)], t.bank_uses(g, 2))
                            eng.sem_inc(merged, 1)
                            continue
                        eng.tensor_tensor(e_c[:, cols], D[t.bank(g)][:, 0:GN], stage[:, s, cols], ALU.mult).then_inc(bank_free[t.bank(g)], 1)
                        eng.wait_ge(bank_free[t.bank(g)], t.bank_uses(g, 2))
                        if j0 + s + g:
                            eng.wait_ge(merged, lin(TG * (j0 + s) + g, 2 * TG, i))
                        a = acc[:, bass.ds(d, 1), cols].squeeze(1)
                        eng.tensor_tensor(a, a, e_c[:, cols], ALU.add).then_inc(merged, 1)

        def read_out(eng, t, groups=range(TG)):
            for g in groups:
                eng.wait_ge(bank_free[t.bank(g)], t.bank_uses(g, 2))

        def out_proj(kind, eng, d):
            t = Tile(OUT0 + d)
            if kind == "sp":
                if d >= 3:
                    read_out(eng, Tile(OUT0 + d - 3), (1, 2))
                else:
                    eng.wait_ge(y_low, 12)
                eng.dma_start(e_3[:, d % 3, :], xT[d]).then_inc(resid_ld[d % 3], 16)
                if d + 2 < KT:
                    load_w(eng, Tile(OUT0 + d + 2), w_full[d + 2])
            if kind == "act" and d < KT - 1:
                make_hi(eng, t.next())
            if kind == "pool":
                make_lo(eng, t.next())
            if kind == "pe":
                for g in range(TG):
                    dense(eng, t, g, None, before=(lambda g, k: eng.wait_ge(mg_lo, k + 1)) if d == 0 else None)
            if kind == "dve":
                eng.wait_ge(resid_ld[d % 3], 16 * (d // 3 + 1))
                for g in range(TG):
                    cols = slice(g * GN, (g + 1) * GN)
                    eng.wait_ge(groups_done, t.number(TG, g + 1))
                    eng.tensor_tensor(acc[:, d, cols], D[t.bank(g)][:, 0:GN], e_3[:, d % 3, cols], ALU.add).then_inc(bank_free[t.bank(g)], 1)
            for k in ([d - 1] if 0 < d else []) + ([d] if d == KT - 1 else []):
                norm_sum(kind, eng, "2", acc, (e_a[:, :], e_b[:, :]), e_c[:, :], k, lambda e, k: read_out(e, Tile(OUT0 + k), (1, 2)))
            if kind == "act" and d == KT - 1:
                make_hi(eng, t.next())

        def ffn_block(kind, eng, i, last):
            for m in range(FT + KT):
                t = Tile(FFN0 + m, FT + KT, i) if not isinstance(i, int) else Tile(FFN0 + m + (FT + KT) * i)
                kt, nkt = (KT, KT if m < FT - 1 else FT) if m < FT else (FT, FT if m < FT + KT - 1 else KT)
                more = not (last and m == FT + KT - 1)
                blk_groups = TG * FT
                if kind == "sp":
                    if m < FT:
                        load_f(eng, t, w_full[lin(KT + m, FT, i)])
                    else:
                        load_f(eng, t, w_half[lin(24 + m - FT, KT, i)], FT)
                if kind == "pool" and more:
                    make_lo(eng, t.next(), nkt)
                if kind == "act" and more:
                    make_hi(eng, t.next(), nkt)
                if kind == "pe":
                    for g in range(TG):
                        if m == 0:
                            eng.wait_ge(*normed("2", g))
                        if m == FT:
                            eng.wait_ge(f_lo, lin(blk_groups - TG + g + 3, blk_groups, i))
                        dense(eng, t, g, None, kt, None if m < FT else (y_hi, y_lo))
                if m == 0 and kind == "act":
                    eng.wait_ge(*normed("2", TG - 1))
                if m < FT and kind in ("act", "dve"):
                    for g in range(TG):
                        cols = slice(g * GN, (g + 1) * GN)
                        c = TG * m + g
                        u, v = (e_a, e_b) if c % 2 == 0 else (e_c, stage[:, 0, :])
                        u, v = u[:, cols], v[:, cols]
                        if kind == "act":
                            eng.wait_ge(f_lo, lin(c + 1, blk_groups, i))
                            eng.wait_ge(groups_done, t.number(TG, g + 1))
                            eng.activation(u, D[t.bank(g)][:, 0:GN], ACT.Relu).then_inc(bank_free[t.bank(g)], 1)
                            eng.wait_ge(bank_free[t.bank(g)], t.bank_uses(g, 2))
                            eng.activation(v, u, ACT.Square).then_inc(f_sq, 1)
                            eng.wait_ge(f_sq, lin(c + 1, blk_groups, i))
                            eng.activation(y_hi[:, m, cols], v, ACT.Copy).then_inc(f_hi, 1)
                        else:
                            eng.wait_ge(f_hi, lin(c + 1, blk_groups, i))
                            eng.tensor_tensor(y_lo[:, m, cols], v, y_hi[:, m, cols].bitcast(F32), ALU.subtract).then_inc(f_lo, 1)
                if m >= FT and kind == "dve":
                    for g in range(TG):
                        cols = slice(g * GN, (g + 1) * GN)
                        eng.wait_ge(groups_done, t.number(TG, g + 1))
                        eng.tensor_tensor(acc[:, m - FT, cols], acc[:, m - FT, cols], D[t.bank(g)][:, 0:GN], ALU.add).then_inc(bank_free[t.bank(g)], 1)
                if last and m >= FT and kind in ("act", "dve"):
                    if m == FT and kind == "act":
                        eng.wait_ge(f_lo, 2 + TG * FT * FB)
                    for k in ([m - FT - 1] if m > FT else []) + ([KT - 1] if m == FT + KT - 1 else []):
                        norm_sum(kind, eng, "3", acc, (e_a[:, :], e_b[:, :]), e_c[:, :], k,
                                 lambda e, k: read_out(e, Tile(FFN0 + FT + k + (FT + KT) * i), (1, 2)))

        ready, halo_st, n_out = sem("ready"), sem("halo_st"), sem("n_out")

        def of_state(x):
            return x.rearrange("b h k v -> k (b h) v")

        def flat_bh(x):
            return x[:, :, :, :].rearrange("k b h v -> k (b h) v")

        GD0 = GD_TILE
        SEG_ROW, SEG_HG = 2, 7
        LOOP_HG, LOOP_GD, LOOP_ML = GD0, GD0 + 19, GD0 + 38
        ROW_SLOTS, GX_SLOTS, ML_SLOTS = 6, 11, 6
        HG_SLOTS = [1, 4, 3, 3, 3, 2, 1, 1]
        GD_SLOTS = [0, 8, 5, 0, 2] + [2] * 10 + [2, 1] + [2, 2, 1, 0]
        chunk_credit = {("hg", "pe"): hg_pe.sem, ("hg", "act"): hg_act.sem, ("hg", "dve"): hg_dve.sem, ("hg", "pool"): hg_pool.sem, ("hg", "out"): hg_out,
                        ("gd", "pe"): gd_pe.sem, ("gd", "act"): gd_act.sem, ("gd", "dve"): gd_dve.sem, ("gd", "pool"): gd_pool.sem, ("gd", "out"): gd_out,
                        ("ml", "pe"): ml_pe.sem, ("ml", "act"): ml_act.sem, ("ml", "dve"): ml_dve.sem, ("ml", "pool"): ml_pool.sem, ("ml", "out"): ml_out}
        mixers = (("hg", hgrn, LOOP_HG, HG_SLOTS, HG_SLOTS[:-1] + [5], [1, 1, 1, 1, 1, 2, 1, 7] + [4, 3, 3, 2], 3),
                  ("gd", gdn, LOOP_GD, GD_SLOTS, GD_SLOTS[:-1] + [6], [3, 3, 3, 3] + [1] * 10 + [5], 3),
                  ("ml", mlstm, LOOP_ML, ML_SLOTS, ML_SLOTS, [3, 3, 3, 3, 2, 4], 2))

        def mix_program(kind, eng):
            f = Filler(kind, eng, Tile(0), SEG_ROW, 1)
            f.before = lambda g, k: eng.wait_ge(*normed("1", g)) if k == 0 else None
            f()
            f.done()
            f = Filler(kind, eng, Tile(SEG_ROW), SEG_HG - SEG_ROW, ROW_SLOTS)
            rows(kind, eng, f)
            f.done()
            if kind != "act":
                eng.wait_ge(masks_ld, 16)
            with eng.Fori(0, (GD0 - SEG_HG) // 2) as i:
                Filler(kind, eng, Tile(SEG_HG, 2, i), 2, 1)()
            carried = None
            for name, mixer, first, slots, slots_e, slots_s, tiles_s in mixers:
                if kind == "dve":
                    clear[name](eng)
                eng.sem_inc(chunk_credit[name, kind], 1)
                if kind == "act":
                    eng.sem_inc(chunk_credit[name, "out"], 16)
                f = Filler(kind, eng, Tile(first + 2 * NCH), tiles_s, slots_s, 4 if name == "ml" else KT)
                if fronts[name] is None:
                    with eng.Fori(0, NCH) as n:
                        g = Filler(kind, eng, Tile(first, 2, n), 2, slots)
                        mixer(kind, eng, n, g, False)
                        g.done()
                else:
                    fronts[name](kind, eng, False, carried)
                    if carried is not None:
                        carried.done()
                    if name == "gd" and kind in ("dve", "pool"):
                        eng.wait_ge(states_out, 16)
                    with eng.Fori(0, NCH - 1) as n:
                        g = Filler(kind, eng, Tile(first, 2, n), 2, slots)
                        mixer(kind, eng, n, g, False, True)
                        g.done()
                    g = Filler(kind, eng, Tile(first + 2 * (NCH - 1)), 2, slots_e)
                    mixer(kind, eng, NCH - 1, g, False)
                    g.done()
                    fronts[name](kind, eng, True, f)
                mixer(kind, eng, 0, f, True)
                if name == "hg":
                    carried = f
                else:
                    f.done()

        def whole_gdn_front(kind, eng, sample, slot):
            parts = {"dve": [(0, 1), (2, 3), (), (), (4,)], "act": [(), (0,), (1,), (2,), (3,)], "pool": [(), (0,), (), (), ()], "pe": [()] * 5}[kind]
            for at, some in enumerate(parts):
                for part in some:
                    gdn_front(kind, eng, 0, 0, part, sample)
                if at < 4:
                    slot()

        fronts = {"hg": lambda kind, eng, sample, slot: hgrn_front(kind, eng, 0, 0, sample), "gd": whole_gdn_front, "ml": None}

        def clear_hg(eng):
            for s in (rw_pe, rw_act, rw_dve):
                eng.wait_ge(*s.all_of(1))
            eng.wait_ge(rw_out, 16)
            eng.wait_ge(rw_mo, 32)
            eng.memset(g_S[:, :], 0.0).then_inc(ready, 1)
            eng.memset(g_kl[:, :], 0.0).then_inc(ready, 1)

        def clear_gd(eng):
            eng.wait_ge(st_out, 16 * 1)
            for s in (hs_pe, hs_act, hs_dve, hs_pool):
                eng.wait_ge(*s.all_of(1))
            eng.wait_ge(hs_st, 16)
            eng.memset(d_S[:, :], 0.0).then_inc(ready, 1)

        def clear_ml(eng):
            eng.wait_ge(st_out, 16 * 3)
            for s in (gx_pe, gx_act, gx_dve, gx_pool):
                eng.wait_ge(*s.all_of(1))
            eng.wait_ge(gx_st, 16)
            eng.memset(m_C[:, :], 0.0).then_inc(ready, 1)
            eng.memset(m_N[:, :], 0.0).then_inc(ready, 1)

        clear = {"hg": clear_hg, "gd": clear_gd, "ml": clear_ml}
        BANKS_BEFORE_FFN = TG * FFN0
        ALL_GROUPS = TG * (FFN0 + FB * (FT + KT))

        def evacuated_all(eng, n_groups):
            eng.wait_ge(bank_free[0], (n_groups + 1) // 2 + 1)
            eng.wait_ge(bank_free[1], n_groups // 2 + 1)

        def mixer_loads(sp, name, mixer, first, slots, slots_e, slots_s, tiles_s, after_first, after_sample):
            mixer("sp", sp, None, lambda: None, False)
            after_first()
            with sp.Fori(0, NCH - 1) as n:
                load_w(sp, Tile(first + 2, 2, n), w_proj[lin(first + 2, 2, n)])
                mixer("sp", sp, n, lambda: load_w(sp, Tile(first + 3, 2, n), w_proj[lin(first + 3, 2, n)]), False)
            for s in range(2):
                load_w(sp, Tile(first + 2 * NCH + s), w_proj[first + 2 * NCH + s])
            mixer("sp", sp, 0, None, True)
            after_sample()
            for t in range(first + 2 * NCH + 2, first + 2 * NCH + 2 + tiles_s):
                load_w(sp, Tile(t), w_proj[t] if t < NPROJ else w_half[t - MERGE0], KT if t < NPROJ else 4)

        block = ctx.enter_context(nc.Block())

        @block.sync
        def _(sp):
            sp.dma_start(prm[:, :], par).then_inc(const_ld, 16)
            sp.dma_start(cst[:, 0:CC_NEGP], con[:, 0:CC_NEGP]).then_inc(const_ld, 16)
            for k in range(KT):
                if k == KT // 2:
                    load_w(sp, Tile(0), w_proj[0])
                sp.dma_start(xin[:, k, :], xT[k]).then_inc(x_ld[k], 16)
            load_w(sp, Tile(1), w_proj[1])
            sp.dma_start(cst[:, CC_NEGP:], con[:, CC_NEGP:]).then_inc(masks_ld, 16)
            sp.wait_ge(ready, 1)
            sp.dma_start(proj[GD_TILE:GD_TILE + 12, :, 0:HALO].rearrange("t p c -> p t c"), halo0[:, :].rearrange("p (t c) -> p t c", c=HALO)).then_inc(halo_st, 16)
            load_w(sp, Tile(2), w_proj[2])
            sp.wait_ge(*nm_dve["1"].all_of(1))
            sp.wait_ge(*nm_act["1"].all_of(1))
            load_w(sp, Tile(3), w_proj[3])
            rows("sp", sp, None)
            for t in range(4, SEG_HG + 2):
                load_w(sp, Tile(t), w_proj[t])
            with sp.Fori(0, (GD0 - SEG_HG) // 2) as i:
                for s in range(2):
                    load_w(sp, Tile(SEG_HG + 2 + s, 2, i), w_proj[lin(SEG_HG + 2 + s, 2, i)])
            sp.wait_ge(halo_st, 16)
            sp.wait_ge(ready, 3)
            stored_all(sp, GD_TILE)

            def out(dst, src, done=st_out):
                sp.dma_start(dst, src).then_inc(done, 16)

            def heads(x):
                return x[:, :].rearrange("p (h v) -> p h v", v=HD)

            def out_p_H():
                sp.wait_ge(*hg_dve.all_of(NCH))
                out(p_H.rearrange("h k v -> k h v"), heads(g_S))

            def out_p_S():
                out(p_S.rearrange("h k v -> k h v"), heads(d_S))
                sp.wait_ge(*gxf_dve.after("sx3"))
                out(s_conv, d_ch[:, 12 * NS:12 * NS + 12 * DEC_BATCH * HALO])

            def out_p_C():
                out(p_conv, proj[GD_TILE:GD_TILE + 12, :, SEQ:SEQ + HALO])
                out(p_C.rearrange("h k v -> k h v"), heads(m_C))
                sp.wait_ge(n_out, 1)
                out(p_n, m_no[:, :])

            mixer_loads(sp, *mixers[0], lambda: None, out_p_H)
            sp.wait_ge(*hs_dve.all_of(1))
            sp.wait_ge(ready, 4)
            stored_all(sp, ML_TILE)
            mixer_loads(sp, *mixers[1], lambda: out(of_state(s_H), flat_bh(g_Ss), states_out), out_p_S)
            sp.wait_ge(*gx_dve.all_of(1))
            sp.wait_ge(ready, 6)
            stored_all(sp, GATE_TILE)
            mixer_loads(sp, *mixers[2], lambda: out(of_state(s_S), flat_bh(d_Ss), states_out), out_p_C)
            sp.wait_ge(*mx_dve.all_of(1))
            out(s_n, m_Ns[:, :, :].rearrange("p b h -> p (b h)"))
            for j in range(4):
                split_y("sp", sp, j)
            out(of_state(s_C), flat_bh(m_Cs), states_out)
            stored_all(sp, NPROJ)
            merge_all("sp", sp)
            for d in range(KT):
                out_proj("sp", sp, d)
            for d in range(KT - 3, KT):
                read_out(sp, Tile(OUT0 + d), (1, 2))
            with sp.Fori(0, FB) as i:
                ffn_block("sp", sp, i, False)
            for k in range(KT):
                sp.wait_ge(*nm_dve["3"].after(f"s{k}"))
                sp.dma_start(yT[k], acc[:, k, :]).then_inc(y_st, 16)
            sp.wait_ge(y_st, 16 * KT)

        @block.gpsimd
        def _(pool):
            pool.memset(halo0[:, :], 0.0).then_inc(ready, 1)
            make_lo(pool, Tile(0))
            mix_program("pool", pool)
            merge_all("pool", pool)
            for d in range(KT):
                out_proj("pool", pool, d)
            with pool.Fori(0, FB - 1) as i:
                ffn_block("pool", pool, i, False)
            ffn_block("pool", pool, FB - 1, True)

        @block.scalar
        def _(act):
            for b in range(2):
                act.sem_inc(bank_free[b], 1)
            act.preload_act_table_set("natural_log_exp_and_others")
            act.wait_ge(*lb_dve.after("d"))
            act.activation(lbt[:, 1, :], lbt[:, 0, :], ACT.Exp).then_inc(*lb_act.step("e"))
            for k in range(KT):
                if k == KT - 2:
                    make_hi(act, Tile(0))
                norm_sum("act", act, "1", xin, (nsq[:, :], ntmp[:, :]), stage[:, 0, :], k, lambda e, k: e.wait_ge(x_ld[k], 16))
            norm_scale("act", act, "1", xin, stage[:, 0, :], nrs[:, :], (nsq[:, :], ntmp[:, :]), PC_N1)
            mix_program("act", act)
            merge_all("act", act)
            act.preload_act_table_set("natural_log_exp_and_others")
            for d in range(KT):
                out_proj("act", act, d)
            norm_scale("act", act, "2", acc, e_c[:, :], stage[:, 0, :], (e_a[:, :], e_b[:, :]), PC_N2)
            with act.Fori(0, FB - 1) as i:
                ffn_block("act", act, i, False)
            ffn_block("act", act, FB - 1, True)
            norm_scale("act", act, "3", acc, e_c[:, :], stage[:, 0, :], None, PC_NF)

        @block.vector
        def _(dve):
            dve.wait_ge(const_ld, 32)
            logits = prm[:, PC_LB:PC_LB + H]
            dve.tensor_tensor(lbt[:, 0, :], logits, logits, ALU.subtract).then_inc(*lb_dve.step("d"))
            dve.wait_ge(*lb_act.after("e"))
            dve.reciprocal(lbt[:, 2, :], lbt[:, 1, :]).then_inc(*lb_dve.step("r"))
            dve.wait_ge(*lb_dve.after("r"))
            dve.tensor_tensor(lbt[:, 3, :], lbt[:, 1, :], lbt[:, 2, :], ALU.mult).then_inc(*lb_dve.step("n"))
            dve.wait_ge(*lb_dve.after("n"))
            dve.tensor_tensor(lbt[:, 4, :], lbt[:, 3, :], lbt[:, 3, :], ALU.subtract).then_inc(*lb_dve.step("lb"))
            dve.wait_ge(*lb_dve.after("lb"))
            dve.tensor_scalar(lbt[:, 5, :], lbt[:, 4, :], -1.0, 1.0, ALU.mult, ALU.add).then_inc(*lb_dve.step("om"))
            dve.wait_ge(*lb_dve.after("om"))
            for k in range(KT):
                norm_sum("dve", dve, "1", xin, (nsq[:, :], ntmp[:, :]), stage[:, 0, :], k)
            norm_scale("dve", dve, "1", xin, stage[:, 0, :], nrs[:, :], (nsq[:, :], ntmp[:, :]), PC_N1)
            mix_program("dve", dve)
            merge_all("dve", dve)
            for d in range(KT):
                out_proj("dve", dve, d)
            norm_scale("dve", dve, "2", acc, e_c[:, :], stage[:, 0, :], (e_a[:, :], e_b[:, :]), PC_N2)
            dve.sem_inc(f_lo, 2)
            with dve.Fori(0, FB - 1) as i:
                ffn_block("dve", dve, i, False)
            ffn_block("dve", dve, FB - 1, True)
            norm_scale("dve", dve, "3", acc, e_c[:, :], stage[:, 0, :], None, PC_NF)

        @block.tensor
        def _(pe):
            pe.wait_ge(const_ld, 32)
            norm_scale("pe", pe, "1", xin, stage[:, 0, :], None, None, PC_N1)
            mix_program("pe", pe)
            merge_all("pe", pe)
            for d in range(KT):
                out_proj("pe", pe, d)
            norm_scale("pe", pe, "2", acc, e_c[:, :], None, None, PC_N2)
            with pe.Fori(0, FB - 1) as i:
                ffn_block("pe", pe, i, False)
            ffn_block("pe", pe, FB - 1, True)
            norm_scale("pe", pe, "3", acc, e_c[:, :], None, None, PC_NF)


def constants():
    s, t = np.arange(P)[:, None], np.arange(P)[None, :]
    seq = np.arange(NS) // DEC_SEQ
    c = np.zeros((P, CC_ALL), np.float32)
    c[:, CC_ID:CC_ID + P] = s == t
    c[:, CC_ONE:CC_ONE + P] = 1
    c[:, CC_NEGP:CC_NEGP + P] = np.where(s <= t, 0, MASKED)
    c[:NS, CC_NEGS:CC_NEGS + NS] = np.where((s <= t)[:NS, :NS] & (seq[:, None] == seq[None, :]), 0, MASKED)
    for j, hf in enumerate(HALVES):
        lev = (s // (2 * hf) == t // (2 * hf)) & (s % (2 * hf) < hf) & (t % (2 * hf) >= hf)
        c[:, CC_LEV + j * P:CC_LEV + (j + 1) * P] = lev
        for n, at, rows_ in ((CH, CC_HGP, P), (NS, CC_HGS, NS)):
            if n == NS and j > 1:
                continue
            part = lev[:rows_, :n][:, np.arange(n) % (2 * hf) >= hf]
            w = H * n // 2
            c[:rows_, at + j * w:at + (j + 1) * w] = np.tile(part, (1, H))
    c[:, CC_SEGP:CC_SEGP + 512] = np.arange(512) % CH != 0
    c[:, CC_SEGS:CC_SEGS + 128] = np.arange(128) % DEC_SEQ != 0
    c[:NS, CC_IND:CC_IND + DEC_BATCH] = seq[:, None] == np.arange(DEC_BATCH)
    at = np.arange(T)
    row = np.where(at < SEQ, at % CH != 0, (at - SEQ) % DEC_SEQ != 0)
    return c, np.tile(row.astype(np.float32), (H, 1))


def tiles(w, k_tiles):
    n = w.shape[1] // P
    return w.reshape(k_tiles, P, n, P).transpose(2, 1, 0, 3).reshape(n, P, k_tiles * P)


def kernel(**inputs):
    import concourse.bacc as _bacc
    from concourse import mybir as _mybir
    from concourse.bass_utils import run_bass_kernel_spmd as _run

    a = {k: np.asarray(v) for k, v in inputs.items()}
    x = np.concatenate([a["x_prompt"].reshape(SEQ, D_MODEL), a["x_sample"].reshape(NS, D_MODEL)], 0)
    w = a["w_in"][0]
    cuts = np.cumsum([0] + [W_MIX] * 4 + [H] * 2 + [W_MIX] * 4 + [H] * 2 + [W_MIX] * 4 + [D_MODEL] * 3)
    (ml_q, ml_k, ml_v, ml_o, ml_i, ml_f, gd_q, gd_k, gd_v, gd_z, gd_b, gd_a, hg_q, hg_f, hg_i, hg_g, ga, gb, gc) = (
        w[:, p:q] for p, q in zip(cuts[:-1], cuts[1:]))
    gates = np.concatenate([ml_i, ml_f, gd_b, gd_a, np.zeros((D_MODEL, P - 4 * H), w.dtype)], 1)
    w_cols = np.concatenate([gates, hg_q, hg_f, hg_i, hg_g, gd_q, gd_k, gd_v, gd_z, ml_q, ml_k, ml_v, ml_o, ga, gb, gc], 1)
    w_proj = tiles(w_cols, KT)
    wb = a["w_branch"][0]
    half = [tiles(wb[b], 4) for b in (HG, GD, ML)]
    down = a["w_down"][0].reshape(FB, FT * P, D_MODEL)
    half += [tiles(down[f], FT) for f in range(FB)]
    w_half = np.concatenate(half, 0)
    w_full = np.concatenate([tiles(a["w_out"][0], KT), tiles(a["w_up"][0], KT)], 0)

    def col(v):
        return v.reshape(-1, P).T

    con, segrow = constants()
    conv_w = a["gd_conv_w"][0].reshape(CONV_W * 12, P).T
    par = np.concatenate([col(a["norm1_w"][0]), col(a["norm2_w"][0]), col(a["final_norm_w"]), col(a["ml_norm_w"][0]),
                          col(a["gd_norm_w"][0]), col(a["hg_norm_w"][0]), col(a["hg_lb_logits"][0]), conv_w], 1)
    rowpar = np.stack([a["ml_i_bias"][0], a["ml_f_bias"][0], a["gd_A_log"][0], a["gd_dt_bias"][0]], 1)
    conv0 = a["state_gdn_conv"][0].reshape(DEC_BATCH, HALO, 12, P).transpose(3, 2, 0, 1).reshape(P, -1)
    ins = {
        "xT": x.T.reshape(KT, P, T), "w_proj": w_proj, "w_half": w_half, "w_full": w_full, "par": par, "con": con,
        "rowpar": rowpar, "segrow": segrow, "m0": a["state_mlstm_m"][0].T, "conv0": conv0, "st_ml": a["state_mlstm_C"][0],
        "st_mn": a["state_mlstm_n"][0].reshape(DEC_BATCH * H, HD).T, "st_gd": a["state_gdn_S"][0], "st_hg": a["state_hgrn_S"][0],
    }
    outs = {
        "yT": (KT, P, T), "p_C": (H, HD, HD), "p_n": (P, H), "p_m": (H, 1), "p_S": (H, HD, HD), "p_conv": (12, P, HALO),
        "p_H": (H, HD, HD), "s_C": (DEC_BATCH, H, HD, HD), "s_n": (P, DEC_BATCH * H), "s_m": (H, DEC_BATCH),
        "s_S": (DEC_BATCH, H, HD, HD), "s_conv": (P, 12 * DEC_BATCH * HALO), "s_H": (DEC_BATCH, H, HD, HD),
    }
    nc = _bacc.Bacc("TRN2", target_bir_lowering=False, num_devices=1)
    arrays, aps = {}, {}
    for k, v in ins.items():
        arrays[f"in_{k}"] = np.ascontiguousarray(v)
        aps[k] = nc.dram_tensor(f"in_{k}", v.shape, _mybir.dt.from_np(v.dtype), kind="ExternalInput").ap()
    for k, shape in outs.items():
        aps[k] = nc.dram_tensor(f"out_{k}", shape, F32, kind="ExternalOutput").ap()
    build(nc, **aps)
    r = _run(nc, [arrays], core_ids=[0]).results[0]
    o = {k: r[f"out_{k}"] for k in outs}
    y = o["yT"].reshape(D_MODEL, T).T
    one = (1, 1)
    return (
        np.ascontiguousarray(y[:SEQ]).reshape(1, SEQ, D_MODEL), np.ascontiguousarray(y[SEQ:]).reshape(DEC_BATCH, DEC_SEQ, D_MODEL),
        o["p_C"].reshape(*one, H, HD, HD), np.ascontiguousarray(o["p_n"].T).reshape(*one, H, HD), o["p_m"].reshape(*one, H),
        o["p_S"].reshape(*one, H, HD, HD), np.ascontiguousarray(o["p_conv"].transpose(2, 0, 1)).reshape(*one, HALO, 3 * W_MIX),
        o["p_H"].reshape(*one, H, HD, HD),
        o["s_C"].reshape(1, DEC_BATCH, H, HD, HD), np.ascontiguousarray(o["s_n"].T).reshape(1, DEC_BATCH, H, HD),
        np.ascontiguousarray(o["s_m"].T).reshape(1, DEC_BATCH, H), o["s_S"].reshape(1, DEC_BATCH, H, HD, HD),
        np.ascontiguousarray(o["s_conv"].reshape(P, 12, DEC_BATCH, HALO).transpose(2, 3, 1, 0)).reshape(1, DEC_BATCH, HALO, 3 * W_MIX),
        o["s_H"].reshape(1, DEC_BATCH, H, HD, HD),
    )
```
